# Optimizing a Trainium2 kernel written in Bass

```python
import math
import jax
import jax.numpy as jnp
from jax import lax
import numpy as np

D_MODEL = 1024
BATCH = 1
SEQ = 1024
DEPTH = 1
DEC_BATCH = 1
DEC_SEQ = 32
PAST_LEN = 2048

CHUNK = 64
HEAD_DIM = 64
N_HEADS_DN = 8
N_HEADS_SB = 8
DN_WIDTH = N_HEADS_DN * HEAD_DIM
SB_WIDTH = N_HEADS_SB * HEAD_DIM
MIX_WIDTH = DN_WIDTH + SB_WIDTH
CONV_K = 4
CONV_DIM = 3 * DN_WIDTH
D_FF = 4 * D_MODEL
PLE_DIM = 256
SB_QBLOCK = 128
SB_SCALE = HEAD_DIM ** -0.5
NORM_EPS = 1e-6
SB_OFFSET = CONV_DIM + DN_WIDTH + 2 * N_HEADS_DN
IN_SPLITS = (CONV_DIM, CONV_DIM + DN_WIDTH, CONV_DIM + DN_WIDTH + N_HEADS_DN, SB_OFFSET,
             SB_OFFSET + SB_WIDTH, SB_OFFSET + 2 * SB_WIDTH)
IN_DIM = SB_OFFSET + 3 * SB_WIDTH

kernel_name = "hybrid_deltanet_stickbreak_stream_step"

def rmsnorm(x, g):
    xf = x.astype(jnp.float32)
    xf = xf * lax.rsqrt(jnp.mean(xf * xf, axis=-1, keepdims=True) + NORM_EPS)
    return xf.astype(x.dtype) * g

def l2norm(x):
    xf = x.astype(jnp.float32)
    return xf * lax.rsqrt(jnp.sum(xf * xf, axis=-1, keepdims=True) + NORM_EPS)

def causal_conv(x, w, state):
    t = x.shape[1]
    xp = jnp.concatenate([state.astype(x.dtype), x], axis=1)
    y = xp[:, 0:t] * w[0]
    for i in range(1, CONV_K):
        y = y + xp[:, i:i + t] * w[i]
    return y, xp[:, t:]

def to_chunks(a, n, l):
    b, _, h = a.shape[:3]
    a = a.reshape((b, n, l, h) + a.shape[3:])
    return jnp.moveaxis(a, (1, 3), (0, 2))

def gated_delta_rule(q, k, v, g, beta, s0):
    b, t, h, dk = q.shape
    dv = v.shape[-1]
    l = min(CHUNK, t)
    n = t // l
    qc, kc, vc = to_chunks(q, n, l), to_chunks(k, n, l), to_chunks(v, n, l)
    gc, bc = to_chunks(g, n, l), to_chunks(beta, n, l)
    gcum = jnp.cumsum(gc, axis=-1)
    idx = jnp.arange(l)
    causal = idx[:, None] >= idx[None, :]
    strict = idx[:, None] > idx[None, :]
    decay = jnp.exp(jnp.where(causal, gcum[..., :, None] - gcum[..., None, :], -jnp.inf))
    kb = kc * bc[..., None]
    a_mat = jnp.where(strict, jnp.einsum('nbhid,nbhjd->nbhij', kb, kc) * decay, 0.0)
    rhs = jnp.concatenate([vc * bc[..., None], kb * jnp.exp(gcum)[..., None]], axis=-1)
    sol = lax.linalg.triangular_solve(a_mat + jnp.eye(l, dtype=a_mat.dtype), rhs,
                                      left_side=True, lower=True, unit_diagonal=True)
    u, w = sol[..., :dv], sol[..., dv:]
    qk = jnp.where(causal, jnp.einsum('nbhid,nbhjd->nbhij', qc, kc) * decay, 0.0)

    def step(s, xs):
        q_i, k_i, u_i, w_i, g_i, qk_i = xs
        v_new = u_i - jnp.einsum('bhld,bhde->bhle', w_i, s)
        o = (jnp.einsum('bhld,bhde->bhle', q_i * jnp.exp(g_i)[..., None], s)
             + jnp.einsum('bhij,bhje->bhie', qk_i, v_new))
        g_last = g_i[..., -1]
        s = (s * jnp.exp(g_last)[..., None, None]
             + jnp.einsum('bhld,bhle->bhde', k_i * jnp.exp(g_last[..., None] - g_i)[..., None], v_new))
        return s, o

    s_fin, o = lax.scan(step, s0, (qc, kc, u, w, gcum, qk))
    o = jnp.moveaxis(o, (0, 2), (1, 3)).reshape(b, t, h, dv)
    return o, s_fin

def stick_breaking_block(q, k, v, q_pos, k_pos):
    z = jnp.einsum('bqhd,bshd->bhqs', q, k).astype(jnp.float32) * SB_SCALE
    valid = k_pos[None, :] < q_pos[:, None]
    log_keep = jnp.where(valid, jax.nn.log_sigmoid(-z), 0.0)
    log_rest = lax.cumsum(log_keep, axis=3, reverse=True) - log_keep
    a = jnp.where(valid, jnp.exp(jax.nn.log_sigmoid(z) + log_rest), 0.0)
    return jnp.einsum('bhqs,bshd->bqhd', a.astype(v.dtype), v)

def stick_breaking(q, k, v, q_offset):
    b, t, h, d = q.shape
    qb = min(SB_QBLOCK, t)
    nb = t // qb
    k_pos = jnp.arange(k.shape[1])
    q_pos = (q_offset + jnp.arange(t)).reshape(nb, qb)
    q_blocks = jnp.moveaxis(q.reshape(b, nb, qb, h, d), 1, 0)
    o = lax.map(lambda a: stick_breaking_block(a[0], k, v, a[1], k_pos), (q_blocks, q_pos))
    return jnp.moveaxis(o, 0, 1).reshape(b, t, h, d)

def trunk_layer(x, p, conv_state, s0, k_past, v_past, g_mix, w_in, conv_w, a_log, dt_bias,
                g_out_dn, g_q_sb, g_k_sb, w_out, g_mlp, w_up, w_down, g_ple, w_ple_gate, w_ple_proj):
    b, t, _ = x.shape
    f32 = jnp.float32
    u = rmsnorm(x, g_mix)
    proj = u @ w_in
    dn_qkv, dn_z, dn_alpha, dn_beta, sb_q, sb_k, sb_v = jnp.split(proj, IN_SPLITS, axis=-1)

    c, new_conv = causal_conv(dn_qkv, conv_w, conv_state)
    c = jax.nn.silu(c)
    qa, ka, va = jnp.split(c, 3, axis=-1)
    qa = l2norm(qa.reshape(b, t, N_HEADS_DN, HEAD_DIM)) * (HEAD_DIM ** -0.5)
    ka = l2norm(ka.reshape(b, t, N_HEADS_DN, HEAD_DIM))
    va = va.reshape(b, t, N_HEADS_DN, HEAD_DIM).astype(f32)
    g = -jnp.exp(a_log.astype(f32)) * jax.nn.softplus(dn_alpha.astype(f32) + dt_bias.astype(f32))
    beta = jax.nn.sigmoid(dn_beta.astype(f32))
    o_a, s_new = gated_delta_rule(qa, ka, va, g, beta, s0.astype(f32))
    z = dn_z.reshape(b, t, N_HEADS_DN, HEAD_DIM)
    o_a = (rmsnorm(o_a.astype(x.dtype), g_out_dn) * jax.nn.silu(z)).reshape(b, t, DN_WIDTH)

    qb = rmsnorm(sb_q.reshape(b, t, N_HEADS_SB, HEAD_DIM), g_q_sb)
    kb = rmsnorm(sb_k.reshape(b, t, N_HEADS_SB, HEAD_DIM), g_k_sb)
    vb = sb_v.reshape(b, t, N_HEADS_SB, HEAD_DIM)
    k_all = jnp.concatenate([k_past.astype(kb.dtype), kb], axis=1)
    v_all = jnp.concatenate([v_past.astype(vb.dtype), vb], axis=1)
    o_b = stick_breaking(qb, k_all, v_all, k_past.shape[1]).reshape(b, t, SB_WIDTH)

    h = x + jnp.concatenate([o_a, o_b.astype(o_a.dtype)], axis=-1) @ w_out
    h = h + jnp.square(jax.nn.relu(rmsnorm(h, g_mlp) @ w_up)) @ w_down
    h = h + jax.nn.sigmoid(rmsnorm(h, g_ple) @ w_ple_gate) * (p @ w_ple_proj)
    return h, new_conv, s_new, kb, vb

def setup_inputs(seed: int = 0) -> dict:
    key = jax.random.key(seed)
    ks = jax.random.split(key, 32)
    f32 = jnp.float32

    def nrm(k, shape, scale):
        return jax.random.normal(k, shape, f32) * scale

    def gain(k, shape):
        return 1.0 + 0.05 * jax.random.normal(k, shape, f32)

    dt = jnp.exp(jax.random.uniform(ks[20], (DEPTH, N_HEADS_DN), f32, math.log(1e-3), math.log(1e-1)))
    return {
        "x_prompt": nrm(ks[0], (BATCH, SEQ, D_MODEL), 1.0),
        "x_sample": nrm(ks[1], (DEC_BATCH, DEC_SEQ, D_MODEL), 1.0),
        "cache_conv": nrm(ks[2], (DEPTH, DEC_BATCH, CONV_K - 1, CONV_DIM), 1.0),
        "state_delta": nrm(ks[3], (DEPTH, DEC_BATCH, N_HEADS_DN, HEAD_DIM, HEAD_DIM), 0.3),
        "cache_k": nrm(ks[4], (DEPTH, DEC_BATCH, PAST_LEN, N_HEADS_SB, HEAD_DIM), 1.0),
        "cache_v": nrm(ks[5], (DEPTH, DEC_BATCH, PAST_LEN, N_HEADS_SB, HEAD_DIM), 1.0),
        "p_prompt": nrm(ks[6], (DEPTH, BATCH, SEQ, PLE_DIM), 1.0),
        "p_sample": nrm(ks[7], (DEPTH, DEC_BATCH, DEC_SEQ, PLE_DIM), 1.0),
        "g_mix": gain(ks[8], (DEPTH, D_MODEL)),
        "w_in": nrm(ks[9], (DEPTH, D_MODEL, IN_DIM), D_MODEL ** -0.5),
        "conv_w": nrm(ks[10], (DEPTH, CONV_K, CONV_DIM), CONV_K ** -0.5),
        "a_log": jnp.log(jax.random.uniform(ks[11], (DEPTH, N_HEADS_DN), f32, 1.0, 16.0)),
        "dt_bias": dt + jnp.log(-jnp.expm1(-dt)),
        "g_out_dn": gain(ks[12], (DEPTH, HEAD_DIM)),
        "g_q_sb": gain(ks[13], (DEPTH, HEAD_DIM)),
        "g_k_sb": gain(ks[14], (DEPTH, HEAD_DIM)),
        "w_out": nrm(ks[15], (DEPTH, MIX_WIDTH, D_MODEL), MIX_WIDTH ** -0.5),
        "g_mlp": gain(ks[16], (DEPTH, D_MODEL)),
        "w_up": nrm(ks[17], (DEPTH, D_MODEL, D_FF), D_MODEL ** -0.5),
        "w_down": nrm(ks[18], (DEPTH, D_FF, D_MODEL), D_FF ** -0.5),
        "g_ple": gain(ks[19], (DEPTH, D_MODEL)),
        "w_ple_gate": nrm(ks[21], (DEPTH, D_MODEL, D_MODEL), D_MODEL ** -0.5),
        "w_ple_proj": nrm(ks[22], (DEPTH, PLE_DIM, D_MODEL), PLE_DIM ** -0.5),
    }

def reference(x_prompt, x_sample, cache_conv, state_delta, cache_k, cache_v, p_prompt, p_sample,
              g_mix, w_in, conv_w, a_log, dt_bias, g_out_dn, g_q_sb, g_k_sb, w_out, g_mlp, w_up,
              w_down, g_ple, w_ple_gate, w_ple_proj):
    bp = x_prompt.shape[0]
    y_prompt, y_sample = x_prompt, x_sample
    conv_p, delta_p, k_p, v_p = [], [], [], []
    conv_s, delta_s, k_s, v_s = [], [], [], []
    for i in range(DEPTH):
        wts = (g_mix[i], w_in[i], conv_w[i], a_log[i], dt_bias[i], g_out_dn[i], g_q_sb[i], g_k_sb[i],
               w_out[i], g_mlp[i], w_up[i], w_down[i], g_ple[i], w_ple_gate[i], w_ple_proj[i])
        y_prompt, c, s, k, v = trunk_layer(
            y_prompt, p_prompt[i],
            jnp.zeros((bp, CONV_K - 1, CONV_DIM), x_prompt.dtype),
            jnp.zeros((bp, N_HEADS_DN, HEAD_DIM, HEAD_DIM), jnp.float32),
            jnp.zeros((bp, 0, N_HEADS_SB, HEAD_DIM), x_prompt.dtype),
            jnp.zeros((bp, 0, N_HEADS_SB, HEAD_DIM), x_prompt.dtype),
            *wts)
        conv_p.append(c); delta_p.append(s); k_p.append(k); v_p.append(v)
        y_sample, c, s, k, v = trunk_layer(
            y_sample, p_sample[i], cache_conv[i], state_delta[i], cache_k[i], cache_v[i], *wts)
        conv_s.append(c); delta_s.append(s); k_s.append(k); v_s.append(v)
    return (y_prompt, y_sample,
            jnp.stack(conv_p), jnp.stack(delta_p), jnp.stack(k_p), jnp.stack(v_p),
            jnp.stack(conv_s), jnp.stack(delta_s), jnp.stack(k_s), jnp.stack(v_s))


_drawn_inputs = setup_inputs


def setup_inputs(seed=0):
    import zlib

    import numpy as np

    out = dict(_drawn_inputs(seed))
    spreads = {}
    factors = {'g_out_dn': 3.507, 'g_q_sb': 5.949, 'g_ple': 29.689}
    for name, (base, spread) in spreads.items():
        noise = np.random.default_rng([zlib.crc32(name.encode()), seed]).standard_normal(out[name].shape)
        drawn = base * np.exp(spread * noise) if base else spread * noise
        out[name] = jnp.asarray(drawn.astype(out[name].dtype))
    for name, factor in factors.items():
        out[name] = (out[name] * factor).astype(out[name].dtype)
    return out
```

```python
from contextlib import ExitStack

import concourse.bass as bass
from concourse import mybir

F32 = mybir.dt.float32
F32R = mybir.dt.float32r
ALU = mybir.AluOpType
ACT = mybir.ActivationFunctionType
AX = mybir.AxisListType

P = 128
EPS = 1e-6


class Chain:

    def __init__(self, eng, sem):
        self.eng, self.sem, self.count, self.offset = eng, sem, 0, 0

    def mark(self, instruction):
        instruction.then_inc(self.sem, 1)
        self.count += 1
        return instruction

    def wait(self):
        self.eng.wait_ge(self.sem, self.count + self.offset)

    def link(self, instruction):
        self.mark(instruction)
        self.wait()

    def enter(self, i, per):
        self.start, self.per, self.offset = self.count, per, i * per

    def leave(self, trips):
        assert self.count - self.start == self.per, (self.count - self.start, self.per)
        self.count = self.start + self.per * trips
        self.offset = 0


def trunk_step(nc, x_prompt, x_sample, cache_conv, state_delta, cache_k, cache_v, p_prompt, p_sample, g_mix,
               w_in, conv_w, a_log, dt_bias, g_out_dn, g_q_sb, g_k_sb, w_out, g_mlp, w_up, w_down, g_ple,
               w_ple_gate, w_ple_proj, y_prompt, y_sample, conv_prompt, delta_prompt, k_prompt, v_prompt,
               conv_sample, delta_sample, k_sample, v_sample):
    D = x_prompt.shape[2]
    TP, TS = x_prompt.shape[1], x_sample.shape[1]
    T = TP + TS
    H, HD = a_log.shape[1], g_out_dn.shape[1]
    W = H * HD
    CD = 3 * W
    PAST = cache_k.shape[2]
    FF = w_up.shape[2]
    PD = p_prompt.shape[3]
    KT = D // P
    NT = TP // P
    CH = T // 3
    WT = W // P
    NC = CD // P
    BLK = 2048
    assert 3 * CH == T and TP % P == 0 and TS == 32 and W == 512 and KT == 8 and HD == 64
    tile_rows = [P] * NT + [TS]
    NTT = len(tile_rows)

    x_rows = [x_prompt[0, P * t:P * (t + 1), :] for t in range(NT)] + [x_sample[0, :, :]]
    p_rows = [p_prompt[0, 0, P * t:P * (t + 1), :] for t in range(NT)] + [p_sample[0, 0, :, :]]
    win = w_in[0].rearrange("(k p) n -> p k n", p=P)
    wout = w_out[0].rearrange("(k p) n -> p k n", p=P)
    wup = w_up[0].rearrange("(k p) n -> p k n", p=P)
    wdown = w_down[0].rearrange("(g k p) n -> g p k n", p=P, k=4)
    wgate = w_ple_gate[0].rearrange("(k p) n -> p k n", p=P)
    wproj = w_ple_proj[0].rearrange("(k p) n -> p k n", p=P)
    k_out = k_prompt[0, 0].rearrange("t h d -> t (h d)")
    v_out = v_prompt[0, 0].rearrange("t h d -> t (h d)")
    ks_out = k_sample[0, 0].rearrange("t h d -> t (h d)")
    vs_out = v_sample[0, 0].rearrange("t h d -> t (h d)")
    kcache = cache_k[0, 0].rearrange("(b p) h d -> p b (h d)", p=P)
    vcache = cache_v[0, 0].rearrange("(b p) h d -> p b (h d)", p=P)
    state_of = {n: a[0, 0].rearrange("(t u) d e -> (u d) t e", u=2)
                for n, a in (("in", state_delta), ("prompt", delta_prompt), ("sample", delta_sample))}
    conv_dram = nc.dram_tensor("conv_scratch", (NC, P, T), F32).ap()
    z_dram = nc.dram_tensor("z_scratch", (T, W), F32).ap()

    with ExitStack() as ctx:
        def sb(name, shape, dt=F32):
            return ctx.enter_context(nc.sbuf_tensor(name, shape, dt))

        def sem(name):
            return ctx.enter_context(nc.semaphore(name))

        act_hi = sb("act_hi", [P, KT, T], F32R)
        act_lo = sb("act_lo", [P, KT, T], F32R)
        w_raw = sb("w_raw", [P, 2, BLK])
        w_hi = sb("w_hi", [P, 2, BLK], F32R)
        w_lo = sb("w_lo", [P, 2, BLK], F32R)
        ident = sb("ident", [P, P])
        ones = sb("ones", [P, P])
        halves = sb("halves", [P, P])
        tri = sb("tri", [P, P])
        tri8 = sb("tri8", [P, P])
        neg_strict = sb("neg_strict", [P, P])
        below = sb("below", [P, P])
        not_below = sb("not_below", [P, P])
        LEVELS = 7
        level = sb("level", [P, LEVELS, P])
        eps = sb("eps", [P, 1])
        below_s = sb("below_s", [P, 2, TS])
        params = sb("params", [P, 100])
        gates = sb("gates", [P, NTT, 2 * H])
        glog = sb("glog", [P, NTT, H])
        beta = sb("beta", [P, NTT, H])
        small = sb("small", [P, 64])
        heads_g = sb("heads_g", [P, 3, HD])
        dn_par = sb("dn_par", [P, 2, H])
        AW = 11776
        area = sb("area", [P, AW])
        with ExitStack() as late:
            hid_hi = late.enter_context(nc.sbuf_tensor("hid_hi", [P, 4, T], F32R))
            hid_lo = late.enter_context(nc.sbuf_tensor("hid_lo", [P, 4, T], F32R))
        area2 = sb("area2", [P, 8 * T])

        psum = ctx.enter_context(nc.psum_tensor("psum", [P, 8, 512], F32))

        def bank(b):
            return psum[:, b, :]

        consts_made = sem("consts_made")
        vecs_loaded = sem("vecs_loaded")
        par_t = sem("par_t")
        par_done = sem("par_done")
        raw_loaded = [sem("raw_loaded0"), sem("raw_loaded1")]
        raw_free = sem("raw_free")
        w_split = sem("w_split")
        ab_loaded = sem("ab_loaded")
        ab_split = sem("ab_split")
        pool_own = sem("pool_own")
        act_own = sem("act_own")
        dve_own = sem("dve_own")
        x_loaded = [sem(f"x_loaded{i}") for i in range(3)]
        x_ms = sem("x_ms")
        x_sd = sem("x_sd")
        x_scaled = sem("x_scaled")
        x_turned = sem("x_turned")
        x_hi = sem("x_hi")
        x_lo = sem("x_lo")
        tok_ready = sem("tok_ready")
        tok_free = sem("tok_free")
        sq_made = sem("sq_made")
        ss_made = sem("ss_made")
        sd_made = sem("sd_made")
        qk_normed = sem("qk_normed")
        qk_turned = sem("qk_turned")
        qk_placed = sem("qk_placed")
        k_stored = [sem("k_stored0"), sem("k_stored1")]
        v_placed = sem("v_placed")
        v_stored = sem("v_stored")
        z_silu = sem("z_silu")
        z_made = sem("z_made")
        z_stored = [sem("z_stored0"), sem("z_stored1")]
        ab_ready = sem("ab_ready")
        ga = sem("ga")
        gd = sem("gd")
        dense_ready = sem("dense_ready")
        dense_free = sem("dense_free")
        added = sem("added")
        relu_free = sem("relu_free")
        xb_ready = sem("xb_ready")
        y_ready = sem("y_ready")
        cs_ready = sem("cs_ready")
        cs_stored = sem("cs_stored")
        tails_made = sem("tails_made")
        tails_t = sem("tails_t")
        tails_c = sem("tails_c")
        tails_stored = sem("tails_stored")

        q_staged = sem("q_staged")
        scores_ready = sem("scores_ready")
        sig_made = sem("sig_made")
        att_made = sem("att_made")
        att_turned = sem("att_turned")
        att_placed = sem("att_placed")
        o_ready = sem("o_ready")
        o_copied = sem("o_copied")
        o_turned = sem("o_turned")
        o_split = sem("o_split")
        s_staged = sem("s_staged")
        kc_loaded = sem("kc_loaded")
        vc_loaded = sem("vc_loaded")
        kc_turned = sem("kc_turned")
        kc_placed = sem("kc_placed")
        s_scores = sem("s_scores")
        s_sig = sem("s_sig")
        s_att = sem("s_att")
        s_turned = sem("s_turned")
        s_placed = sem("s_placed")
        so_ready = sem("so_ready")
        so_copied = sem("so_copied")
        so_turned = sem("so_turned")
        so_split = sem("so_split")

        c_loaded = sem("c_loaded")
        z_loaded = sem("z_loaded")
        gu_made = sem("gu_made")
        gc_ready = sem("gc_ready")
        eg_made = sem("eg_made")
        t0_made = sem("t0_made")
        dt_made = sem("dt_made")
        sq2_made = sem("sq2_made")
        ss_ready = sem("ss_ready")
        sd2_made = sem("sd2_made")
        cn_made = sem("cn_made")
        kv_turned = sem("kv_turned")
        kv_placed = sem("kv_placed")
        g_ready = sem("g_ready")
        qk_ready = sem("qk_ready")
        dts_made = sem("dts_made")
        dtq_made = sem("dtq_made")
        kd_made = sem("kd_made")
        kg_made = sem("kg_made")
        sdec_made = sem("sdec_made")
        at_made = sem("at_made")
        qt_made = sem("qt_made")
        qg_made = sem("qg_made")
        m_ready = sem("m_ready")
        m_made = sem("m_made")
        xt_ready = sem("xt_ready")
        xt_made = sem("xt_made")
        ks_ready = sem("ks_ready")
        r_made = sem("r_made")
        vn_ready = sem("vn_ready")
        vn_made = sem("vn_made")
        ds_ready = sem("ds_ready")
        s_new = sem("s_new")
        s_stored = sem("s_stored")
        s_loaded = sem("s_loaded")
        o_made = sem("o_made")
        osq_made = sem("osq_made")
        ored_made = sem("ored_made")
        osd_made = sem("osd_made")
        on_made = sem("on_made")
        ot_ready = sem("ot_ready")
        mix_split = sem("mix_split")
        xr_loaded = [sem(f"xr_loaded{i}") for i in range(3)]
        xr_turned = sem("xr_turned")
        h_placed = sem("h_placed")
        nsq_made = sem("nsq_made")
        nsum = sem("nsum")
        nsd = sem("nsd")
        ntmp = sem("ntmp")
        nhi = sem("nhi")
        nlo = sem("nlo")
        relu_made = sem("relu_made")
        hid_split = sem("hid_split")
        p_loaded = [sem(f"p_loaded{i}") for i in range(2)]
        p_turned = sem("p_turned")
        p_hi = sem("p_hi")
        p_lo = sem("p_lo")
        ple_ready = sem("ple_ready")
        sg_made = sem("sg_made")
        y_made = sem("y_made")
        y_stored = [sem(f"y_stored{i}") for i in range(2)]

        def carve(base, at, *shape):
            n = 1
            for d in shape:
                n *= d
            flat = base[:, at:at + n]
            if len(shape) == 1:
                return flat
            names = "abcd"[:len(shape)]
            return flat.rearrange(f"p ({' '.join(names)}) -> p {' '.join(names)}",
                                  **dict(zip(names, shape)))

        x_in = carve(area, 0, 3, D)
        x_sc = carve(area, 3 * D, 2, D)
        junk = carve(area, 5 * D, D)
        gmix_b = carve(area, 6 * D, D)
        param_rows = carve(area, 7 * D, P)
        q_t = carve(area2, 0, WT, T)
        k_t = carve(area2, WT * T, WT, T)
        v_tok = carve(area, 0, NTT, W)
        tok0 = NTT * W
        HC = 256
        HH, HT, HALF = HC // HD, HC // P, 2 * NTT
        sq_buf = carve(area, tok0, HC)
        qk_buf = carve(area, tok0 + W, 2, HC)
        z_buf = carve(area, tok0 + 3 * W, 2, HC)
        XB = T + 6
        YB = T + 3
        xb = carve(area, tok0 + 5 * W, 2, XB)
        yb = carve(area, tok0 + 5 * W + 2 * XB, YB)
        cb = carve(area, tok0 + 5 * W + 2 * XB + YB, 1, YB)
        tails = sb("tails", [P, 2, 3, NC])
        sp_x = carve(area, tok0, 2, NTT, H)
        sp_x = (sp_x[:, 0, :, :], sp_x[:, 1, :, :])
        sp_e = carve(area, tok0 + 2 * NTT * H, NTT, H)
        tails_out = carve(area, tok0 + 4 * NTT * H, P)[0:72, :]
        ab_raw = sb("ab_raw", [P, KT, 2 * H])
        ab_hi = sb("ab_hi", [P, KT, 2 * H], F32R)
        ab_lo = sb("ab_lo", [P, KT, 2 * H], F32R)

        SW = PAST + TS
        assert SW == 2 * (TP + TS // 2) and 4 * TS == P
        keep_buf = carve(area, tok0, 2, SW // 2)
        sig_buf = carve(area, tok0 + SW, 2, SW // 2)
        at_buf = carve(area, tok0 + 2 * SW, 2, TP)
        q_stage = carve(area, tok0 + 2 * SW + 2 * TP, 2, P)
        o_buf = carve(area, tok0 + 2 * SW + 2 * TP + 2 * P, 2, P)
        q_s = carve(area, tok0 + 2 * SW + 2 * TP + 4 * P, WT, 2, TS)
        k_s = carve(area, tok0 + 2 * SW + 2 * TP + 6 * P, WT, TS)
        v_s = sb("v_s", [P, W])
        PB = PAST // P
        k_raw = carve(area2, 0, PB, 256)
        kc_t = carve(area2, PB * 256, 2, PAST)
        v_c = carve(area, 0, PB, 256)
        keep_s = carve(area, tok0, SW)
        sig_s = carve(area, tok0 + SW, SW)

        d_c = carve(area, 0, NC, P)
        d_cn = carve(area, 1536, KT, P)
        d_rs = carve(area, 2560, KT, P)
        d_z = carve(area, 3584, W)
        d_k = carve(area, 4096, W)
        d_v = carve(area, 4608, W)
        d_gu = carve(area, 5120, H, P)
        d_eg = carve(area, 6144, H, P)
        d_dt = carve(area, 7168, H, P)
        d_dts = carve(area, 8192, H, P)
        d_dtq = carve(area, 9216, H, P)
        d_at = carve(area, 10240, H, P)
        d_gc = carve(area, 11264, H)
        d_qt = carve(area2, 0, H, P)
        d_t = carve(area2, 1024, H, P)
        d_x = carve(area2, 2048, H, P)
        d_m = carve(area2, 3072, H, P)
        d_kg = carve(area2, 4096, WT, P)
        d_qg = carve(area2, 4608, WT, P)
        d_kd = carve(area2, 5120, W)
        d_s = carve(area2, 5632, WT, HD)
        d_sd = carve(area2, 5888, WT, HD)
        d_r = carve(area2, 6144, W)
        d_vn = carve(area2, 6656, W)
        d_oq = carve(area2, 7168, W)
        d_on = carve(area2, 7680, W)
        CHUNKS = NT + 1

        def place_of(h):
            return 4 * (h % 2) + h // 2

        def heads(x, n):
            return x[0:n, :].rearrange("p (k u d) -> p u k d", u=2, d=HD)

        def per_head(x, n, width):
            return x.rearrange("p (u k) -> p u k", u=2).unsqueeze(3).to_broadcast([n, 2, WT, width])

        def value_banks(n):
            return psum[0:n, 6:8, 0:4 * HD].rearrange("p u (k d) -> p u k d", k=WT)

        def head_banks(b, rows, n):
            return psum[0:rows, b:b + 2, :].rearrange("p a (h t) -> p (a h) t", h=4)[:, :, 0:n]

        def levels_of(n):
            return n.bit_length() - 1

        def step_of(c, l, g):
            return 2 * LEVELS * c + 2 * l + g + 1

        h_t = carve(area, 0, KT, T)
        wide = carve(area, KT * T, 3, T)
        xr_in = carve(area2, 0, 3, D)
        sg_buf = carve(area, KT * T, 2, 512)
        y_buf = carve(area, KT * T + 1024, 2, 512)
        p_in = v_s[:, :].rearrange("p (s n) -> p s n", s=2)
        proj_hi = hid_hi[:, 2:4, :].rearrange("p k t -> p (k t)")[:, 0:BLK]
        proj_lo = hid_lo[:, 2:4, :].rearrange("p k t -> p (k t)")[:, 0:BLK]
        OUT0 = NC
        MLP0 = OUT0 + KT
        PER = 12
        ROUNDS = FF // 512

        whi_cols = w_hi[:, :, :].rearrange("p s (k n) -> p s k n", k=KT)
        wlo_cols = w_lo[:, :, :].rearrange("p s (k n) -> p s k n", k=KT)
        SBCOL = CD + W + 2 * H

        def halves_of(rows):
            return slice(0, rows)

        def token_banks(b, rows):
            return psum[:, b:b + 2, :].rearrange("p a (k t) -> p (a k) t", k=4)[:, :, 0:rows]

        UNITS = 2 * NT

        def earlier(i, j, lag):
            return UNITS * i + max(j - lag + 1, 0)

        block = ctx.enter_context(nc.Block())

        @block.sync
        def _(sp):
            sp.dma_start(gmix_b, g_mix.broadcast_to([P, D])).then_inc(vecs_loaded, 16)
            sp.wait_ge(consts_made, 1)
            sp.dma_start(param_rows[0:8, :], g_mlp[0].rearrange("(a b) -> a b", b=P)).then_inc(vecs_loaded, 16)
            sp.dma_start(param_rows[8:16, :], g_ple[0].rearrange("(a b) -> a b", b=P)).then_inc(vecs_loaded, 16)
            sp.dma_start(param_rows[16:64, :], conv_w[0].rearrange("i (m b) -> (i m) b", b=P)).then_inc(vecs_loaded, 16)
            sp.dma_start(param_rows[64:100, :], cache_conv[0, 0].rearrange("i (m b) -> (i m) b", b=P)).then_inc(vecs_loaded, 16)
            for n, g in enumerate((g_q_sb, g_k_sb, g_out_dn)):
                sp.dma_start(heads_g[:, n, :], g.broadcast_to([P, HD])).then_inc(vecs_loaded, 16)
            sp.dma_start(dn_par[:, 0, :], a_log.broadcast_to([P, H])).then_inc(vecs_loaded, 16)
            sp.dma_start(dn_par[:, 1, :], dt_bias.broadcast_to([P, H])).then_inc(vecs_loaded, 16)
            for t, rows in enumerate(tile_rows):
                if t >= 3:
                    sp.wait_ge(x_scaled, t - 2)
                sp.dma_start(x_in[0:rows, t % 3, :], x_rows[t]).then_inc(x_loaded[t % 3], 16)
                if t == 2:
                    sp.dma_start(ab_raw[:], win[:, :, CD + W:SBCOL]).then_inc(ab_loaded, 16)

            def block_in(n, slot, src):
                sp.wait_ge(raw_free, n + 1)
                dst = w_raw[:, slot, :].rearrange("p (k n) -> p k n", k=src.shape[1])
                sp.dma_start(dst, src).then_inc(raw_loaded[slot], 16)

            with sp.Fori(0, 3) as i:
                for u in range(2):
                    block_in(2 * i + u, u, win[:, :, bass.ds(SBCOL + 512 * i + 256 * u, 256)])
            for u in range(2):
                block_in(6 + u, u, win[:, :, CD + 256 * u:CD + 256 * u + 256])
            with sp.Fori(0, 3) as i:
                for u in range(2):
                    block_in(8 + 2 * i + u, u, win[:, :, bass.ds(512 * i + 256 * u, 256)])
            sp.wait_ge(tails_c, 1)
            sp.wait_ge(tails_c, 1)
            for n, dst in enumerate((conv_prompt, conv_sample)):
                sp.dma_start(dst[0, 0].rearrange("i (m b) -> (i m) b", b=P),
                             tails_out[36 * n:36 * n + 36, :]).then_inc(tails_stored, 16)
            sp.wait_ge(o_split, 1 + WT * NT)
            sp.wait_ge(s_staged, 1)
            for g in range(2):
                if g:
                    sp.wait_ge(kc_turned, 8)
                sp.dma_start(k_raw, kcache[:, :, 256 * g:256 * g + 256]).then_inc(kc_loaded, 16)
                if g:
                    sp.wait_ge(so_ready, 1)
                sp.dma_start(v_c, vcache[:, :, 256 * g:256 * g + 256]).then_inc(vc_loaded, 16)
            sp.wait_ge(so_split, 2)
            sp.wait_ge(cs_stored, 1 + 32 * NC)
            for u in range(2):
                sp.wait_ge(z_stored[u], 16 * NTT)

            def chunk_in(c, n):
                cols = bass.ds(P * c, n)
                sp.wait_ge(kv_placed, 1 + c)
                sp.dma_start(d_c[:, :, 0:n], conv_dram[:, :, cols].rearrange("m p t -> p m t")).then_inc(c_loaded, 16)
                sp.wait_ge(on_made, 1 + c)
                sp.dma_start(d_z[0:n, :], z_dram[cols, :]).then_inc(z_loaded, 16)

            with sp.Fori(0, NT) as c:
                chunk_in(c, P)
            chunk_in(NT, TS)
            sp.wait_ge(s_new, NT + 1)
            sp.dma_start(state_of["prompt"], d_s).then_inc(s_stored, 16)
            sp.wait_ge(s_stored, 16)
            sp.dma_start(d_s, state_of["in"]).then_inc(s_loaded, 16)
            with sp.Fori(0, 2) as i:
                for u in range(2):
                    block_in(14 + 2 * i + u, u, wout[:, :, bass.ds(512 * i + 256 * u, 256)])
            sp.wait_ge(s_new, NT + 2)
            sp.dma_start(state_of["sample"], d_s).then_inc(s_stored, 16)
            sp.wait_ge(mix_split, 1 + CHUNKS)
            for t, rows in enumerate(tile_rows):
                if t >= 3:
                    sp.wait_ge(xr_turned, t - 2)
                sp.dma_start(xr_in[0:rows, t % 3, :], x_rows[t]).then_inc(xr_loaded[t % 3], 16)
            with sp.Fori(0, ROUNDS) as g:
                for u in range(2):
                    block_in(18 + 4 * g + u, u, wup[:, :, bass.ds(512 * g + 256 * u, 256)])
                for u in range(2):
                    src = wdown[bass.ds(g, 1), :, :, 512 * u:512 * (u + 1)].rearrange("g p k n -> (g p) k n")
                    block_in(20 + 4 * g + u, u, src)
            block_in(50, 0, wproj[:, :, :])
            block_in(51, 1, wgate[:, :, 0:256])
            for t, rows in enumerate(tile_rows):
                if t >= 2:
                    sp.wait_ge(p_turned, t - 1)
                sp.dma_start(p_in[0:rows, t % 2, :], p_rows[t]).then_inc(p_loaded[t % 2], 16)
            for b in range(1, 4):
                block_in(51 + b, (1 + b) % 2, wgate[:, :, 256 * b:256 * (b + 1)])
            for y in range(2 * NTT):
                t, rows, c = y % NTT, tile_rows[y % NTT], 512 * (y // NTT)
                sp.wait_ge(y_made, y + 1)
                dst = y_prompt[0, P * t:P * t + rows, c:c + 512] if t < NT else y_sample[0, :, c:c + 512]
                sp.dma_start(dst, y_buf[0:rows, y % 2, :]).then_inc(y_stored[y % 2], 16)
            for u in range(2):
                sp.wait_ge(k_stored[u], 16 * NTT)
                sp.wait_ge(z_stored[u], 16 * NTT)
                sp.wait_ge(y_stored[u], 16 * NTT)
            sp.wait_ge(v_stored, 32)
            sp.wait_ge(cs_stored, 1 + 32 * NC)
            sp.wait_ge(tails_stored, 32)
            sp.wait_ge(s_stored, 32)

        @block.gpsimd
        def _(pool):
            own = Chain(pool, pool_own)
            for started in (q_staged,):
                pool.sem_inc(started, 1)
            pool.memset(param_rows, 0.0).then_inc(consts_made, 1)
            for m, value in ((ident, 0.0), (ones, 1.0), (halves, 1.0), (tri, 1.0), (tri8, HD ** -0.5),
                             (neg_strict, -1.0), (below, 1.0), (not_below, 1.0)):
                own.mark(pool.memset(m[:], value))
            own.mark(pool.memset(eps[:], EPS))
            own.mark(pool.memset(level[:], 1.0))
            own.mark(pool.memset(below_s[:, 0, :], 1.0))
            own.mark(pool.memset(gates[:], 0.0))
            own.wait()

            def keep(m, op, base, pattern, mult, fill=0.0):
                own.mark(pool.affine_select(out=m, in_=m, compare_op=op, fill=fill, base=base,
                                            pattern=pattern, channel_multiplier=mult))

            keep(ident[:], ALU.not_equal, 0, [[-1, P]], 1, 1.0)
            keep(tri[:], ALU.is_ge, 0, [[1, P]], -1)
            keep(tri8[:], ALU.is_ge, 0, [[1, P]], -1)
            keep(neg_strict[:], ALU.is_gt, 0, [[1, P]], -1)
            keep(below[:], ALU.is_gt, 0, [[-1, P]], 1)
            keep(not_below[:], ALU.is_ge, 0, [[1, P]], -1)
            keep(halves[:, 0:HD], ALU.is_gt, HD, [[0, HD]], -1)
            keep(halves[:, HD:P], ALU.is_ge, -HD, [[0, HD]], 1)
            for l in range(LEVELS):
                b = 1 << l
                v = level[:, l, :].rearrange("p (n c) -> p n c", c=2 * b)
                own.wait()
                keep(v, ALU.is_ge, -b, [[-2 * b, P // (2 * b)], [0, 2 * b]], 1)
                own.wait()
                keep(v, ALU.is_gt, 2 * b, [[2 * b, P // (2 * b)], [0, 2 * b]], -1)
                own.wait()
                keep(v, ALU.is_gt, b, [[0, P // (2 * b)], [-1, 2 * b]], 0)
            for j in range(4):
                own.wait()
                rows = below_s[TS * j:TS * (j + 1), 0, :]
                keep(rows, ALU.is_gt, 0, [[-1, TS]], 1)
            own.wait()
            own.mark(pool.tensor_scalar(below_s[:, 1, :], below_s[:, 0, :], -1.0, 1.0, ALU.mult, ALU.add))
            own.wait()
            pool.sem_inc(consts_made, 1)
            pool.sem_inc(raw_free, 2)
            pool.wait_ge(ab_loaded, 16)
            own.link(pool.tensor_copy(ab_hi[:], ab_raw[:]))
            pool.tensor_tensor(ab_lo[:], ab_raw[:], ab_hi[:].bitcast(F32), ALU.subtract).then_inc(ab_split, 1)

            def split(turn, slot, used, count, hi=None, lo=None):
                hi = w_hi[:, slot, :] if hi is None else hi
                lo = w_lo[:, slot, :] if lo is None else lo
                pool.wait_ge(raw_loaded[slot], 16 * turn)
                pool.wait_ge(used, count)
                own.link(pool.tensor_tensor(hi, w_raw[:, slot, :], ones[:, 0:1].to_broadcast([P, BLK]), ALU.mult))
                own.mark(pool.tensor_tensor(lo, w_raw[:, slot, :], hi.bitcast(F32), ALU.subtract))
                own.wait()
                pool.sem_inc(w_split, 1)
                pool.sem_inc(raw_free, 1)

            for u in range(2):
                split(1, u, consts_made, 2)
            with pool.Fori(1, 5) as i:
                own.enter(i - 1, 4)
                for u in range(2):
                    split(i + 1, u, tok_ready, NTT * (2 * i + u - 1))
                own.leave(4)
            with pool.Fori(0, 2) as i:
                own.enter(i, 4)
                for u in range(2):
                    split(i + 6, u, dense_ready, 4 * i + 2 * u + 2)
                own.leave(2)

            pool.wait_ge(tails_c, 1)
            pool.wait_ge(cs_stored, 1 + 32 * NC)
            own.link(pool.memset(q_stage, 0.0))
            own.link(pool.memset(q_s, 0.0))
            own.link(pool.tensor_copy(q_s[0:HD, :, 0, :], q_t[0:HD, :, TP:T]))
            own.link(pool.tensor_copy(q_s[HD:P, :, 1, :], q_t[HD:P, :, TP:T]))
            own.link(pool.tensor_copy(k_s, k_t[:, :, TP:T]))
            own.mark(pool.tensor_copy(v_s[0:TS, :], v_tok[0:TS, NT, :]))
            own.wait()
            pool.sem_inc(s_staged, 1)
            with pool.Fori(0, WT) as i:
                for j in range(UNITS):
                    u, t = j % 2, j // 2
                    pool.wait_ge(scores_ready, 1 + earlier(i, j, 2))
                    pool.wait_ge(q_staged, 1 + UNITS * i + j)
                    rows = slice(HD * u, HD * (u + 1))
                    src = q_t[rows, bass.ds(i, 1), P * t:P * (t + 1)].rearrange("p o t -> p (o t)")
                    pool.tensor_tensor(q_stage[rows, u, :], src, ones[rows, :], ALU.mult).then_inc(q_staged, 1)

            def decays(c, n):
                tt = pool.tensor_tensor
                b = beta[0:n, bass.ds(c, 1), :].rearrange("p o h -> p h o").to_broadcast([n, H, n])
                dt, dts = d_dt[0:n, :, 0:n], d_dts[0:n, :, 0:n]
                pool.wait_ge(dt_made, c + 1)
                own.link(tt(dts, dt, b, ALU.mult))
                tt(dts, dts, neg_strict[0:n, 0:n].unsqueeze(1).to_broadcast([n, H, n]), ALU.mult).then_inc(dts_made, 1)
                pool.wait_ge(dts_made, c + 1)
                tt(d_dtq[0:n, :, 0:n], dt, tri8[0:n, 0:n].unsqueeze(1).to_broadcast([n, H, n]),
                   ALU.mult).then_inc(dtq_made, 1)
                pool.wait_ge(dtq_made, c + 1)
                pool.wait_ge(cn_made, c + 1)
                eg = d_eg.rearrange("p (u k) t -> p u k t", u=2)
                own.link(tt(d_kg[0:HD, :, 0:n], d_cn[0:HD, WT:KT, 0:n], eg[0:HD, 0, :, 0:n], ALU.mult))
                tt(d_kg[HD:P, :, 0:n], d_cn[HD:P, WT:KT, 0:n], eg[HD:P, 1, :, 0:n], ALU.mult).then_inc(kg_made, 1)
                pool.wait_ge(kg_made, c + 1)
                pool.wait_ge(kv_placed, 1 + c + 1)
                last = dt[:, :, n - 1:n].rearrange("p h o -> p (h o)")
                tt(heads(d_kd, n), heads(d_k, n), per_head(last, n, HD), ALU.mult)\
                    .then_inc(kd_made, 1)
                pool.wait_ge(kd_made, c + 1)
                pool.wait_ge(s_new, c + 1)
                own.link(tt(d_sd[0:HD], d_s[0:HD], eg[0:HD, 0, :, n - 1:n].to_broadcast([HD, WT, HD]), ALU.mult))
                tt(d_sd[HD:P], d_s[HD:P], eg[HD:P, 1, :, n - 1:n].to_broadcast([HD, WT, HD]),
                   ALU.mult).then_inc(sdec_made, 1)
                pool.wait_ge(sdec_made, c + 1)

            with pool.Fori(0, NT) as c:
                own.enter(c, 3)
                decays(c, P)
                own.leave(NT)
            pool.wait_ge(s_loaded, 16)
            decays(NT, TS)

            with pool.Fori(0, 2) as i:
                own.enter(i, 4)
                for u in range(2):
                    split(i + 8, u, dense_ready, 4 * i + 2 * u + 10)
                own.leave(2)
            with pool.Fori(0, ROUNDS) as g:
                own.enter(g, 8)
                for b, used in enumerate((-2, 0, 2, 4)):
                    split(2 * g + 10 + b // 2, b % 2, dense_ready, PER * g + MLP0 + used)
                own.leave(ROUNDS)
            split(26, 0, dense_ready, MLP0 + PER * ROUNDS, proj_hi, proj_lo)
            for b in range(2):
                split(26 + b, 1 - b, dense_ready, MLP0 + PER * ROUNDS)
            for b in range(2):
                split(27 + b, 1 - b, ple_ready, NTT)

        @block.scalar
        def _(act):
            own = Chain(act, act_own)
            for started in (sig_made, att_placed, cs_ready, cs_stored, kv_placed):
                act.sem_inc(started, 1)
            act.wait_ge(par_t, 1)
            act.activation(params[:], bank(7)[:, 0:100], ACT.Copy).then_inc(par_done, 1)

            def square_x(t, rows):
                act.wait_ge(x_loaded[t % 3], 16 * (t // 3 + 1))
                own.link(act.activation(junk[0:rows, :], x_in[0:rows, t % 3, :], ACT.Square,
                                        accum_out=small[0:rows, t:t + 1]))
                act.activation(small[0:rows, 16 + t:17 + t], small[0:rows, t:t + 1], ACT.Sqrt, scale=1.0 / D,
                               bias=eps[0:rows, :]).then_inc(x_sd, 1)

            act.wait_ge(consts_made, 2)
            square_x(0, P)
            for t, rows in enumerate(tile_rows):
                if t + 1 < NTT:
                    square_x(t + 1, tile_rows[t + 1])
                act.wait_ge(x_turned, t + 1)
                act.activation(act_hi[:, :, P * t:P * t + rows], token_banks(2 * (t % 2), rows),
                               ACT.Copy).then_inc(x_hi, 1)

            def place(y):
                t, rows = y % NTT, tile_rows[y % NTT]
                part, h = y // HALF, y // NTT % 2
                act.wait_ge(qk_turned, y + 1)
                act.activation((q_t, k_t)[part][:, HT * h:HT * (h + 1), P * t:P * t + rows],
                               bank(2 + y % 2)[:, 0:HC].rearrange("p (k t) -> p k t", k=HT)[:, :, 0:rows],
                               ACT.Copy).then_inc(qk_placed, 1)

            def store(y):
                t, rows = y % NTT, tile_rows[y % NTT]
                if y >= HALF:
                    c = HC * (y // NTT % 2)
                    act.wait_ge(qk_normed, y + 1)
                    act.dma_start(k_out[P * t:P * t + rows, c:c + HC] if t < NT else ks_out[:, c:c + HC],
                                  qk_buf[0:rows, y % 2, :]).then_inc(k_stored[y % 2], 16)

            for y in range(2 * HALF):
                rows = tile_rows[y % NTT]
                act.wait_ge(tok_ready, y + 1)
                if y:
                    act.wait_ge(ss_made, y)
                act.activation(sq_buf[0:rows, :], bank(y % 2)[0:rows, 0:HC], ACT.Square).then_inc(sq_made, 1)
                act.wait_ge(ss_made, y + 1)
                act.activation(small[0:rows, 8:8 + HH], small[0:rows, 0:HH], ACT.Sqrt, scale=1.0 / HD,
                               bias=eps[0:rows, :]).then_inc(sd_made, 1)
                if y:
                    store(y - 1)
                    place(y - 1)
            store(2 * HALF - 1)
            place(2 * HALF - 1)
            for y in range(2 * HALF, 3 * HALF):
                t, rows, c = y % NTT, tile_rows[y % NTT], HC * (y // NTT % 2)
                act.wait_ge(tok_ready, y + 1)
                act.activation(v_tok[0:rows, t, c:c + HC], bank(y % 2)[0:rows, 0:HC], ACT.Copy).then_inc(tok_free, 1)
            act.wait_ge(tok_free, 3 * HALF + 2)
            act.dma_start(v_out.rearrange("(t p) c -> p t c", p=P), v_tok[:, 0:NT, :]).then_inc(v_stored, 16)
            act.dma_start(vs_out, v_tok[0:TS, NT, :]).then_inc(v_stored, 16)
            for n in range(HALF):
                y, t, rows, c = 3 * HALF + n, n % NTT, tile_rows[n % NTT], HC * (n // NTT)
                act.wait_ge(tok_ready, y + 1)
                if n >= 2:
                    act.wait_ge(z_stored[n % 2], 16 * (n // 2))
                act.activation(z_buf[0:rows, n % 2, :], bank(y % 2)[0:rows, 0:HC], ACT.Silu).then_inc(z_silu, 1)
                act.wait_ge(z_made, n + 1)
                act.sem_inc(tok_free, 1)
                act.dma_start(z_dram[P * t:P * t + rows, c:c + HC], z_buf[0:rows, n % 2, :])\
                   .then_inc(z_stored[n % 2], 16)

            act.wait_ge(ab_ready, 1)
            both = bank(6)[:, 0:2 * H * NTT].rearrange("p (t a k u) -> p t a k u", a=2, u=2, k=WT)
            into = gates[:].rearrange("p t (a u k) -> p t a u k", a=2, u=2)
            for a in range(2):
                for u in range(2):
                    own.mark(act.activation(into[:, 0:NT, a, u, :], both[:, 0:NT, a, :, u], ACT.Copy))
                    own.mark(act.activation(into[0:TS, NT, a, u, :], both[0:TS, NT, a, :, u], ACT.Copy))
            own.wait()
            act.activation(beta[:], gates[:, :, H:2 * H], ACT.Sigmoid).then_inc(ga, 1)
            act.wait_ge(gd, 1)
            own.link(act.activation(sp_e, sp_x[1], ACT.Exp))
            act.activation(sp_e, sp_e, ACT.Ln, bias=ones[:, 0:1]).then_inc(ga, 1)
            act.activation(small[:, 56:64].rearrange("p (u k) -> p u k", u=2),
                           dn_par[:, 0, :].rearrange("p (k u) -> p u k", u=2), ACT.Exp).then_inc(ga, 1)

            with act.Fori(0, 3) as i:
                own.enter(i, 8)
                for j in range(4):
                    m = 4 * i + j
                    act.wait_ge(dense_ready, m + 1)
                    own.wait()
                    x3 = xb[:, j % 2, :]
                    pieces = [(0, 0, CH, 3), (1, 0, CH, 3 + CH), (2, 0, TP - 2 * CH, 3 + 2 * CH),
                              (2, TP - 2 * CH, CH, TP + 6)]
                    for b, lo, hi, to in pieces:
                        last = act.activation(x3[:, to:to + hi - lo], bank(3 * (j % 2) + b)[:, lo:hi], ACT.Copy)
                    own.link(last)
                    act.sem_inc(dense_free, 1)
                    hist = params[:, 64:100].rearrange("p (i m) -> p i m", m=NC)
                    act.activation(x3[:, TP + 3:TP + 6].unsqueeze(2), hist[:, :, bass.ds(m, 1)], ACT.Copy).then_inc(xb_ready, 1)
                    act.activation(tails[:, 0, :, bass.ds(m, 1)], x3[:, TP:TP + 3].unsqueeze(2), ACT.Copy)
                    own.mark(act.activation(tails[:, 1, :, bass.ds(m, 1)], x3[:, T + 3:T + 6].unsqueeze(2), ACT.Copy))
                    act.wait_ge(y_ready, m + 1)
                    act.wait_ge(cs_stored, 1 + 32 * m)
                    act.activation(cb[:, 0, :], yb, ACT.Silu).then_inc(cs_ready, 1)
                    act.wait_ge(cs_ready, 1 + m + 1)
                    dst = conv_dram[bass.ds(m, 1), :, :].rearrange("o p t -> p (o t)")
                    act.dma_start(dst[:, 0:TP], cb[:, 0, 0:TP]).then_inc(cs_stored, 16)
                    act.dma_start(dst[:, TP:T], cb[:, 0, TP + 3:T + 3]).then_inc(cs_stored, 16)
                own.leave(3)
            own.wait()
            act.sem_inc(tails_made, 1)
            act.wait_ge(tails_t, 1)
            act.activation(tails_out, bank(7)[0:72, 0:P], ACT.Copy).then_inc(tails_c, 1)

            def sigmoids(i, j):
                u, w = j % 2, P * (j // 2 + 1)
                act.wait_ge(scores_ready, 1 + UNITS * i + j + 1)
                act.wait_ge(att_turned, 1 + earlier(i, j, 2))
                z = psum[:, 2 * u:2 * u + 2, :].rearrange("p b c -> p (b c)")[:, 0:w]
                act.activation(keep_buf[:, u, 0:w], z, ACT.Sigmoid, scale=-(HD ** -0.5))
                act.activation(sig_buf[:, u, 0:w], z, ACT.Sigmoid, scale=HD ** -0.5).then_inc(sig_made, 1)

            def copy_out(i, t):
                act.wait_ge(o_ready, 1 + UNITS * i + 2 * t + 2)
                act.activation(o_buf[:, t % 2, :], bank(6 + t % 2)[:, 0:P], ACT.Copy).then_inc(o_copied, 1)

            act.wait_ge(cs_stored, 1 + 32 * NC)
            act.wait_ge(tails_stored, 32)
            for u in range(2):
                act.wait_ge(k_stored[u], 16 * NTT)
                act.wait_ge(z_stored[u], 16 * NTT)
            def copy_weights(i, j):
                w = P * (j // 2 + 1)
                act.wait_ge(att_turned, 1 + UNITS * i + j + 1)
                act.wait_ge(o_ready, 1 + earlier(i, j, 2))
                act.activation(at_buf[:, j % 2, 0:w], psum[:, 4:6, :].rearrange("p b c -> p (b c)")[:, 0:w],
                               ACT.Copy).then_inc(att_placed, 1)

            with act.Fori(0, WT) as i:
                sigmoids(i, 0)
                sigmoids(i, 1)
                copy_weights(i, 0)
                for j in range(UNITS):
                    if j + 2 < UNITS:
                        sigmoids(i, j + 2)
                    if j + 1 < UNITS:
                        copy_weights(i, j + 1)
                    if j and j % 2 == 0:
                        copy_out(i, j // 2 - 1)
                copy_out(i, NT - 1)

            for g in range(2):
                for n in range(8):
                    act.wait_ge(kc_turned, 8 * g + n + 1)
                    act.activation(kc_t[:, n // 4, 512 * (n % 4):512 * (n % 4 + 1)], bank(4 + n % 2),
                                   ACT.Copy).then_inc(kc_placed, 1)
                act.wait_ge(s_scores, g + 1)
                old = psum[:, 0:4, :].rearrange("p b c -> p (b c)")
                for dst, sign in ((keep_s, -1.0), (sig_s, 1.0)):
                    act.activation(dst[:, 0:PAST], old, ACT.Sigmoid, scale=sign * HD ** -0.5)
                    last = act.activation(dst[:, PAST:SW], bank(6)[:, 0:TS], ACT.Sigmoid, scale=sign * HD ** -0.5)
                last.then_inc(s_sig, 1)
                for n in range(5):
                    act.wait_ge(s_turned, 5 * g + n + 1)
                    rows, w = (P, 512) if n < 4 else (TS, P)
                    act.activation(at_buf[0:rows, n % 2, 0:w], bank(4 + n % 2)[0:rows, 0:w],
                                   ACT.Copy).then_inc(s_placed, 1)
                act.wait_ge(so_ready, g + 1)
                act.activation(o_buf[:, g, 0:HD], bank(7)[:, 0:HD], ACT.Copy).then_inc(so_copied, 1)

            act.wait_ge(so_split, 2)

            def act_chunk(c, n):
                act.wait_ge(c_loaded, 16 * c + 16)
                act.activation(d_rs[:, :, 0:n], d_c[:, 0:KT, 0:n], ACT.Square).then_inc(sq2_made, 1)
                act.wait_ge(gc_ready, c + 1)
                act.activation(d_gc[0:n, :], bank(5)[0:n, 0:H], ACT.Copy)
                act.activation(d_eg[:, :, 0:n], head_banks(6, P, n), ACT.Exp).then_inc(eg_made, 1)
                act.wait_ge(t0_made, c + 1)
                act.activation(d_dt[0:n, :, 0:n], d_dt[0:n, :, 0:n], ACT.Exp).then_inc(dt_made, 1)
                act.wait_ge(ss_ready, c + 1)
                act.activation(d_rs[:, :, 0:n], head_banks(0, P, n), ACT.Sqrt, bias=eps[:]).then_inc(sd2_made, 1)
                act.wait_ge(kv_turned, c + 1)
                act.activation(d_k[0:n, :], bank(2)[0:n, :], ACT.Copy)
                act.activation(d_v[0:n, :], bank(3)[0:n, :], ACT.Copy).then_inc(kv_placed, 1)
                act.wait_ge(o_made, c + 1)
                act.activation(d_oq[0:n, :].rearrange("p (u v) -> p u v", u=2), psum[0:n, 6:8, 0:4 * HD],
                               ACT.Square).then_inc(osq_made, 1)
                act.wait_ge(ored_made, c + 1)
                act.activation(small[0:n, 8:16], small[0:n, 0:8], ACT.Sqrt, scale=1.0 / HD,
                               bias=eps[0:n, :]).then_inc(osd_made, 1)

            with act.Fori(0, NT) as c:
                act_chunk(c, P)
            act_chunk(NT, TS)

            act.wait_ge(s_stored, 32)
            for t, rows in enumerate(tile_rows):
                act.wait_ge(xr_turned, t + 1)
                act.activation(h_t[:, :, P * t:P * t + rows], token_banks(2 * (t % 2), rows),
                               ACT.Copy).then_inc(h_placed, 1)

            def norm_squares(n, tiles):
                act.wait_ge(added, tiles + 2)
                for k in range(KT):
                    if k >= 2:
                        act.wait_ge(nsum, KT * n + k - 1)
                    act.activation(wide[:, k % 2, :], h_t[:, k, :], ACT.Square).then_inc(nsq_made, 1)
                act.wait_ge(nsum, KT * (n + 1))
                act.activation(wide[:, 2, :].rearrange("p (c t) -> p c t", c=3), psum[:, 0:3, 0:CH], ACT.Sqrt,
                               scale=1.0 / D, bias=eps[:]).then_inc(nsd, 1)
                for k in range(KT):
                    act.wait_ge(ntmp, KT * n + k + 1)
                    act.activation(act_hi[:, k, :], wide[:, k % 2, :], ACT.Copy).then_inc(nhi, 1)

            norm_squares(0, KT)
            with act.Fori(0, ROUNDS) as g:
                own.enter(g, 4)
                for j in range(4):
                    act.wait_ge(dense_ready, PER * g + MLP0 + j + 1)
                    act.wait_ge(hid_split, 1 + 4 * g + max(j - 1, 0))
                    w = wide[:, j % 2, :]
                    own.link(act.activation(w.rearrange("p (c t) -> p c t", c=3),
                                            psum[:, 3 * (j % 2):3 * (j % 2) + 3, 0:CH], ACT.Relu))
                    act.sem_inc(relu_free, 1)
                    act.activation(w, w, ACT.Square).then_inc(relu_made, 1)
                own.leave(ROUNDS)
            for t, rows in enumerate(tile_rows):
                act.wait_ge(p_turned, t + 1)
                act.activation(hid_hi[:, 0:2, P * t:P * t + rows],
                               bank(6 + t % 2)[:, 0:256].rearrange("p (k t) -> p k t", k=2)[:, :, 0:rows],
                               ACT.Copy).then_inc(p_hi, 1)
            norm_squares(1, KT + KT * ROUNDS)
            act.wait_ge(nlo, 2 * KT)
            for y in range(2 * NTT):
                rows = tile_rows[y % NTT]
                act.wait_ge(ple_ready, y + 1)
                act.activation(sg_buf[0:rows, y % 2, :], bank(y % 2)[0:rows, :], ACT.Sigmoid).then_inc(sg_made, 1)

        @block.vector
        def _(dve):
            own = Chain(dve, dve_own)
            for started in (o_split, on_made, mix_split, hid_split):
                dve.sem_inc(started, 1)
            dve.wait_ge(vecs_loaded, 160)

            def scale_x(t, rows):
                dve.wait_ge(x_sd, t + 1)
                own.link(dve.reciprocal(small[0:rows, 32 + t:33 + t], small[0:rows, 16 + t:17 + t]))
                if t >= 2:
                    dve.wait_ge(x_turned, t - 1)
                dve.scalar_tensor_tensor(out=x_sc[0:rows, t % 2, :], in0=x_in[0:rows, t % 3, :],
                                         scalar=small[0:rows, 32 + t:33 + t], in1=gmix_b[0:rows, :],
                                         op0=ALU.mult, op1=ALU.mult).then_inc(x_scaled, 1)

            scale_x(0, P)
            for t, rows in enumerate(tile_rows):
                if t + 1 < NTT:
                    scale_x(t + 1, tile_rows[t + 1])
                dve.wait_ge(x_hi, t + 1)
                cols = slice(P * t, P * t + rows)
                dve.tensor_tensor(act_lo[:, :, cols], token_banks(2 * (t % 2), rows),
                                  act_hi[:, :, cols].bitcast(F32), ALU.subtract).then_inc(x_lo, 1)

            dve.wait_ge(x_sd, NTT)
            for y in range(2 * HALF):
                rows = tile_rows[y % NTT]
                dve.wait_ge(sq_made, y + 1)
                dve.tensor_reduce(small[0:rows, 0:HH], sq_buf[0:rows, :].rearrange("p (h d) -> p h d", h=HH),
                                  AX.X, ALU.add).then_inc(ss_made, 1)
                dve.wait_ge(sd_made, y + 1)
                own.link(dve.reciprocal(small[0:rows, 48:48 + HH], small[0:rows, 8:8 + HH]))
                if y >= 2:
                    dve.wait_ge(qk_turned, y - 1)
                if y >= HALF + 2:
                    dve.wait_ge(k_stored[y % 2], 16 * ((y - HALF) // 2))
                buf = qk_buf[0:rows, y % 2, :].rearrange("p (h d) -> p h d", h=HH)
                own.link(dve.tensor_tensor(buf, bank(y % 2)[0:rows, 0:HC].rearrange("p (h d) -> p h d", h=HH),
                                           small[0:rows, 48:48 + HH].unsqueeze(2).to_broadcast([rows, HH, HD]),
                                           ALU.mult))
                dve.sem_inc(tok_free, 1)
                g = heads_g[0:rows, y // HALF:y // HALF + 1, :].to_broadcast([rows, HH, HD])
                dve.tensor_tensor(buf, buf, g, ALU.mult).then_inc(qk_normed, 1)
            for n in range(HALF):
                rows = tile_rows[n % NTT]
                dve.wait_ge(z_silu, n + 1)
                buf = z_buf[0:rows, n % 2, :].rearrange("p (h d) -> p h d", h=HH)
                dve.tensor_tensor(buf, buf, heads_g[0:rows, 2:3, :].to_broadcast([rows, HH, HD]),
                                  ALU.mult).then_inc(z_made, 1)
            dve.wait_ge(ga, 1)
            al, nal = sp_x
            bias = dn_par[:, 1, :].rearrange("p (k u) -> p u k", u=2).unsqueeze(1).to_broadcast([P, NTT, 2, WT])
            own.link(dve.tensor_tensor(al.rearrange("p t (u k) -> p t u k", u=2),
                                       gates[:, :, 0:H].rearrange("p t (u k) -> p t u k", u=2), bias, ALU.add))
            dve.scalar_tensor_tensor(out=nal, in0=al, scalar=-1.0, in1=al, op0=ALU.mult, op1=ALU.min).then_inc(gd, 1)
            dve.wait_ge(ga, 3)
            own.link(dve.scalar_tensor_tensor(out=al, in0=al, scalar=0.0, in1=sp_e, op0=ALU.max, op1=ALU.add))
            own.link(dve.scalar_tensor_tensor(out=glog[:], in0=al, scalar=-1.0,
                                              in1=small[:, 56:64].unsqueeze(1).to_broadcast([P, NTT, H]),
                                              op0=ALU.mult, op1=ALU.mult))
            own.link(dve.memset(xb[:, :, 0:3], 0.0))
            with dve.Fori(0, 3) as i:
                own.enter(i, 12)
                for j in range(4):
                    m = 4 * i + j
                    dve.wait_ge(xb_ready, m + 1)
                    dve.wait_ge(cs_ready, 1 + m)
                    taps = params[:, 16:64].rearrange("p (i m) -> p i m", m=NC)
                    x3 = xb[:, j % 2, :]
                    for tap in range(4):
                        w = taps[:, tap, bass.ds(m, 1)]
                        if tap == 0:
                            own.link(dve.tensor_scalar(yb, x3[:, 0:YB], w, None, ALU.mult))
                        elif tap < 3:
                            own.link(dve.scalar_tensor_tensor(out=yb, in0=x3[:, tap:tap + YB], scalar=w, in1=yb,
                                                              op0=ALU.mult, op1=ALU.add))
                        else:
                            dve.scalar_tensor_tensor(out=yb, in0=x3[:, tap:tap + YB], scalar=w, in1=yb,
                                                     op0=ALU.mult, op1=ALU.add).then_inc(y_ready, 1)
                own.leave(3)

            def split_out(i, t):
                dve.wait_ge(o_turned, NT * i + t + 1)
                src = bank(6 + t % 2)[:, P:2 * P].unsqueeze(1)
                cols = slice(P * t, P * (t + 1))
                dst = act_hi[:, bass.ds(WT + i, 1), cols]
                own.link(dve.tensor_copy(dst, src))
                own.link(dve.tensor_tensor(act_lo[:, bass.ds(WT + i, 1), cols], src, dst.bitcast(F32),
                                           ALU.subtract))
                dve.sem_inc(o_split, 1)

            with dve.Fori(0, WT) as i:
                own.enter(i, 3 * UNITS + 2 * NT)
                for j in range(UNITS):
                    u, w = j % 2, P * (j // 2 + 1)
                    keep, sig = keep_buf[:, u, :], sig_buf[:, u, :]
                    dve.wait_ge(sig_made, 1 + UNITS * i + j + 1)
                    own.mark(dve.tensor_tensor(sig[:, w - P:w], sig[:, w - P:w], below[:], ALU.mult))
                    own.link(dve.tensor_tensor(keep[:, w - P:w], keep[:, w - P:w], not_below[:], ALU.max))
                    back = keep[:, 0:w][:, ::-1]
                    own.link(dve.tensor_tensor_scan(back, back, back, 1.0, ALU.mult, ALU.min))
                    dve.tensor_tensor(sig[:, 0:w - 1], sig[:, 0:w - 1], keep[:, 1:w], ALU.mult).then_inc(att_made, 1)
                    if j % 2 and j >= 5:
                        split_out(i, (j - 5) // 2)
                split_out(i, NT - 2)
                split_out(i, NT - 1)
                own.leave(WT)

            for g in range(2):
                dve.wait_ge(s_sig, g + 1)
                own.mark(dve.tensor_tensor(sig_s[:, PAST:SW], sig_s[:, PAST:SW], below_s[:, 0, :], ALU.mult))
                own.link(dve.tensor_tensor(keep_s[:, PAST:SW], keep_s[:, PAST:SW], below_s[:, 1, :], ALU.max))
                back = keep_s[:, ::-1]
                own.link(dve.tensor_tensor_scan(back, back, back, 1.0, ALU.mult, ALU.min))
                dve.tensor_tensor(sig_s[:, 0:SW - 1], sig_s[:, 0:SW - 1], keep_s[:, 1:SW],
                                  ALU.mult).then_inc(s_att, 1)
                dve.wait_ge(so_turned, g + 1)
                src = psum[:, 5:7, 64:64 + TS]
                dst = act_hi[:, WT + 2 * g:WT + 2 * g + 2, TP:T]
                own.link(dve.tensor_copy(dst, src))
                dve.tensor_tensor(act_lo[:, WT + 2 * g:WT + 2 * g + 2, TP:T], src, dst.bitcast(F32),
                                  ALU.subtract).then_inc(so_split, 1)

            dve.memset(d_s, 0.0).then_inc(s_new, 1)

            def dve_chunk(c, n):
                tt = dve.tensor_tensor
                L = levels_of(n)
                square = [n, H, n]
                g = glog[0:n, bass.ds(c, 1), :].rearrange("p o h -> p h o").to_broadcast(square)
                tt(d_gu[0:n, :, 0:n], tri[0:n, 0:n].unsqueeze(1).to_broadcast(square), g, ALU.mult).then_inc(gu_made, 1)
                dve.wait_ge(eg_made, c + 1)
                dt = d_dt[0:n, :, 0:n]
                own.link(tt(dt, head_banks(6, n, n), d_gc[0:n, :].unsqueeze(2).to_broadcast(square), ALU.subtract))
                dve.tensor_scalar(dt, dt, 0.0, None, ALU.min).then_inc(t0_made, 1)
                dve.wait_ge(sd2_made, c + 1)
                rs = d_rs[:, :, 0:n]
                own.link(dve.reciprocal(rs, rs))
                own.mark(tt(d_cn[:, :, 0:n], d_c[:, 0:KT, 0:n], rs, ALU.mult))
                own.wait()
                dve.sem_inc(cn_made, 1)
                for u in range(2):
                    rows = slice(HD * u, HD * (u + 1))
                    own.mark(dve.scalar_tensor_tensor(out=d_qg[rows, :, 0:n], in0=d_cn[rows, 0:WT, 0:n],
                                                      scalar=HD ** -0.5, in1=d_eg[rows, 4 * u:4 * u + 4, 0:n],
                                                      op0=ALU.mult, op1=ALU.mult))
                dve.wait_ge(g_ready, c + 1)
                dve.wait_ge(dts_made, c + 1)
                tt(d_at[0:n, :, 0:n], head_banks(0, n, n), d_dts[0:n, :, 0:n], ALU.mult).then_inc(at_made, 1)
                dve.wait_ge(qk_ready, c + 1)
                dve.wait_ge(dtq_made, c + 1)
                own.mark(tt(d_qt[0:n, :, 0:n], head_banks(4, n, n), d_dtq[0:n, :, 0:n], ALU.mult))
                own.wait()
                dve.sem_inc(qt_made, 1)
                for l in range(L):
                    for g in range(2):
                        hs = slice(4 * g, 4 * g + 4)
                        dve.wait_ge(m_ready, step_of(c, l, g))
                        tt(d_m[0:n, hs, 0:n], bank(g)[0:n, :].rearrange("p (h t) -> p h t", h=4)[:, :, 0:n],
                           level[0:n, l, 0:n].unsqueeze(1).to_broadcast([n, 4, n]), ALU.mult).then_inc(m_made, 1)
                    for g in range(2):
                        hs = slice(4 * g, 4 * g + 4)
                        dve.wait_ge(m_made, step_of(c, l, g))
                        dve.wait_ge(xt_ready, step_of(c, l, g))
                        eye = ident[0:n, 0:n].unsqueeze(1).to_broadcast([n, 4, n])
                        t_, x_ = d_t[0:n, hs, 0:n], d_x[0:n, hs, 0:n]
                        pt, px = (bank(b + g)[0:n, :].rearrange("p (h t) -> p h t", h=4)[:, :, 0:n] for b in (2, 4))
                        if l == 0:
                            own.mark(tt(t_, d_m[0:n, hs, 0:n], eye, ALU.add))
                        elif l < L - 1:
                            own.mark(tt(t_, pt, t_, ALU.add))
                        own.mark(tt(x_, px, eye if l == 0 else x_, ALU.add))
                        own.wait()
                        dve.sem_inc(xt_made, 1)
                dve.wait_ge(ks_ready, c + 1)
                tt(heads(d_r, n), heads(d_v, n), value_banks(n), ALU.subtract).then_inc(r_made, 1)
                dve.wait_ge(vn_ready, c + 1)
                b = per_head(beta[0:n, bass.ds(c, 1), :].rearrange("p o h -> p (o h)"), n, HD)
                tt(heads(d_vn, n), heads(bank(3), n), b, ALU.mult)\
                    .then_inc(vn_made, 1)
                dve.wait_ge(ds_ready, c + 1)
                dve.wait_ge(sdec_made, c + 1)
                tt(d_s, bank(2)[:, 0:4 * HD].rearrange("p (k e) -> p k e", k=WT), d_sd, ALU.add).then_inc(s_new, 1)
                dve.wait_ge(osq_made, c + 1)
                dve.tensor_reduce(small[0:n, 0:8], d_oq[0:n, :].rearrange("p (h d) -> p h d", h=H), AX.X,
                                  ALU.add).then_inc(ored_made, 1)
                dve.wait_ge(osd_made, c + 1)
                own.link(dve.reciprocal(small[0:n, 48:56], small[0:n, 8:16]))
                own.link(tt(heads(d_on, n), value_banks(n), per_head(small[0:n, 48:56], n, HD), ALU.mult))
                dve.wait_ge(z_loaded, 16 * c + 16)
                tt(d_on[0:n, :], d_on[0:n, :], d_z[0:n, :], ALU.mult).then_inc(on_made, 1)
                dve.wait_ge(ot_ready, c + 1)
                src = bank(5).rearrange("p (k t) -> p k t", k=WT)[:, :, 0:n]
                cols = bass.ds(P * c, n)
                own.link(dve.tensor_copy(act_hi[:, 0:WT, cols], src))
                own.link(tt(act_lo[:, 0:WT, cols], src, act_hi[:, 0:WT, cols].bitcast(F32), ALU.subtract))
                dve.sem_inc(mix_split, 1)

            with dve.Fori(0, NT) as c:
                own.enter(c, 6 + 4 * LEVELS - 2 + 4)
                dve_chunk(c, P)
                own.leave(NT)
            dve_chunk(NT, TS)

            def add_tile(J, b, k):
                dve.wait_ge(dense_ready, J + 1)
                h3 = h_t[:, k, :].rearrange("p o (c t) -> p (o c) t", c=3)
                dve.tensor_tensor(h3, psum[:, b:b + 3, 0:CH], h3, ALU.add).then_inc(added, 1)

            dve.wait_ge(h_placed, NTT)
            with dve.Fori(0, 2) as i:
                for j in range(4):
                    add_tile(4 * i + j + OUT0, 3 * (j % 2), bass.ds(4 * i + j, 1))

            def norm_scale(n, gain):
                dve.wait_ge(nsd, n + 1)
                own.link(dve.reciprocal(wide[:, 2, :], wide[:, 2, :]))

                def scaled(k):
                    dve.scalar_tensor_tensor(out=wide[:, k % 2, :], in0=h_t[:, k, :],
                                             scalar=params[:, gain + k:gain + k + 1], in1=wide[:, 2, :],
                                             op0=ALU.mult, op1=ALU.mult).then_inc(ntmp, 1)

                scaled(0)
                for k in range(KT):
                    if k + 1 < KT:
                        if k:
                            dve.wait_ge(nlo, KT * n + k)
                        scaled(k + 1)
                    dve.wait_ge(nhi, KT * n + k + 1)
                    dve.tensor_tensor(act_lo[:, k, :], wide[:, k % 2, :], act_hi[:, k, :].bitcast(F32),
                                      ALU.subtract).then_inc(nlo, 1)

            norm_scale(0, 0)
            with dve.Fori(0, ROUNDS) as g:
                own.enter(g, 4)
                for j in range(4):
                    dve.wait_ge(relu_made, 4 * g + j + 1)
                    own.link(dve.tensor_copy(hid_hi[:, j, :], wide[:, j % 2, :]))
                    dve.tensor_tensor(hid_lo[:, j, :], wide[:, j % 2, :], hid_hi[:, j, :].bitcast(F32),
                                      ALU.subtract).then_inc(hid_split, 1)
                for j in range(KT):
                    add_tile(PER * g + MLP0 + 4 + j, 3 * (j % 2), slice(j, j + 1))
                own.leave(ROUNDS)
            for t, rows in enumerate(tile_rows):
                cols = slice(P * t, P * t + rows)
                dve.wait_ge(p_hi, t + 1)
                dve.tensor_tensor(hid_lo[:, 0:2, cols],
                                  bank(6 + t % 2)[:, 0:256].rearrange("p (k t) -> p k t", k=2)[:, :, 0:rows],
                                  hid_hi[:, 0:2, cols].bitcast(F32), ALU.subtract).then_inc(p_lo, 1)
            norm_scale(1, KT)
            for y in range(2 * NTT):
                rows = tile_rows[y % NTT]
                dve.wait_ge(sg_made, y + 1)
                sg = sg_buf[0:rows, y % 2, :]
                own.link(dve.tensor_tensor(sg, bank(2 + y % 2)[0:rows, :], sg, ALU.mult))
                if y >= 2:
                    dve.wait_ge(y_stored[y % 2], 16 * (y // 2))
                dve.tensor_tensor(y_buf[0:rows, y % 2, :], bank(4 + y % 2)[0:rows, :], sg, ALU.add).then_inc(y_made, 1)

        @block.tensor
        def _(pe):
            for started in (scores_ready, att_turned, o_ready):
                pe.sem_inc(started, 1)
            pe.sem_inc(tok_free, 2)
            pe.sem_inc(dense_free, 2)
            pe.sem_inc(added, 2)
            pe.wait_ge(consts_made, 2)
            pe.wait_ge(vecs_loaded, 160)
            pe.transpose(bank(7)[:, 0:100], param_rows[0:100, :], ident[0:100, 0:100]).then_inc(par_t, 1)
            for t, rows in enumerate(tile_rows):
                pe.wait_ge(x_scaled, t + 1)
                if t >= 2:
                    pe.wait_ge(x_lo, t - 1)
                for k in range(KT):
                    last = pe.transpose(bank(2 * (t % 2) + k // 4)[:, P * (k % 4):P * (k % 4) + rows],
                                        x_sc[0:rows, t % 2, P * k:P * k + P], ident[0:rows, 0:rows])
                last.then_inc(x_turned, 1)
            pe.wait_ge(x_lo, NTT)

            def token_product(out, rows, t, w_h, w_l, K=KT, hi=act_hi, lo=act_lo):
                cols = slice(P * t, P * t + rows)
                for k in range(K):
                    pe.matmul(out, hi[:, k, cols], w_h(k), start=(k == 0), stop=False)
                    pe.matmul(out, hi[:, k, cols], w_l(k), start=False, stop=False)
                    last = pe.matmul(out, lo[:, k, cols], w_h(k), start=False, stop=(k == K - 1))
                return last

            def turn_qk(y):
                t, rows = y % NTT, tile_rows[y % NTT]
                pe.wait_ge(qk_normed, y + 1)
                if y >= 2:
                    pe.wait_ge(qk_placed, y - 1)
                for k in range(HT):
                    last = pe.transpose(bank(2 + y % 2)[:, P * k:P * k + rows],
                                        qk_buf[0:rows, y % 2, P * k:P * k + P], ident[0:rows, 0:rows])
                last.then_inc(qk_turned, 1)

            for b in range(8):
                pe.wait_ge(w_split, b + 1)
                for t, rows in enumerate(tile_rows):
                    y = NTT * b + t
                    pe.wait_ge(tok_free, y + 1)
                    token_product(bank(y % 2)[0:rows, 0:HC], rows, t, lambda k: whi_cols[:, b % 2, k, :],
                                  lambda k: wlo_cols[:, b % 2, k, :]).then_inc(tok_ready, 1)
                    if 1 <= y <= 2 * HALF:
                        turn_qk(y - 1)
            pe.wait_ge(ab_split, 1)
            for t, rows in enumerate(tile_rows):
                last = token_product(bank(6)[0:rows, 2 * H * t:2 * H * (t + 1)], rows, t,
                                     lambda k: ab_hi[:, k, :], lambda k: ab_lo[:, k, :])
            last.then_inc(ab_ready, 1)

            def dense(base, lhs_hi, lhs_lo, K=KT, hi=act_hi, lo=act_lo, before=None):
                for k in range(K):
                    if before:
                        before(k)
                    for w, a in ((lhs_hi, hi), (lhs_hi, lo), (lhs_lo, hi)):
                        for c in range(3):
                            last = pe.matmul(bank(base + c)[:, 0:CH], w(k), a[:, k, CH * c:CH * (c + 1)],
                                             start=(k == 0 and w is lhs_hi and a is hi),
                                             stop=(k == K - 1 and w is lhs_lo))
                return last

            pe.wait_ge(tok_free, 4 * HALF + 2)
            pe.wait_ge(qk_placed, 2 * HALF)
            with pe.Fori(0, 3) as i:
                for j in range(4):
                    slot, mm = j // 2, j % 2
                    if mm == 0:
                        pe.wait_ge(w_split, 8 + 2 * i + slot + 1)
                    pe.wait_ge(dense_free, 4 * i + j + 1)
                    last = dense(3 * (j % 2), lambda k: whi_cols[:, slot, k, P * mm:P * mm + P],
                                 lambda k: wlo_cols[:, slot, k, P * mm:P * mm + P])
                    last.then_inc(dense_ready, 1)
            pe.wait_ge(tails_made, 1)
            pe.transpose(bank(7)[0:72, 0:P], tails[:].rearrange("p a i m -> p (a i m)"), ident[:]).then_inc(tails_t, 1)

            def scores(i, j):
                u, w = j % 2, P * (j // 2 + 1)
                pe.wait_ge(q_staged, 1 + UNITS * i + j + 1)
                pe.wait_ge(sig_made, 1 + earlier(i, j, 2))
                for c in range(0, w, 512):
                    n = min(512, w - c)
                    last = pe.matmul(bank(2 * u + c // 512)[:, 0:n], q_stage[:, u, :],
                                     k_t[:, bass.ds(i, 1), c:c + n].rearrange("p o t -> p (o t)"),
                                     start=True, stop=True)
                last.then_inc(scores_ready, 1)

            def turn_out(i, t):
                pe.wait_ge(o_copied, NT * i + t + 1)
                pe.transpose(bank(6 + t % 2)[:, P:2 * P], o_buf[:, t % 2, :], ident[:]).then_inc(o_turned, 1)

            def turn_weights(i, j):
                pe.wait_ge(att_made, UNITS * i + j + 1)
                pe.wait_ge(att_placed, 1 + UNITS * i + j)
                for n in range(j // 2 + 1):
                    last = pe.transpose(bank(4 + n // 4)[:, P * (n % 4):P * (n % 4 + 1)],
                                        sig_buf[:, j % 2, P * n:P * (n + 1)], ident[:])
                last.then_inc(att_turned, 1)

            def values(i, j):
                u, t = j % 2, j // 2
                pe.wait_ge(att_placed, 1 + UNITS * i + j + 1)
                if u == 0:
                    pe.wait_ge(o_split, 1 + NT * i + max(t - 1, 0))
                for n in range(t + 1):
                    v = v_tok[:, n, bass.ds(P * i + HD * u, HD)]
                    last = pe.matmul(bank(6 + t % 2)[:, HD * u:HD * (u + 1)], at_buf[:, u, P * n:P * (n + 1)], v,
                                     start=(n == 0), stop=(n == t))
                last.then_inc(o_ready, 1)

            with pe.Fori(0, WT) as i:
                scores(i, 0)
                scores(i, 1)
                turn_weights(i, 0)
                for j in range(UNITS):
                    if j + 2 < UNITS:
                        scores(i, j + 2)
                    if j + 1 < UNITS:
                        turn_weights(i, j + 1)
                    values(i, j)
                    if j % 2 and j >= 3:
                        turn_out(i, (j - 3) // 2)
                turn_out(i, NT - 1)

            pe.wait_ge(o_split, 1 + WT * NT)
            pe.wait_ge(s_staged, 1)
            for g in range(2):
                pe.wait_ge(kc_loaded, 16 * (g + 1))
                if g:
                    pe.wait_ge(so_split, g)
                for n in range(8):
                    if 8 * g + n >= 2:
                        pe.wait_ge(kc_placed, 8 * g + n - 1)
                    for b in range(4):
                        last = pe.transpose(bank(4 + n % 2)[:, P * b:P * (b + 1)],
                                            k_raw[:, 4 * (n % 4) + b, P * (n // 4):P * (n // 4 + 1)], ident[:])
                    last.then_inc(kc_turned, 1)
                pe.wait_ge(kc_placed, 8 * (g + 1))
                for j in range(4):
                    q = q_s[:, 2 * g + j // 2, j % 2, :]
                    for c in range(PAST // 512):
                        pe.matmul(psum[TS * j:TS * (j + 1), c, :], q, kc_t[:, j // 2, 512 * c:512 * (c + 1)],
                                  start=True, stop=True)
                    last = pe.matmul(psum[TS * j:TS * (j + 1), 6, 0:TS], q, k_s[:, 2 * g + j // 2, :],
                                     start=True, stop=True)
                last.then_inc(s_scores, 1)
                pe.wait_ge(s_att, g + 1)
                pe.wait_ge(vc_loaded, 16 * (g + 1))

                def turn_stacked(n):
                    rows = P if n < 4 else TS
                    if n >= 2:
                        pe.wait_ge(s_placed, 5 * g + n - 1)
                    for b in range(4 if n < 4 else 1):
                        src = sig_s[:, 512 * n + P * b:512 * n + P * b + rows]
                        last = pe.transpose(bank(4 + n % 2)[0:rows, P * b:P * (b + 1)], src, ident[:])
                    last.then_inc(s_turned, 1)

                turn_stacked(0)
                for n in range(5):
                    if n < 4:
                        turn_stacked(n + 1)
                    pe.wait_ge(s_placed, 5 * g + n + 1)
                    for b in range(4 if n < 4 else 1):
                        for j in range(4):
                            rows = P if n < 4 else TS
                            v = v_c[:, 4 * n + b, HD * j:HD * (j + 1)] if n < 4 else \
                                v_s[0:TS, HD * (4 * g + j):HD * (4 * g + j + 1)]
                            last = pe.matmul(bank(7)[TS * j:TS * (j + 1), 0:HD],
                                             at_buf[0:rows, n % 2, P * b + TS * j:P * b + TS * (j + 1)], v,
                                             start=(n == 0 and b == 0), stop=(n == 4))
                last.then_inc(so_ready, 1)
                pe.wait_ge(so_copied, g + 1)
                for j in range(4):
                    rows = slice(TS * j, TS * (j + 1))
                    last = pe.matmul(psum[HD * (j % 2):HD * (j % 2 + 1), 5 + j // 2, 64:64 + TS],
                                     o_buf[rows, g, 0:HD], ident[rows, rows], start=True, stop=True)
                last.then_inc(so_turned, 1)

            pe.wait_ge(so_split, 2)

            def pe_chunk(c, n):
                L = levels_of(n)

                def group(b, h):
                    return bank(b + h % 2)[0:n, P * (h // 2):P * (h // 2) + n]

                def value(h):
                    return bank(6 + h % 2)[0:n, HD * (h // 2):HD * (h // 2 + 1)]

                def half(h):
                    return slice(HD * (h % 2), HD * (h % 2) + HD)

                pe.wait_ge(mix_split, 1 + c)
                pe.wait_ge(gu_made, c + 1)
                for g in range(2):
                    pe.matmul(bank(6 + g).rearrange("p (h t) -> p h t", h=4)[:, :, 0:n], ones[0:n, :],
                              d_gu[0:n, 4 * g:4 * g + 4, 0:n], start=True, stop=True)
                pe.matmul(bank(5)[0:n, 0:H], tri[0:n, 0:n], glog[0:n, bass.ds(c, 1), :].rearrange("p o h -> p (o h)"),
                          start=True, stop=True).then_inc(gc_ready, 1)
                pe.wait_ge(sq2_made, c + 1)
                for g in range(2):
                    last = pe.matmul(bank(g).rearrange("p (h t) -> p h t", h=4)[:, :, 0:n], halves[:],
                                     d_rs[:, 4 * g:4 * g + 4, 0:n], start=True, stop=True)
                last.then_inc(ss_ready, 1)
                pe.wait_ge(cn_made, c + 1)
                for k in range(WT):
                    pe.transpose(bank(2)[0:n, P * k:P * (k + 1)], d_cn[:, WT + k, 0:n], ident[:])
                for k in range(WT):
                    last = pe.transpose(bank(3)[0:n, P * k:P * (k + 1)], d_c[:, 2 * WT + k, 0:n], ident[:])
                last.then_inc(kv_turned, 1)
                for b, at, signal in ((0, WT, g_ready), (4, 0, qk_ready)):
                    if at == 0:
                        pe.wait_ge(eg_made, c + 1)
                    for h in range(H):
                        last = pe.matmul(group(b, h), d_cn[half(h), WT + h // 2, 0:n],
                                         d_cn[half(h), at + h // 2, 0:n], start=True, stop=True)
                    last.then_inc(signal, 1)
                for l in range(L):
                    for g in range(2):
                        if l == 0:
                            pe.wait_ge(at_made, c + 1)
                        else:
                            pe.wait_ge(xt_made, step_of(c, l - 1, g))
                        for h in range(g, H, 2):
                            if l == 0:
                                last = pe.transpose(group(0, h), d_at[0:n, place_of(h), 0:n], ident[0:n, 0:n])
                            else:
                                last = pe.matmul(group(0, h), d_at[0:n, place_of(h), 0:n], d_t[0:n, place_of(h), 0:n],
                                                 start=True, stop=True)
                        last.then_inc(m_ready, 1)
                    for g in range(2):
                        pe.wait_ge(m_made, step_of(c, l, g))
                        if l == 0:
                            pe.wait_ge(kv_placed, 1 + c + 1)
                            pe.wait_ge(qt_made, c + 1)
                        for h in range(g, H, 2):
                            m = d_m[0:n, place_of(h), 0:n]
                            if l == 0:
                                last = pe.transpose(group(4, h), m, ident[0:n, 0:n])
                            else:
                                if l < L - 1:
                                    pe.matmul(group(2, h), d_x[0:n, place_of(h), 0:n], m, start=True, stop=True)
                                last = pe.matmul(group(4, h), m, d_x[0:n, place_of(h), 0:n], start=True, stop=True)
                        last.then_inc(xt_ready, 1)
                pe.wait_ge(kg_made, c + 1)
                pe.wait_ge(s_new, c + 1)
                if n == TS:
                    pe.wait_ge(s_loaded, 16)
                for h in range(H):
                    last = pe.matmul(value(h), d_kg[half(h), h // 2, 0:n],
                                     d_s[half(h), h // 2, :], start=True, stop=True)
                last.then_inc(ks_ready, 1)
                pe.wait_ge(r_made, c + 1)
                pe.wait_ge(xt_made, step_of(c, L - 1, 1))
                for h in range(H):
                    cols = slice(HD * h, HD * (h + 1))
                    last = pe.matmul(bank(3)[0:n, cols], d_x[0:n, place_of(h), 0:n], d_r[0:n, cols], start=True, stop=True)
                last.then_inc(vn_ready, 1)
                pe.wait_ge(vn_made, c + 1)
                for h in range(H):
                    cols = slice(HD * h, HD * (h + 1))
                    pe.matmul(value(h), d_qg[half(h), h // 2, 0:n], d_s[half(h), h // 2, :],
                              start=True, stop=False)
                    last = pe.matmul(value(h), d_qt[0:n, place_of(h), 0:n], d_vn[0:n, cols], start=False, stop=True)
                last.then_inc(o_made, 1)
                pe.wait_ge(kd_made, c + 1)
                for h in range(H):
                    cols = slice(HD * h, HD * (h + 1))
                    last = pe.matmul(bank(2)[half(h), HD * (h // 2):HD * (h // 2 + 1)], d_kd[0:n, cols],
                                     d_vn[0:n, cols], start=True, stop=True)
                last.then_inc(ds_ready, 1)
                pe.wait_ge(on_made, 1 + c + 1)
                for k in range(WT):
                    last = pe.transpose(bank(5)[:, P * k:P * k + n], d_on[0:n, P * k:P * (k + 1)], ident[0:n, 0:n])
                last.then_inc(ot_ready, 1)

            with pe.Fori(0, NT) as c:
                pe_chunk(c, P)
            pe_chunk(NT, TS)

            pe.wait_ge(mix_split, 1 + CHUNKS)
            for t, rows in enumerate(tile_rows):
                pe.wait_ge(xr_loaded[t % 3], 16 * (t // 3 + 1))
                if t >= 2:
                    pe.wait_ge(h_placed, t - 1)
                for k in range(KT):
                    last = pe.transpose(bank(2 * (t % 2) + k // 4)[:, P * (k % 4):P * (k % 4) + rows],
                                        xr_in[0:rows, t % 3, P * k:P * k + P], ident[0:rows, 0:rows])
                last.then_inc(xr_turned, 1)
            pe.wait_ge(h_placed, NTT)
            with pe.Fori(0, 2) as i:
                for j in range(4):
                    slot, mm = j // 2, j % 2
                    if mm == 0:
                        pe.wait_ge(w_split, 14 + 2 * i + slot + 1)
                    pe.wait_ge(added, 4 * i + j + 1)
                    dense(3 * (j % 2), lambda k: whi_cols[:, slot, k, P * mm:P * mm + P],
                          lambda k: wlo_cols[:, slot, k, P * mm:P * mm + P]).then_inc(dense_ready, 1)

            def norm_sums(n, tiles):
                pe.wait_ge(added, tiles + 2)
                for k in range(KT):
                    pe.wait_ge(nsq_made, KT * n + k + 1)
                    for c in range(3):
                        last = pe.matmul(bank(c)[:, 0:CH], ones[:], wide[:, k % 2, CH * c:CH * (c + 1)],
                                         start=(k == 0), stop=(k == KT - 1))
                    last.then_inc(nsum, 1)

            norm_sums(0, KT)
            pe.wait_ge(nsd, 1)
            whi_down = w_hi[:, :, :].rearrange("p s (k n) -> p s k n", k=4)
            wlo_down = w_lo[:, :, :].rearrange("p s (k n) -> p s k n", k=4)
            with pe.Fori(0, ROUNDS) as g:
                for j in range(PER):
                    if 2 <= j < 6:
                        pe.wait_ge(relu_free, 4 * g + j - 1)
                    else:
                        pe.wait_ge(added, KT * g + KT + (1 + j if j < 2 else j - 3))
                    if j < 4:
                        slot, mm = j // 2, j % 2
                        if mm == 0:
                            pe.wait_ge(w_split, 18 + 4 * g + slot + 1)
                        last = dense(3 * (j % 2), lambda k: whi_cols[:, slot, k, P * mm:P * mm + P],
                                     lambda k: wlo_cols[:, slot, k, P * mm:P * mm + P],
                                     before=(lambda k: pe.wait_ge(nlo, k + 1)) if j == 0 else None)
                    else:
                        slot, mm = (j - 4) // 4, (j - 4) % 4
                        if mm == 0:
                            pe.wait_ge(w_split, 20 + 4 * g + slot + 1)
                        last = dense(3 * (j % 2), lambda k: whi_down[:, slot, k, P * mm:P * mm + P],
                                     lambda k: wlo_down[:, slot, k, P * mm:P * mm + P], 4, hid_hi, hid_lo,
                                     before=(lambda k: pe.wait_ge(hid_split, 1 + 4 * g + k + 1)) if j == 4 else None)
                    last.then_inc(dense_ready, 1)

            for t, rows in enumerate(tile_rows):
                pe.wait_ge(p_loaded[t % 2], 16 * (t // 2 + 1))
                if t >= 2:
                    pe.wait_ge(p_lo, t - 1)
                for k in range(2):
                    last = pe.transpose(bank(6 + t % 2)[:, P * k:P * k + rows], p_in[0:rows, t % 2, P * k:P * k + P],
                                        ident[0:rows, 0:rows])
                last.then_inc(p_turned, 1)
            norm_sums(1, KT + KT * ROUNDS)
            pe.wait_ge(nlo, 2 * KT)
            pe.wait_ge(p_lo, NTT)
            pj_hi = proj_hi.rearrange("p (k n) -> p k n", k=2)
            pj_lo = proj_lo.rearrange("p (k n) -> p k n", k=2)
            for half in range(2):
                pe.wait_ge(w_split, 53 + 2 * half)
                for t, rows in enumerate(tile_rows):
                    y = NTT * half + t
                    if y >= 2:
                        pe.wait_ge(y_made, y - 1)
                    token_product(bank(y % 2)[0:rows, :], rows, t, lambda k: whi_cols[:, ::-1, k, :],
                                  lambda k: wlo_cols[:, ::-1, k, :])
                    token_product(bank(2 + y % 2)[0:rows, :], rows, t, lambda k: pj_hi[:, k, 512 * half:512 * half + 512],
                                  lambda k: pj_lo[:, k, 512 * half:512 * half + 512], 2, hid_hi, hid_lo)
                    for f in range(4):
                        last = pe.transpose(bank(4 + y % 2)[0:rows, P * f:P * (f + 1)],
                                            h_t[:, 4 * half + f, P * t:P * t + rows], ident[:])
                    last.then_inc(ple_ready, 1)


_INS = ["x_prompt", "x_sample", "cache_conv", "state_delta", "cache_k", "cache_v", "p_prompt", "p_sample", "g_mix",
        "w_in", "conv_w", "a_log", "dt_bias", "g_out_dn", "g_q_sb", "g_k_sb", "w_out", "g_mlp", "w_up", "w_down",
        "g_ple", "w_ple_gate", "w_ple_proj"]


def kernel(**inputs):
    import numpy as _np
    import concourse.bacc as _bacc
    from concourse import mybir as _mybir
    from concourse.bass_utils import run_bass_kernel_spmd as _run

    nc = _bacc.Bacc("TRN2", target_bir_lowering=False, num_devices=1)
    arrays, args = {}, []
    for name in _INS:
        a = _np.ascontiguousarray(inputs[name])
        arrays[f"in_{name}_dram"] = a
        args.append(nc.dram_tensor(f"in_{name}_dram", a.shape, _mybir.dt.from_np(a.dtype), kind="ExternalInput").ap())
    depth, streams, seq = 1, inputs["x_prompt"].shape[0], inputs["x_prompt"].shape[1]
    conv, delta = tuple(inputs["cache_conv"].shape), tuple(inputs["state_delta"].shape)
    heads = tuple(inputs["cache_k"].shape[3:])
    dec = inputs["x_sample"].shape[1]
    outs = [tuple(inputs["x_prompt"].shape), tuple(inputs["x_sample"].shape),
            conv, delta, (depth, streams, seq) + heads, (depth, streams, seq) + heads,
            conv, delta, (depth, streams, dec) + heads, (depth, streams, dec) + heads]
    for i, shape in enumerate(outs):
        args.append(nc.dram_tensor(f"out_{i}_dram", shape, _mybir.dt.float32, kind="ExternalOutput").ap())
    trunk_step(nc, *args)
    r = _run(nc, [arrays], core_ids=[0])
    return tuple(r.results[0][f"out_{i}_dram"] for i in range(len(outs)))
```

```python
from contextlib import ExitStack

import concourse.bass as bass
from concourse import mybir

F32 = mybir.dt.float32
F32R = mybir.dt.float32r
ALU = mybir.AluOpType
ACT = mybir.ActivationFunctionType
AX = mybir.AxisListType

P = 128
EPS = 1e-6


class Chain:

    def __init__(self, eng, sem):
        self.eng, self.sem, self.count, self.offset = eng, sem, 0, 0

    def mark(self, instruction):
        instruction.then_inc(self.sem, 1)
        self.count += 1
        return instruction

    def wait(self):
        self.eng.wait_ge(self.sem, self.count + self.offset)

    def link(self, instruction):
        self.mark(instruction)
        self.wait()

    def enter(self, i, per):
        self.start, self.per, self.offset = self.count, per, i * per

    def leave(self, trips):
        assert self.count - self.start == self.per, (self.count - self.start, self.per)
        self.count = self.start + self.per * trips
        self.offset = 0


def trunk_step(nc, x_prompt, x_sample, cache_conv, state_delta, cache_k, cache_v, p_prompt, p_sample, g_mix,
               w_in, conv_w, a_log, dt_bias, g_out_dn, g_q_sb, g_k_sb, w_out, g_mlp, w_up, w_down, g_ple,
               w_ple_gate, w_ple_proj, y_prompt, y_sample, conv_prompt, delta_prompt, k_prompt, v_prompt,
               conv_sample, delta_sample, k_sample, v_sample):
    D = x_prompt.shape[2]
    TP, TS = x_prompt.shape[1], x_sample.shape[1]
    T = TP + TS
    H, HD = a_log.shape[1], g_out_dn.shape[1]
    W = H * HD
    CD = 3 * W
    PAST = cache_k.shape[2]
    FF = w_up.shape[2]
    PD = p_prompt.shape[3]
    KT = D // P
    NT = TP // P
    CH = T // 3
    WT = W // P
    NC = CD // P
    BLK = 2048
    assert 3 * CH == T and TP % P == 0 and TS == 32 and W == 512 and KT == 8 and HD == 64
    tile_rows = [P] * NT + [TS]
    NTT = len(tile_rows)

    x_rows = [x_prompt[0, P * t:P * (t + 1), :] for t in range(NT)] + [x_sample[0, :, :]]
    p_rows = [p_prompt[0, 0, P * t:P * (t + 1), :] for t in range(NT)] + [p_sample[0, 0, :, :]]
    win = w_in[0].rearrange("(k p) n -> p k n", p=P)
    wout = w_out[0].rearrange("(k p) n -> p k n", p=P)
    wup = w_up[0].rearrange("(k p) n -> p k n", p=P)
    wdown = w_down[0].rearrange("(g k p) n -> g p k n", p=P, k=4)
    wgate = w_ple_gate[0].rearrange("(k p) n -> p k n", p=P)
    wproj = w_ple_proj[0].rearrange("(k p) n -> p k n", p=P)
    k_out = k_prompt[0, 0].rearrange("t h d -> t (h d)")
    v_out = v_prompt[0, 0].rearrange("t h d -> t (h d)")
    ks_out = k_sample[0, 0].rearrange("t h d -> t (h d)")
    vs_out = v_sample[0, 0].rearrange("t h d -> t (h d)")
    kcache = cache_k[0, 0].rearrange("(b p) h d -> p b (h d)", p=P)
    vcache = cache_v[0, 0].rearrange("(b p) h d -> p b (h d)", p=P)
    state_of = {n: a[0, 0].rearrange("(t u) d e -> (u d) t e", u=2)
                for n, a in (("in", state_delta), ("prompt", delta_prompt), ("sample", delta_sample))}
    conv_dram = nc.dram_tensor("conv_scratch", (NC, P, T), F32).ap()
    z_dram = nc.dram_tensor("z_scratch", (T, W), F32).ap()

    with ExitStack() as ctx:
        def sb(name, shape, dt=F32):
            return ctx.enter_context(nc.sbuf_tensor(name, shape, dt))

        def sem(name):
            return ctx.enter_context(nc.semaphore(name))

        act_hi = sb("act_hi", [P, KT, T], F32R)
        act_lo = sb("act_lo", [P, KT, T], F32R)
        w_raw = sb("w_raw", [P, 2, BLK])
        w_hi = sb("w_hi", [P, 2, BLK], F32R)
        w_lo = sb("w_lo", [P, 2, BLK], F32R)
        ident = sb("ident", [P, P])
        ones = sb("ones", [P, P])
        halves = sb("halves", [P, P])
        tri = sb("tri", [P, P])
        tri8 = sb("tri8", [P, P])
        neg_strict = sb("neg_strict", [P, P])
        below = sb("below", [P, P])
        not_below = sb("not_below", [P, P])
        LEVELS = 7
        level = sb("level", [P, LEVELS, P])
        eps = sb("eps", [P, 1])
        below_s = sb("below_s", [P, 2, TS])
        params = sb("params", [P, 100])
        gates = sb("gates", [P, NTT, 2 * H])
        glog = sb("glog", [P, NTT, H])
        beta = sb("beta", [P, NTT, H])
        small = sb("small", [P, 64])
        heads_g = sb("heads_g", [P, 3, HD])
        dn_par = sb("dn_par", [P, 2, H])
        AW = 11776
        area = sb("area", [P, AW])
        with ExitStack() as late:
            hid_hi = late.enter_context(nc.sbuf_tensor("hid_hi", [P, 4, T], F32R))
            hid_lo = late.enter_context(nc.sbuf_tensor("hid_lo", [P, 4, T], F32R))
        area2 = sb("area2", [P, 8 * T])

        psum = ctx.enter_context(nc.psum_tensor("psum", [P, 8, 512], F32))

        def bank(b):
            return psum[:, b, :]

        consts_made = sem("consts_made")
        vecs_loaded = sem("vecs_loaded")
        par_t = sem("par_t")
        par_done = sem("par_done")
        raw_loaded = [sem("raw_loaded0"), sem("raw_loaded1")]
        raw_free = sem("raw_free")
        w_split = sem("w_split")
        ab_loaded = sem("ab_loaded")
        ab_split = sem("ab_split")
        pool_own = sem("pool_own")
        act_own = sem("act_own")
        dve_own = sem("dve_own")
        x_loaded = [sem(f"x_loaded{i}") for i in range(3)]
        x_ms = sem("x_ms")
        x_sd = sem("x_sd")
        x_scaled = sem("x_scaled")
        x_turned = sem("x_turned")
        x_hi = sem("x_hi")
        x_lo = sem("x_lo")
        tok_ready = sem("tok_ready")
        tok_free = sem("tok_free")
        sq_made = sem("sq_made")
        ss_made = sem("ss_made")
        sd_made = sem("sd_made")
        qk_normed = sem("qk_normed")
        qk_turned = sem("qk_turned")
        qk_placed = sem("qk_placed")
        k_stored = [sem("k_stored0"), sem("k_stored1")]
        v_placed = sem("v_placed")
        v_stored = sem("v_stored")
        z_silu = sem("z_silu")
        z_made = sem("z_made")
        z_stored = [sem("z_stored0"), sem("z_stored1")]
        ab_ready = sem("ab_ready")
        ga = sem("ga")
        gd = sem("gd")
        dense_ready = sem("dense_ready")
        dense_free = sem("dense_free")
        added = sem("added")
        relu_free = sem("relu_free")
        xb_ready = sem("xb_ready")
        y_ready = sem("y_ready")
        cs_ready = sem("cs_ready")
        cs_stored = sem("cs_stored")
        tails_made = sem("tails_made")
        tails_t = sem("tails_t")
        tails_c = sem("tails_c")
        tails_stored = sem("tails_stored")

        q_staged = sem("q_staged")
        scores_ready = sem("scores_ready")
        sig_made = sem("sig_made")
        att_made = sem("att_made")
        att_turned = sem("att_turned")
        att_placed = sem("att_placed")
        o_ready = sem("o_ready")
        o_copied = sem("o_copied")
        o_turned = sem("o_turned")
        o_split = sem("o_split")
        s_staged = sem("s_staged")
        kc_loaded = sem("kc_loaded")
        vc_loaded = sem("vc_loaded")
        kc_turned = sem("kc_turned")
        kc_placed = sem("kc_placed")
        s_scores = sem("s_scores")
        s_sig = sem("s_sig")
        s_att = sem("s_att")
        s_turned = sem("s_turned")
        s_placed = sem("s_placed")
        so_ready = sem("so_ready")
        so_copied = sem("so_copied")
        so_turned = sem("so_turned")
        so_split = sem("so_split")

        c_loaded = sem("c_loaded")
        z_loaded = sem("z_loaded")
        gu_made = sem("gu_made")
        gc_ready = sem("gc_ready")
        eg_made = sem("eg_made")
        t0_made = sem("t0_made")
        t1_made = sem("t1_made")
        el_made = sem("el_made")
        dt_made = sem("dt_made")
        sq2_made = sem("sq2_made")
        ss_ready = sem("ss_ready")
        sd2_made = sem("sd2_made")
        cn_made = sem("cn_made")
        kv_turned = sem("kv_turned")
        kv_placed = sem("kv_placed")
        g_ready = sem("g_ready")
        qk_ready = sem("qk_ready")
        dts_made = sem("dts_made")
        dtq_made = sem("dtq_made")
        kd_made = sem("kd_made")
        kg_made = sem("kg_made")
        sdec_made = sem("sdec_made")
        at_made = sem("at_made")
        qt_made = sem("qt_made")
        qg_made = sem("qg_made")
        m_ready = sem("m_ready")
        m_made = sem("m_made")
        t_ready = sem("t_ready")
        x_ready = sem("x_ready")
        t_made = sem("t_made")
        x_made = sem("x_made")
        ks_ready = sem("ks_ready")
        r_made = sem("r_made")
        vn_ready = sem("vn_ready")
        vn_made = sem("vn_made")
        ds_ready = sem("ds_ready")
        s_new = sem("s_new")
        s_stored = sem("s_stored")
        s_loaded = sem("s_loaded")
        o_made = sem("o_made")
        osq_made = sem("osq_made")
        ored_made = sem("ored_made")
        osd_made = sem("osd_made")
        on_made = sem("on_made")
        ot_ready = sem("ot_ready")
        mix_hi = sem("mix_hi")
        mix_split = sem("mix_split")
        xr_loaded = [sem(f"xr_loaded{i}") for i in range(3)]
        xr_turned = sem("xr_turned")
        h_placed = sem("h_placed")
        nsq_made = sem("nsq_made")
        nsum = sem("nsum")
        nsd = sem("nsd")
        ntmp = sem("ntmp")
        nhi = sem("nhi")
        nlo = sem("nlo")
        relu_made = sem("relu_made")
        hid_split = sem("hid_split")
        p_loaded = [sem(f"p_loaded{i}") for i in range(2)]
        p_turned = sem("p_turned")
        p_hi = sem("p_hi")
        p_lo = sem("p_lo")
        ple_ready = sem("ple_ready")
        sg_made = sem("sg_made")
        y_made = sem("y_made")
        y_stored = [sem(f"y_stored{i}") for i in range(2)]

        def carve(base, at, *shape):
            n = 1
            for d in shape:
                n *= d
            flat = base[:, at:at + n]
            if len(shape) == 1:
                return flat
            names = "abcd"[:len(shape)]
            return flat.rearrange(f"p ({' '.join(names)}) -> p {' '.join(names)}",
                                  **dict(zip(names, shape)))

        x_in = carve(area, 0, 3, D)
        x_sc = carve(area, 3 * D, 2, D)
        junk = carve(area, 5 * D, D)
        gmix_b = carve(area, 6 * D, D)
        param_rows = carve(area, 7 * D, P)
        q_t = carve(area2, 0, WT, T)
        k_t = carve(area2, WT * T, WT, T)
        v_tok = carve(area, 0, NTT, W)
        tok0 = NTT * W
        HC = 256
        HH, HT, HALF = HC // HD, HC // P, 2 * NTT
        sq_buf = carve(area, tok0, HC)
        qk_buf = carve(area, tok0 + W, 2, HC)
        z_buf = carve(area, tok0 + 3 * W, 2, HC)
        XB = T + 6
        YB = T + 3
        xb = carve(area, tok0 + 5 * W, 2, XB)
        yb = carve(area, tok0 + 5 * W + 2 * XB, YB)
        cb = carve(area, tok0 + 5 * W + 2 * XB + YB, 1, YB)
        tails = sb("tails", [P, 2, 3, NC])
        sp_x = carve(area, tok0, 2, NTT, H)
        sp_x = (sp_x[:, 0, :, :], sp_x[:, 1, :, :])
        sp_e = carve(area, tok0 + 2 * NTT * H, NTT, H)
        tails_out = carve(area, tok0 + 4 * NTT * H, P)[0:72, :]
        ab_raw = sb("ab_raw", [P, KT, 2 * H])
        ab_hi = sb("ab_hi", [P, KT, 2 * H], F32R)
        ab_lo = sb("ab_lo", [P, KT, 2 * H], F32R)

        SW = PAST + TS
        assert SW == 2 * (TP + TS // 2) and 4 * TS == P
        keep_buf = carve(area, tok0, 2, SW // 2)
        sig_buf = carve(area, tok0 + SW, 2, SW // 2)
        at_buf = carve(area, tok0 + 2 * SW, 2, TP)
        q_stage = carve(area, tok0 + 2 * SW + 2 * TP, 2, P)
        o_buf = carve(area, tok0 + 2 * SW + 2 * TP + 2 * P, 2, P)
        q_s = carve(area, tok0 + 2 * SW + 2 * TP + 4 * P, WT, 2, TS)
        k_s = carve(area, tok0 + 2 * SW + 2 * TP + 6 * P, WT, TS)
        v_s = sb("v_s", [P, W])
        PB = PAST // P
        k_raw = carve(area2, 0, PB, 256)
        kc_t = carve(area2, PB * 256, 2, PAST)
        v_c = carve(area, 0, PB, 256)
        keep_s = carve(area, tok0, SW)
        sig_s = carve(area, tok0 + SW, SW)

        d_c = carve(area, 0, NC, P)
        d_cn = carve(area, 1536, KT, P)
        d_rs = carve(area, 2560, KT, P)
        d_gu = carve(area, 2560, H, P)
        d_z = carve(area, 3584, W)
        d_eg = carve(area, 4096, H, P)
        d_dt = carve(area, 5120, H, P)
        d_m = carve(area, 6144, H, P)
        d_t = carve(area, 7168, H, P)
        d_x = carve(area2, 2048, 2, H, P)
        d_at = carve(area, 8192, 2, H, P)
        d_qt = carve(area2, 0, 2, H, P)
        d_kg = carve(area, 10240, 2, WT, P)
        d_qg = carve(area2, 4096, 2, WT, P)
        d_kd = carve(area2, 5120, 2, W)
        d_v = carve(area2, 6144, 2, W)
        d_r = carve(area, 11264, W)
        d_oq = carve(area, 11264, W)
        d_vn = carve(area2, 7168, W)
        d_on = carve(area2, 7168, W)
        d_s = carve(area2, 7680, WT, HD)
        d_sd = carve(area2, 7936, WT, HD)
        d_gc = carve(area2, 8192, H)
        d_el = carve(area2, 8200, 2, H)
        CHUNKS = NT + 1

        def place_of(h):
            return 4 * (h % 2) + h // 2

        def heads(x, n):
            return x[0:n, :].rearrange("p (k u d) -> p u k d", u=2, d=HD)

        def per_head(x, n, width):
            return x.rearrange("p (u k) -> p u k", u=2).unsqueeze(3).to_broadcast([n, 2, WT, width])

        def value_banks(n):
            return psum[0:n, 6:8, 0:4 * HD].rearrange("p u (k d) -> p u k d", k=WT)

        def head_banks(b, rows, n):
            return psum[0:rows, b:b + 2, :].rearrange("p a (h t) -> p (a h) t", h=4)[:, :, 0:n]

        def levels_of(n):
            return n.bit_length() - 1

        def step_of(c, l, g):
            return 2 * LEVELS * c + 2 * l + g + 1

        def t_step(c, l, g):
            return 2 * (LEVELS - 1) * c + 2 * l + g + 1

        def t_product(c, l, g):
            return 2 * (LEVELS - 2) * c + 2 * (l - 1) + g + 1

        h_t = carve(area, 0, KT, T)
        wide = carve(area, KT * T, 3, T)
        xr_in = carve(area2, 0, 3, D)
        sg_buf = carve(area, KT * T, 2, 512)
        y_buf = carve(area, KT * T + 1024, 2, 512)
        p_in = v_s[:, :].rearrange("p (s n) -> p s n", s=2)
        proj_hi = hid_hi[:, 2:4, :].rearrange("p k t -> p (k t)")[:, 0:BLK]
        proj_lo = hid_lo[:, 2:4, :].rearrange("p k t -> p (k t)")[:, 0:BLK]
        OUT0 = NC
        MLP0 = OUT0 + KT
        PER = 12
        ROUNDS = FF // 512

        whi_cols = w_hi[:, :, :].rearrange("p s (k n) -> p s k n", k=KT)
        wlo_cols = w_lo[:, :, :].rearrange("p s (k n) -> p s k n", k=KT)
        SBCOL = CD + W + 2 * H

        def halves_of(rows):
            return slice(0, rows)

        def token_banks(b, rows):
            return psum[:, b:b + 2, :].rearrange("p a (k t) -> p (a k) t", k=4)[:, :, 0:rows]

        UNITS = 2 * NT

        def earlier(i, j, lag):
            return UNITS * i + max(j - lag + 1, 0)

        block = ctx.enter_context(nc.Block())

        @block.sync
        def _(sp):
            sp.dma_start(gmix_b, g_mix.broadcast_to([P, D])).then_inc(vecs_loaded, 16)
            sp.wait_ge(consts_made, 1)
            sp.dma_start(param_rows[0:8, :], g_mlp[0].rearrange("(a b) -> a b", b=P)).then_inc(vecs_loaded, 16)
            sp.dma_start(param_rows[8:16, :], g_ple[0].rearrange("(a b) -> a b", b=P)).then_inc(vecs_loaded, 16)
            sp.dma_start(param_rows[16:64, :], conv_w[0].rearrange("i (m b) -> (i m) b", b=P)).then_inc(vecs_loaded, 16)
            sp.dma_start(param_rows[64:100, :], cache_conv[0, 0].rearrange("i (m b) -> (i m) b", b=P)).then_inc(vecs_loaded, 16)
            for n, g in enumerate((g_q_sb, g_k_sb, g_out_dn)):
                sp.dma_start(heads_g[:, n, :], g.broadcast_to([P, HD])).then_inc(vecs_loaded, 16)
            sp.dma_start(dn_par[:, 0, :], a_log.broadcast_to([P, H])).then_inc(vecs_loaded, 16)
            sp.dma_start(dn_par[:, 1, :], dt_bias.broadcast_to([P, H])).then_inc(vecs_loaded, 16)
            for t, rows in enumerate(tile_rows):
                if t >= 3:
                    sp.wait_ge(x_scaled, t - 2)
                sp.dma_start(x_in[0:rows, t % 3, :], x_rows[t]).then_inc(x_loaded[t % 3], 16)
                if t == 2:
                    sp.dma_start(ab_raw[:], win[:, :, CD + W:SBCOL]).then_inc(ab_loaded, 16)

            def block_in(n, slot, src):
                sp.wait_ge(raw_free, n + 1)
                dst = w_raw[:, slot, :].rearrange("p (k n) -> p k n", k=src.shape[1])
                sp.dma_start(dst, src).then_inc(raw_loaded[slot], 16)

            with sp.Fori(0, 3) as i:
                for u in range(2):
                    block_in(2 * i + u, u, win[:, :, bass.ds(SBCOL + 512 * i + 256 * u, 256)])
            for u in range(2):
                block_in(6 + u, u, win[:, :, CD + 256 * u:CD + 256 * u + 256])
            with sp.Fori(0, 3) as i:
                for u in range(2):
                    block_in(8 + 2 * i + u, u, win[:, :, bass.ds(512 * i + 256 * u, 256)])
            sp.wait_ge(tails_c, 1)
            sp.wait_ge(tails_c, 1)
            for n, dst in enumerate((conv_prompt, conv_sample)):
                sp.dma_start(dst[0, 0].rearrange("i (m b) -> (i m) b", b=P),
                             tails_out[36 * n:36 * n + 36, :]).then_inc(tails_stored, 16)
            sp.wait_ge(o_split, 1 + WT * NT)
            sp.wait_ge(s_staged, 1)
            for g in range(2):
                if g:
                    sp.wait_ge(kc_turned, 8)
                sp.dma_start(k_raw, kcache[:, :, 256 * g:256 * g + 256]).then_inc(kc_loaded, 16)
                if g:
                    sp.wait_ge(so_ready, 1)
                sp.dma_start(v_c, vcache[:, :, 256 * g:256 * g + 256]).then_inc(vc_loaded, 16)
            sp.wait_ge(so_split, 2)
            sp.wait_ge(cs_stored, 1 + 32 * NC)
            for u in range(2):
                sp.wait_ge(z_stored[u], 16 * NTT)

            def conv_in(c, n):
                cols = bass.ds(P * c, n)
                sp.dma_start(d_c[:, :, 0:n], conv_dram[:, :, cols].rearrange("m p t -> p m t")).then_inc(c_loaded, 16)

            def z_in(c, n):
                sp.dma_start(d_z[0:n, :], z_dram[bass.ds(P * c, n), :]).then_inc(z_loaded, 16)

            conv_in(0, P)
            z_in(0, P)
            sp.wait_ge(kv_turned, 1)
            conv_in(1, P)
            with sp.Fori(1, NT - 1) as c:
                sp.wait_ge(kv_turned, c + 1)
                conv_in(c + 1, P)
                sp.wait_ge(on_made, c)
                z_in(c, P)
            sp.wait_ge(kv_turned, NT)
            conv_in(NT, TS)
            sp.wait_ge(on_made, NT - 1)
            z_in(NT - 1, P)
            sp.wait_ge(s_new, NT + 1)
            sp.dma_start(state_of["prompt"], d_s).then_inc(s_stored, 16)
            sp.wait_ge(s_stored, 16)
            sp.dma_start(d_s, state_of["in"]).then_inc(s_loaded, 16)
            sp.wait_ge(on_made, NT)
            z_in(NT, TS)
            with sp.Fori(0, 2) as i:
                for u in range(2):
                    block_in(14 + 2 * i + u, u, wout[:, :, bass.ds(512 * i + 256 * u, 256)])
            sp.wait_ge(s_new, NT + 2)
            sp.dma_start(state_of["sample"], d_s).then_inc(s_stored, 16)
            sp.wait_ge(mix_split, 1 + CHUNKS)
            for t, rows in enumerate(tile_rows):
                if t >= 3:
                    sp.wait_ge(xr_turned, t - 2)
                sp.dma_start(xr_in[0:rows, t % 3, :], x_rows[t]).then_inc(xr_loaded[t % 3], 16)
            with sp.Fori(0, ROUNDS) as g:
                for u in range(2):
                    block_in(18 + 4 * g + u, u, wup[:, :, bass.ds(512 * g + 256 * u, 256)])
                for u in range(2):
                    src = wdown[bass.ds(g, 1), :, :, 512 * u:512 * (u + 1)].rearrange("g p k n -> (g p) k n")
                    block_in(20 + 4 * g + u, u, src)
            block_in(50, 0, wproj[:, :, :])
            block_in(51, 1, wgate[:, :, 0:256])
            for t, rows in enumerate(tile_rows):
                if t >= 2:
                    sp.wait_ge(p_turned, t - 1)
                sp.dma_start(p_in[0:rows, t % 2, :], p_rows[t]).then_inc(p_loaded[t % 2], 16)
            for b in range(1, 4):
                block_in(51 + b, (1 + b) % 2, wgate[:, :, 256 * b:256 * (b + 1)])
            for y in range(2 * NTT):
                t, rows, c = y % NTT, tile_rows[y % NTT], 512 * (y // NTT)
                sp.wait_ge(y_made, y + 1)
                dst = y_prompt[0, P * t:P * t + rows, c:c + 512] if t < NT else y_sample[0, :, c:c + 512]
                sp.dma_start(dst, y_buf[0:rows, y % 2, :]).then_inc(y_stored[y % 2], 16)
            for u in range(2):
                sp.wait_ge(k_stored[u], 16 * NTT)
                sp.wait_ge(z_stored[u], 16 * NTT)
                sp.wait_ge(y_stored[u], 16 * NTT)
            sp.wait_ge(v_stored, 32)
            sp.wait_ge(cs_stored, 1 + 32 * NC)
            sp.wait_ge(tails_stored, 32)
            sp.wait_ge(s_stored, 32)

        @block.gpsimd
        def _(pool):
            own = Chain(pool, pool_own)
            for started in (q_staged,):
                pool.sem_inc(started, 1)
            pool.memset(param_rows, 0.0).then_inc(consts_made, 1)
            for m, value in ((ident, 0.0), (ones, 1.0), (halves, 1.0), (tri, 1.0), (tri8, HD ** -0.5),
                             (neg_strict, -1.0), (below, 1.0), (not_below, 1.0)):
                own.mark(pool.memset(m[:], value))
            own.mark(pool.memset(eps[:], EPS))
            own.mark(pool.memset(level[:], 1.0))
            own.mark(pool.memset(below_s[:, 0, :], 1.0))
            own.mark(pool.memset(gates[:], 0.0))
            own.wait()

            def keep(m, op, base, pattern, mult, fill=0.0):
                own.mark(pool.affine_select(out=m, in_=m, compare_op=op, fill=fill, base=base,
                                            pattern=pattern, channel_multiplier=mult))

            keep(ident[:], ALU.not_equal, 0, [[-1, P]], 1, 1.0)
            keep(tri[:], ALU.is_ge, 0, [[1, P]], -1)
            keep(tri8[:], ALU.is_ge, 0, [[1, P]], -1)
            keep(neg_strict[:], ALU.is_gt, 0, [[1, P]], -1)
            keep(below[:], ALU.is_gt, 0, [[-1, P]], 1)
            keep(not_below[:], ALU.is_ge, 0, [[1, P]], -1)
            keep(halves[:, 0:HD], ALU.is_gt, HD, [[0, HD]], -1)
            keep(halves[:, HD:P], ALU.is_ge, -HD, [[0, HD]], 1)
            for l in range(LEVELS):
                b = 1 << l
                v = level[:, l, :].rearrange("p (n c) -> p n c", c=2 * b)
                own.wait()
                keep(v, ALU.is_ge, -b, [[-2 * b, P // (2 * b)], [0, 2 * b]], 1)
                own.wait()
                keep(v, ALU.is_gt, 2 * b, [[2 * b, P // (2 * b)], [0, 2 * b]], -1)
                own.wait()
                keep(v, ALU.is_gt, b, [[0, P // (2 * b)], [-1, 2 * b]], 0)
            for j in range(4):
                own.wait()
                rows = below_s[TS * j:TS * (j + 1), 0, :]
                keep(rows, ALU.is_gt, 0, [[-1, TS]], 1)
            own.wait()
            own.mark(pool.tensor_scalar(below_s[:, 1, :], below_s[:, 0, :], -1.0, 1.0, ALU.mult, ALU.add))
            own.wait()
            pool.sem_inc(consts_made, 1)
            pool.sem_inc(raw_free, 2)
            pool.wait_ge(ab_loaded, 16)
            own.link(pool.tensor_copy(ab_hi[:], ab_raw[:]))
            pool.tensor_tensor(ab_lo[:], ab_raw[:], ab_hi[:].bitcast(F32), ALU.subtract).then_inc(ab_split, 1)

            def split(turn, slot, used, count, hi=None, lo=None):
                hi = w_hi[:, slot, :] if hi is None else hi
                lo = w_lo[:, slot, :] if lo is None else lo
                pool.wait_ge(raw_loaded[slot], 16 * turn)
                pool.wait_ge(used, count)
                own.link(pool.tensor_tensor(hi, w_raw[:, slot, :], ones[:, 0:1].to_broadcast([P, BLK]), ALU.mult))
                own.mark(pool.tensor_tensor(lo, w_raw[:, slot, :], hi.bitcast(F32), ALU.subtract))
                own.wait()
                pool.sem_inc(w_split, 1)
                pool.sem_inc(raw_free, 1)

            for u in range(2):
                split(1, u, consts_made, 2)
            with pool.Fori(1, 5) as i:
                own.enter(i - 1, 4)
                for u in range(2):
                    split(i + 1, u, tok_ready, NTT * (2 * i + u - 1))
                own.leave(4)
            with pool.Fori(0, 2) as i:
                own.enter(i, 4)
                for u in range(2):
                    split(i + 6, u, dense_ready, 4 * i + 2 * u + 2)
                own.leave(2)

            pool.wait_ge(tails_c, 1)
            pool.wait_ge(cs_stored, 1 + 32 * NC)
            own.link(pool.memset(q_stage, 0.0))
            own.link(pool.memset(q_s, 0.0))
            own.link(pool.tensor_copy(q_s[0:HD, :, 0, :], q_t[0:HD, :, TP:T]))
            own.link(pool.tensor_copy(q_s[HD:P, :, 1, :], q_t[HD:P, :, TP:T]))
            own.link(pool.tensor_copy(k_s, k_t[:, :, TP:T]))
            own.mark(pool.tensor_copy(v_s[0:TS, :], v_tok[0:TS, NT, :]))
            own.wait()
            pool.sem_inc(s_staged, 1)
            with pool.Fori(0, WT) as i:
                for j in range(UNITS):
                    u, t = j % 2, j // 2
                    pool.wait_ge(scores_ready, 1 + earlier(i, j, 2))
                    pool.wait_ge(q_staged, 1 + UNITS * i + j)
                    rows = slice(HD * u, HD * (u + 1))
                    src = q_t[rows, bass.ds(i, 1), P * t:P * (t + 1)].rearrange("p o t -> p (o t)")
                    pool.tensor_tensor(q_stage[rows, u, :], src, ones[rows, :], ALU.mult).then_inc(q_staged, 1)

            tt = pool.tensor_tensor

            def decays(c, s, n):
                b = beta[0:n, bass.ds(c, 1), :].rearrange("p o h -> p h o").to_broadcast([n, H, n])
                dt, at, qt = (x[0:n, :, 0:n] for x in (d_dt, d_at[:, s], d_qt[:, s]))
                pool.wait_ge(dt_made, c + 1)
                own.link(tt(at, dt, b, ALU.mult))
                tt(at, at, neg_strict[0:n, 0:n].unsqueeze(1).to_broadcast([n, H, n]), ALU.mult).then_inc(dts_made, 1)
                pool.wait_ge(dts_made, c + 1)
                tt(qt, dt, tri8[0:n, 0:n].unsqueeze(1).to_broadcast([n, H, n]), ALU.mult).then_inc(dtq_made, 1)
                pool.wait_ge(dtq_made, c + 1)
                pool.wait_ge(cn_made, c + 1)
                eg = d_eg.rearrange("p (u k) t -> p u k t", u=2)
                own.link(tt(d_kg[0:HD, s, :, 0:n], d_cn[0:HD, WT:KT, 0:n], eg[0:HD, 0, :, 0:n], ALU.mult))
                tt(d_kg[HD:P, s, :, 0:n], d_cn[HD:P, WT:KT, 0:n], eg[HD:P, 1, :, 0:n], ALU.mult).then_inc(kg_made, 1)
                pool.wait_ge(kg_made, c + 1)

            def decay_state(c, s):
                pool.wait_ge(s_new, c + 1)
                if s is None:
                    s = NT % 2
                    pool.wait_ge(s_loaded, 16)
                el = d_el[:, s, :].rearrange("p (u k) -> p u k", u=2).unsqueeze(3)
                own.link(tt(d_sd[0:HD], d_s[0:HD], el[0:HD, 0].to_broadcast([HD, WT, HD]), ALU.mult))
                tt(d_sd[HD:P], d_s[HD:P], el[HD:P, 1].to_broadcast([HD, WT, HD]), ALU.mult).then_inc(sdec_made, 1)
                pool.wait_ge(sdec_made, c + 1)

            decays(0, 0, P)
            decays(1, 1, P)
            with pool.Fori(0, (NT - 2) // 2) as i:
                own.enter(i, 6)
                for u in range(2):
                    decay_state(2 * i + u, u)
                    decays(2 * i + u + 2, u, P)
                own.leave((NT - 2) // 2)
            decay_state(NT - 2, (NT - 2) % 2)
            decays(NT, NT % 2, TS)
            decay_state(NT - 1, (NT - 1) % 2)
            decay_state(NT, None)

            with pool.Fori(0, 2) as i:
                own.enter(i, 4)
                for u in range(2):
                    split(i + 8, u, dense_ready, 4 * i + 2 * u + 10)
                own.leave(2)
            with pool.Fori(0, ROUNDS) as g:
                own.enter(g, 8)
                for b, used in enumerate((-2, 0, 2, 4)):
                    split(2 * g + 10 + b // 2, b % 2, dense_ready, PER * g + MLP0 + used)
                own.leave(ROUNDS)
            split(26, 0, dense_ready, MLP0 + PER * ROUNDS, proj_hi, proj_lo)
            for b in range(2):
                split(26 + b, 1 - b, dense_ready, MLP0 + PER * ROUNDS)
            for b in range(2):
                split(27 + b, 1 - b, ple_ready, NTT)

        @block.scalar
        def _(act):
            own = Chain(act, act_own)
            for started in (sig_made, att_placed, cs_ready, cs_stored):
                act.sem_inc(started, 1)
            act.wait_ge(par_t, 1)
            act.activation(params[:], bank(7)[:, 0:100], ACT.Copy).then_inc(par_done, 1)

            def square_x(t, rows):
                act.wait_ge(x_loaded[t % 3], 16 * (t // 3 + 1))
                own.link(act.activation(junk[0:rows, :], x_in[0:rows, t % 3, :], ACT.Square,
                                        accum_out=small[0:rows, t:t + 1]))
                act.activation(small[0:rows, 16 + t:17 + t], small[0:rows, t:t + 1], ACT.Sqrt, scale=1.0 / D,
                               bias=eps[0:rows, :]).then_inc(x_sd, 1)

            act.wait_ge(consts_made, 2)
            square_x(0, P)
            for t, rows in enumerate(tile_rows):
                if t + 1 < NTT:
                    square_x(t + 1, tile_rows[t + 1])
                act.wait_ge(x_turned, t + 1)
                act.activation(act_hi[:, :, P * t:P * t + rows], token_banks(2 * (t % 2), rows),
                               ACT.Copy).then_inc(x_hi, 1)

            def place(y):
                t, rows = y % NTT, tile_rows[y % NTT]
                part, h = y // HALF, y // NTT % 2
                act.wait_ge(qk_turned, y + 1)
                act.activation((q_t, k_t)[part][:, HT * h:HT * (h + 1), P * t:P * t + rows],
                               bank(2 + y % 2)[:, 0:HC].rearrange("p (k t) -> p k t", k=HT)[:, :, 0:rows],
                               ACT.Copy).then_inc(qk_placed, 1)

            def store(y):
                t, rows = y % NTT, tile_rows[y % NTT]
                if y >= HALF:
                    c = HC * (y // NTT % 2)
                    act.wait_ge(qk_normed, y + 1)
                    act.dma_start(k_out[P * t:P * t + rows, c:c + HC] if t < NT else ks_out[:, c:c + HC],
                                  qk_buf[0:rows, y % 2, :]).then_inc(k_stored[y % 2], 16)

            for y in range(2 * HALF):
                rows = tile_rows[y % NTT]
                act.wait_ge(tok_ready, y + 1)
                if y:
                    act.wait_ge(ss_made, y)
                act.activation(sq_buf[0:rows, :], bank(y % 2)[0:rows, 0:HC], ACT.Square).then_inc(sq_made, 1)
                act.wait_ge(ss_made, y + 1)
                act.activation(small[0:rows, 8:8 + HH], small[0:rows, 0:HH], ACT.Sqrt, scale=1.0 / HD,
                               bias=eps[0:rows, :]).then_inc(sd_made, 1)
                if y:
                    store(y - 1)
                    place(y - 1)
            store(2 * HALF - 1)
            place(2 * HALF - 1)
            for y in range(2 * HALF, 3 * HALF):
                t, rows, c = y % NTT, tile_rows[y % NTT], HC * (y // NTT % 2)
                act.wait_ge(tok_ready, y + 1)
                act.activation(v_tok[0:rows, t, c:c + HC], bank(y % 2)[0:rows, 0:HC], ACT.Copy).then_inc(tok_free, 1)
            act.wait_ge(tok_free, 3 * HALF + 2)
            act.dma_start(v_out.rearrange("(t p) c -> p t c", p=P), v_tok[:, 0:NT, :]).then_inc(v_stored, 16)
            act.dma_start(vs_out, v_tok[0:TS, NT, :]).then_inc(v_stored, 16)
            for n in range(HALF):
                y, t, rows, c = 3 * HALF + n, n % NTT, tile_rows[n % NTT], HC * (n // NTT)
                act.wait_ge(tok_ready, y + 1)
                if n >= 2:
                    act.wait_ge(z_stored[n % 2], 16 * (n // 2))
                act.activation(z_buf[0:rows, n % 2, :], bank(y % 2)[0:rows, 0:HC], ACT.Silu).then_inc(z_silu, 1)
                act.wait_ge(z_made, n + 1)
                act.sem_inc(tok_free, 1)
                act.dma_start(z_dram[P * t:P * t + rows, c:c + HC], z_buf[0:rows, n % 2, :])\
                   .then_inc(z_stored[n % 2], 16)

            act.wait_ge(ab_ready, 1)
            both = bank(6)[:, 0:2 * H * NTT].rearrange("p (t a k u) -> p t a k u", a=2, u=2, k=WT)
            into = gates[:].rearrange("p t (a u k) -> p t a u k", a=2, u=2)
            for a in range(2):
                for u in range(2):
                    own.mark(act.activation(into[:, 0:NT, a, u, :], both[:, 0:NT, a, :, u], ACT.Copy))
                    own.mark(act.activation(into[0:TS, NT, a, u, :], both[0:TS, NT, a, :, u], ACT.Copy))
            own.wait()
            act.activation(beta[:], gates[:, :, H:2 * H], ACT.Sigmoid).then_inc(ga, 1)
            act.wait_ge(gd, 1)
            own.link(act.activation(sp_e, sp_x[1], ACT.Exp))
            act.activation(sp_e, sp_e, ACT.Ln, bias=ones[:, 0:1]).then_inc(ga, 1)
            act.activation(small[:, 56:64].rearrange("p (u k) -> p u k", u=2),
                           dn_par[:, 0, :].rearrange("p (k u) -> p u k", u=2), ACT.Exp).then_inc(ga, 1)

            with act.Fori(0, 3) as i:
                own.enter(i, 8)
                for j in range(4):
                    m = 4 * i + j
                    act.wait_ge(dense_ready, m + 1)
                    own.wait()
                    x3 = xb[:, j % 2, :]
                    pieces = [(0, 0, CH, 3), (1, 0, CH, 3 + CH), (2, 0, TP - 2 * CH, 3 + 2 * CH),
                              (2, TP - 2 * CH, CH, TP + 6)]
                    for b, lo, hi, to in pieces:
                        last = act.activation(x3[:, to:to + hi - lo], bank(3 * (j % 2) + b)[:, lo:hi], ACT.Copy)
                    own.link(last)
                    act.sem_inc(dense_free, 1)
                    hist = params[:, 64:100].rearrange("p (i m) -> p i m", m=NC)
                    act.activation(x3[:, TP + 3:TP + 6].unsqueeze(2), hist[:, :, bass.ds(m, 1)], ACT.Copy).then_inc(xb_ready, 1)
                    act.activation(tails[:, 0, :, bass.ds(m, 1)], x3[:, TP:TP + 3].unsqueeze(2), ACT.Copy)
                    own.mark(act.activation(tails[:, 1, :, bass.ds(m, 1)], x3[:, T + 3:T + 6].unsqueeze(2), ACT.Copy))
                    act.wait_ge(y_ready, m + 1)
                    act.wait_ge(cs_stored, 1 + 32 * m)
                    act.activation(cb[:, 0, :], yb, ACT.Silu).then_inc(cs_ready, 1)
                    act.wait_ge(cs_ready, 1 + m + 1)
                    dst = conv_dram[bass.ds(m, 1), :, :].rearrange("o p t -> p (o t)")
                    act.dma_start(dst[:, 0:TP], cb[:, 0, 0:TP]).then_inc(cs_stored, 16)
                    act.dma_start(dst[:, TP:T], cb[:, 0, TP + 3:T + 3]).then_inc(cs_stored, 16)
                own.leave(3)
            own.wait()
            act.sem_inc(tails_made, 1)
            act.wait_ge(tails_t, 1)
            act.activation(tails_out, bank(7)[0:72, 0:P], ACT.Copy).then_inc(tails_c, 1)

            def sigmoids(i, j):
                u, w = j % 2, P * (j // 2 + 1)
                act.wait_ge(scores_ready, 1 + UNITS * i + j + 1)
                act.wait_ge(att_turned, 1 + earlier(i, j, 2))
                z = psum[:, 2 * u:2 * u + 2, :].rearrange("p b c -> p (b c)")[:, 0:w]
                act.activation(keep_buf[:, u, 0:w], z, ACT.Sigmoid, scale=-(HD ** -0.5))
                act.activation(sig_buf[:, u, 0:w], z, ACT.Sigmoid, scale=HD ** -0.5).then_inc(sig_made, 1)

            def copy_out(i, t):
                act.wait_ge(o_ready, 1 + UNITS * i + 2 * t + 2)
                act.activation(o_buf[:, t % 2, :], bank(6 + t % 2)[:, 0:P], ACT.Copy).then_inc(o_copied, 1)

            act.wait_ge(cs_stored, 1 + 32 * NC)
            act.wait_ge(tails_stored, 32)
            for u in range(2):
                act.wait_ge(k_stored[u], 16 * NTT)
                act.wait_ge(z_stored[u], 16 * NTT)
            def copy_weights(i, j):
                w = P * (j // 2 + 1)
                act.wait_ge(att_turned, 1 + UNITS * i + j + 1)
                act.wait_ge(o_ready, 1 + earlier(i, j, 2))
                act.activation(at_buf[:, j % 2, 0:w], psum[:, 4:6, :].rearrange("p b c -> p (b c)")[:, 0:w],
                               ACT.Copy).then_inc(att_placed, 1)

            with act.Fori(0, WT) as i:
                sigmoids(i, 0)
                sigmoids(i, 1)
                copy_weights(i, 0)
                for j in range(UNITS):
                    if j + 2 < UNITS:
                        sigmoids(i, j + 2)
                    if j + 1 < UNITS:
                        copy_weights(i, j + 1)
                    if j and j % 2 == 0:
                        copy_out(i, j // 2 - 1)
                copy_out(i, NT - 1)

            for g in range(2):
                for n in range(8):
                    act.wait_ge(kc_turned, 8 * g + n + 1)
                    act.activation(kc_t[:, n // 4, 512 * (n % 4):512 * (n % 4 + 1)], bank(4 + n % 2),
                                   ACT.Copy).then_inc(kc_placed, 1)
                act.wait_ge(s_scores, g + 1)
                old = psum[:, 0:4, :].rearrange("p b c -> p (b c)")
                for dst, sign in ((keep_s, -1.0), (sig_s, 1.0)):
                    act.activation(dst[:, 0:PAST], old, ACT.Sigmoid, scale=sign * HD ** -0.5)
                    last = act.activation(dst[:, PAST:SW], bank(6)[:, 0:TS], ACT.Sigmoid, scale=sign * HD ** -0.5)
                last.then_inc(s_sig, 1)
                for n in range(5):
                    act.wait_ge(s_turned, 5 * g + n + 1)
                    rows, w = (P, 512) if n < 4 else (TS, P)
                    act.activation(at_buf[0:rows, n % 2, 0:w], bank(4 + n % 2)[0:rows, 0:w],
                                   ACT.Copy).then_inc(s_placed, 1)
                act.wait_ge(so_ready, g + 1)
                act.activation(o_buf[:, g, 0:HD], bank(7)[:, 0:HD], ACT.Copy).then_inc(so_copied, 1)

            act.wait_ge(so_split, 2)

            def prepare(c, s, n, first=False):
                act.wait_ge(gc_ready, c + 1)
                if not first:
                    act.wait_ge(kg_made, c)
                    act.wait_ge(qg_made, 2 * c)
                act.activation(d_gc[0:n, :], bank(4)[0:n, 0:H], ACT.Copy)
                act.activation(d_eg[:, :, 0:n], head_banks(6, P, n), ACT.Exp).then_inc(eg_made, 1)
                act.wait_ge(c_loaded, 16 * c + 16)
                act.activation(d_rs[:, :, 0:n], d_c[:, 0:KT, 0:n], ACT.Square).then_inc(sq2_made, 1)
                act.wait_ge(eg_made, c + 1)
                act.activation(d_el[:, s, :].unsqueeze(2), d_eg[:, :, n - 1:n], ACT.Copy).then_inc(el_made, 1)
                act.wait_ge(t0_made, c + 1)
                dt = d_dt[0:n, :, 0:n]
                act.activation(dt, dt, ACT.Relu, scale=-1.0).then_inc(t1_made, 1)
                act.wait_ge(t1_made, c + 1)
                act.activation(dt, dt, ACT.Exp, scale=-1.0).then_inc(dt_made, 1)
                act.wait_ge(ss_ready, c + 1)
                act.activation(d_rs[:, :, 0:n], head_banks(4, P, n), ACT.Sqrt, bias=eps[:]).then_inc(sd2_made, 1)
                act.wait_ge(kv_turned, c + 1)
                act.activation(d_v[0:n, s, :], bank(7)[0:n, :], ACT.Copy).then_inc(kv_placed, 1)

            def output(c, n):
                act.wait_ge(o_made, c + 1)
                act.activation(d_oq[0:n, :].rearrange("p (u v) -> p u v", u=2), psum[0:n, 6:8, 0:4 * HD],
                               ACT.Square).then_inc(osq_made, 1)
                act.wait_ge(ored_made, c + 1)
                act.activation(small[0:n, 8:16], small[0:n, 0:8], ACT.Sqrt, scale=1.0 / HD,
                               bias=eps[0:n, :]).then_inc(osd_made, 1)
                act.wait_ge(ot_ready, c + 1)
                src = bank(5).rearrange("p (k t) -> p k t", k=WT)[:, :, 0:n]
                act.activation(act_hi[:, 0:WT, bass.ds(P * c, n)], src, ACT.Copy).then_inc(mix_hi, 1)

            prepare(0, 0, P, True)
            prepare(1, 1, P)
            with act.Fori(0, (NT - 2) // 2) as i:
                for u in range(2):
                    output(2 * i + u, P)
                    prepare(2 * i + u + 2, u, P)
            output(NT - 2, P)
            prepare(NT, NT % 2, TS)
            output(NT - 1, P)
            output(NT, TS)

            act.wait_ge(s_stored, 32)
            for t, rows in enumerate(tile_rows):
                act.wait_ge(xr_turned, t + 1)
                act.activation(h_t[:, :, P * t:P * t + rows], token_banks(2 * (t % 2), rows),
                               ACT.Copy).then_inc(h_placed, 1)

            def norm_squares(n, tiles):
                act.wait_ge(added, tiles + 2)
                for k in range(KT):
                    if k >= 2:
                        act.wait_ge(nsum, KT * n + k - 1)
                    act.activation(wide[:, k % 2, :], h_t[:, k, :], ACT.Square).then_inc(nsq_made, 1)
                act.wait_ge(nsum, KT * (n + 1))
                act.activation(wide[:, 2, :].rearrange("p (c t) -> p c t", c=3), psum[:, 0:3, 0:CH], ACT.Sqrt,
                               scale=1.0 / D, bias=eps[:]).then_inc(nsd, 1)
                for k in range(KT):
                    act.wait_ge(ntmp, KT * n + k + 1)
                    act.activation(act_hi[:, k, :], wide[:, k % 2, :], ACT.Copy).then_inc(nhi, 1)

            norm_squares(0, KT)
            with act.Fori(0, ROUNDS) as g:
                own.enter(g, 4)
                for j in range(4):
                    act.wait_ge(dense_ready, PER * g + MLP0 + j + 1)
                    act.wait_ge(hid_split, 1 + 4 * g + max(j - 1, 0))
                    w = wide[:, j % 2, :]
                    own.link(act.activation(w.rearrange("p (c t) -> p c t", c=3),
                                            psum[:, 3 * (j % 2):3 * (j % 2) + 3, 0:CH], ACT.Relu))
                    act.sem_inc(relu_free, 1)
                    act.activation(w, w, ACT.Square).then_inc(relu_made, 1)
                own.leave(ROUNDS)
            for t, rows in enumerate(tile_rows):
                act.wait_ge(p_turned, t + 1)
                act.activation(hid_hi[:, 0:2, P * t:P * t + rows],
                               bank(6 + t % 2)[:, 0:256].rearrange("p (k t) -> p k t", k=2)[:, :, 0:rows],
                               ACT.Copy).then_inc(p_hi, 1)
            norm_squares(1, KT + KT * ROUNDS)
            act.wait_ge(nlo, 2 * KT)
            for y in range(2 * NTT):
                rows = tile_rows[y % NTT]
                act.wait_ge(ple_ready, y + 1)
                act.activation(sg_buf[0:rows, y % 2, :], bank(y % 2)[0:rows, :], ACT.Sigmoid).then_inc(sg_made, 1)

        @block.vector
        def _(dve):
            own = Chain(dve, dve_own)
            for started in (o_split, mix_split, hid_split):
                dve.sem_inc(started, 1)
            dve.wait_ge(vecs_loaded, 160)

            def scale_x(t, rows):
                dve.wait_ge(x_sd, t + 1)
                own.link(dve.reciprocal(small[0:rows, 32 + t:33 + t], small[0:rows, 16 + t:17 + t]))
                if t >= 2:
                    dve.wait_ge(x_turned, t - 1)
                dve.scalar_tensor_tensor(out=x_sc[0:rows, t % 2, :], in0=x_in[0:rows, t % 3, :],
                                         scalar=small[0:rows, 32 + t:33 + t], in1=gmix_b[0:rows, :],
                                         op0=ALU.mult, op1=ALU.mult).then_inc(x_scaled, 1)

            scale_x(0, P)
            for t, rows in enumerate(tile_rows):
                if t + 1 < NTT:
                    scale_x(t + 1, tile_rows[t + 1])
                dve.wait_ge(x_hi, t + 1)
                cols = slice(P * t, P * t + rows)
                dve.tensor_tensor(act_lo[:, :, cols], token_banks(2 * (t % 2), rows),
                                  act_hi[:, :, cols].bitcast(F32), ALU.subtract).then_inc(x_lo, 1)

            dve.wait_ge(x_sd, NTT)
            for y in range(2 * HALF):
                rows = tile_rows[y % NTT]
                dve.wait_ge(sq_made, y + 1)
                dve.tensor_reduce(small[0:rows, 0:HH], sq_buf[0:rows, :].rearrange("p (h d) -> p h d", h=HH),
                                  AX.X, ALU.add).then_inc(ss_made, 1)
                dve.wait_ge(sd_made, y + 1)
                own.link(dve.reciprocal(small[0:rows, 48:48 + HH], small[0:rows, 8:8 + HH]))
                if y >= 2:
                    dve.wait_ge(qk_turned, y - 1)
                if y >= HALF + 2:
                    dve.wait_ge(k_stored[y % 2], 16 * ((y - HALF) // 2))
                buf = qk_buf[0:rows, y % 2, :].rearrange("p (h d) -> p h d", h=HH)
                own.link(dve.tensor_tensor(buf, bank(y % 2)[0:rows, 0:HC].rearrange("p (h d) -> p h d", h=HH),
                                           small[0:rows, 48:48 + HH].unsqueeze(2).to_broadcast([rows, HH, HD]),
                                           ALU.mult))
                dve.sem_inc(tok_free, 1)
                g = heads_g[0:rows, y // HALF:y // HALF + 1, :].to_broadcast([rows, HH, HD])
                dve.tensor_tensor(buf, buf, g, ALU.mult).then_inc(qk_normed, 1)
            for n in range(HALF):
                rows = tile_rows[n % NTT]
                dve.wait_ge(z_silu, n + 1)
                buf = z_buf[0:rows, n % 2, :].rearrange("p (h d) -> p h d", h=HH)
                dve.tensor_tensor(buf, buf, heads_g[0:rows, 2:3, :].to_broadcast([rows, HH, HD]),
                                  ALU.mult).then_inc(z_made, 1)
            dve.wait_ge(ga, 1)
            al, nal = sp_x
            bias = dn_par[:, 1, :].rearrange("p (k u) -> p u k", u=2).unsqueeze(1).to_broadcast([P, NTT, 2, WT])
            own.link(dve.tensor_tensor(al.rearrange("p t (u k) -> p t u k", u=2),
                                       gates[:, :, 0:H].rearrange("p t (u k) -> p t u k", u=2), bias, ALU.add))
            dve.scalar_tensor_tensor(out=nal, in0=al, scalar=-1.0, in1=al, op0=ALU.mult, op1=ALU.min).then_inc(gd, 1)
            dve.wait_ge(ga, 3)
            own.link(dve.scalar_tensor_tensor(out=al, in0=al, scalar=0.0, in1=sp_e, op0=ALU.max, op1=ALU.add))
            own.link(dve.scalar_tensor_tensor(out=glog[:], in0=al, scalar=-1.0,
                                              in1=small[:, 56:64].unsqueeze(1).to_broadcast([P, NTT, H]),
                                              op0=ALU.mult, op1=ALU.mult))
            own.link(dve.memset(xb[:, :, 0:3], 0.0))
            with dve.Fori(0, 3) as i:
                own.enter(i, 12)
                for j in range(4):
                    m = 4 * i + j
                    dve.wait_ge(xb_ready, m + 1)
                    dve.wait_ge(cs_ready, 1 + m)
                    taps = params[:, 16:64].rearrange("p (i m) -> p i m", m=NC)
                    x3 = xb[:, j % 2, :]
                    for tap in range(4):
                        w = taps[:, tap, bass.ds(m, 1)]
                        if tap == 0:
                            own.link(dve.tensor_scalar(yb, x3[:, 0:YB], w, None, ALU.mult))
                        elif tap < 3:
                            own.link(dve.scalar_tensor_tensor(out=yb, in0=x3[:, tap:tap + YB], scalar=w, in1=yb,
                                                              op0=ALU.mult, op1=ALU.add))
                        else:
                            dve.scalar_tensor_tensor(out=yb, in0=x3[:, tap:tap + YB], scalar=w, in1=yb,
                                                     op0=ALU.mult, op1=ALU.add).then_inc(y_ready, 1)
                own.leave(3)

            def split_out(i, t):
                dve.wait_ge(o_turned, NT * i + t + 1)
                src = bank(6 + t % 2)[:, P:2 * P].unsqueeze(1)
                cols = slice(P * t, P * (t + 1))
                dst = act_hi[:, bass.ds(WT + i, 1), cols]
                own.link(dve.tensor_copy(dst, src))
                own.link(dve.tensor_tensor(act_lo[:, bass.ds(WT + i, 1), cols], src, dst.bitcast(F32),
                                           ALU.subtract))
                dve.sem_inc(o_split, 1)

            with dve.Fori(0, WT) as i:
                own.enter(i, 3 * UNITS + 2 * NT)
                for j in range(UNITS):
                    u, w = j % 2, P * (j // 2 + 1)
                    keep, sig = keep_buf[:, u, :], sig_buf[:, u, :]
                    dve.wait_ge(sig_made, 1 + UNITS * i + j + 1)
                    own.mark(dve.tensor_tensor(sig[:, w - P:w], sig[:, w - P:w], below[:], ALU.mult))
                    own.link(dve.tensor_tensor(keep[:, w - P:w], keep[:, w - P:w], not_below[:], ALU.max))
                    back = keep[:, 0:w][:, ::-1]
                    own.link(dve.tensor_tensor_scan(back, back, back, 1.0, ALU.mult, ALU.min))
                    dve.tensor_tensor(sig[:, 0:w - 1], sig[:, 0:w - 1], keep[:, 1:w], ALU.mult).then_inc(att_made, 1)
                    if j % 2 and j >= 5:
                        split_out(i, (j - 5) // 2)
                split_out(i, NT - 2)
                split_out(i, NT - 1)
                own.leave(WT)

            for g in range(2):
                dve.wait_ge(s_sig, g + 1)
                own.mark(dve.tensor_tensor(sig_s[:, PAST:SW], sig_s[:, PAST:SW], below_s[:, 0, :], ALU.mult))
                own.link(dve.tensor_tensor(keep_s[:, PAST:SW], keep_s[:, PAST:SW], below_s[:, 1, :], ALU.max))
                back = keep_s[:, ::-1]
                own.link(dve.tensor_tensor_scan(back, back, back, 1.0, ALU.mult, ALU.min))
                dve.tensor_tensor(sig_s[:, 0:SW - 1], sig_s[:, 0:SW - 1], keep_s[:, 1:SW],
                                  ALU.mult).then_inc(s_att, 1)
                dve.wait_ge(so_turned, g + 1)
                src = psum[:, 5:7, 64:64 + TS]
                dst = act_hi[:, WT + 2 * g:WT + 2 * g + 2, TP:T]
                own.link(dve.tensor_copy(dst, src))
                dve.tensor_tensor(act_lo[:, WT + 2 * g:WT + 2 * g + 2, TP:T], src, dst.bitcast(F32),
                                  ALU.subtract).then_inc(so_split, 1)

            dve.memset(d_s, 0.0).then_inc(s_new, 1)

            tt = dve.tensor_tensor

            def decay_logs(c, n):
                square = [n, H, n]
                g = glog[0:n, bass.ds(c, 1), :].rearrange("p o h -> p h o").to_broadcast(square)
                tt(d_gu[0:n, :, 0:n], tri[0:n, 0:n].unsqueeze(1).to_broadcast(square), g, ALU.mult).then_inc(gu_made, 1)

            def decay_differences(c, n):
                dve.wait_ge(eg_made, c + 1)
                tt(d_dt[0:n, :, 0:n], head_banks(6, n, n), d_gc[0:n, :].unsqueeze(2).to_broadcast([n, H, n]),
                   ALU.subtract).then_inc(t0_made, 1)

            def unit_norms(c, n):
                dve.wait_ge(sd2_made, c + 1)
                rs = d_rs[:, :, 0:n]
                own.link(dve.reciprocal(rs, rs))
                tt(d_cn[:, :, 0:n], d_c[:, 0:KT, 0:n], rs, ALU.mult).then_inc(cn_made, 1)

            def decayed_queries(c, s, n):
                dve.wait_ge(cn_made, c + 1)
                for u in range(2):
                    rows = slice(HD * u, HD * (u + 1))
                    dve.scalar_tensor_tensor(out=d_qg[rows, s, :, 0:n], in0=d_cn[rows, 0:WT, 0:n], scalar=HD ** -0.5,
                                             in1=d_eg[rows, 4 * u:4 * u + 4, 0:n], op0=ALU.mult,
                                             op1=ALU.mult).then_inc(qg_made, 1)

            def decayed_keys(c, s, n):
                dve.wait_ge(kv_turned, c + 1)
                dve.wait_ge(dt_made, c + 1)
                last = d_dt[0:n, :, n - 1:n].rearrange("p h o -> p (h o)")
                tt(heads(d_kd[:, s], n), heads(bank(6), n), per_head(last, n, HD), ALU.mult).then_inc(kd_made, 1)

            def key_matrix(c, s, n):
                dve.wait_ge(g_ready, c + 1)
                dve.wait_ge(dts_made, c + 1)
                at = d_at[0:n, s, :, 0:n]
                tt(at, head_banks(4, n, n), at, ALU.mult).then_inc(at_made, 1)

            def query_matrix(c, s, n):
                dve.wait_ge(qk_ready, c + 1)
                dve.wait_ge(dtq_made, c + 1)
                qt = d_qt[0:n, s, :, 0:n]
                tt(qt, head_banks(6, n, n), qt, ALU.mult).then_inc(qt_made, 1)

            def rest_of_values(c, s, n):
                dve.wait_ge(ks_ready, c + 1)
                dve.wait_ge(kv_placed, c + 1)
                tt(heads(d_r, n), heads(d_v[:, s], n), value_banks(n), ALU.subtract).then_inc(r_made, 1)

            def new_values(c, n):
                dve.wait_ge(vn_ready, c + 1)
                b = per_head(beta[0:n, bass.ds(c, 1), :].rearrange("p o h -> p (o h)"), n, HD)
                tt(heads(d_vn, n), heads(bank(5), n), b, ALU.mult).then_inc(vn_made, 1)

            def new_state(c):
                dve.wait_ge(ds_ready, c + 1)
                dve.wait_ge(sdec_made, c + 1)
                tt(d_s, bank(5)[:, 0:4 * HD].rearrange("p (k e) -> p k e", k=WT), d_sd, ALU.add).then_inc(s_new, 1)

            def output_squares(c, n):
                dve.wait_ge(osq_made, c + 1)
                dve.tensor_reduce(small[0:n, 0:8], d_oq[0:n, :].rearrange("p (h d) -> p h d", h=H), AX.X,
                                  ALU.add).then_inc(ored_made, 1)

            def normed_output(c, n):
                dve.wait_ge(osd_made, c + 1)
                own.link(dve.reciprocal(small[0:n, 48:56], small[0:n, 8:16]))
                own.link(tt(heads(d_on, n), value_banks(n), per_head(small[0:n, 48:56], n, HD), ALU.mult))
                dve.wait_ge(z_loaded, 16 * c + 16)
                tt(d_on[0:n, :], d_on[0:n, :], d_z[0:n, :], ALU.mult).then_inc(on_made, 1)

            def split_output(c, n):
                dve.wait_ge(mix_hi, c + 1)
                src = bank(5).rearrange("p (k t) -> p k t", k=WT)[:, :, 0:n]
                cols = bass.ds(P * c, n)
                tt(act_lo[:, 0:WT, cols], src, act_hi[:, 0:WT, cols].bitcast(F32), ALU.subtract).then_inc(mix_split, 1)

            def mask(c, l, n):
                for g in range(2):
                    dve.wait_ge(m_ready, step_of(c, l, g))
                    tt(d_m[0:n, 4 * g:4 * g + 4, 0:n], bank(g)[0:n, :].rearrange("p (h t) -> p h t", h=4)[:, :, 0:n],
                       level[0:n, l, 0:n].unsqueeze(1).to_broadcast([n, 4, n]), ALU.mult).then_inc(m_made, 1)

            def renew(c, s, l, n):
                eye = ident[0:n, 0:n].unsqueeze(1).to_broadcast([n, 4, n])
                for g in range(2):
                    hs = slice(4 * g, 4 * g + 4)
                    m, t_, x_ = d_m[0:n, hs, 0:n], d_t[0:n, hs, 0:n], d_x[0:n, s, hs, 0:n]
                    pt, px = (bank(b + g)[0:n, :].rearrange("p (h t) -> p h t", h=4)[:, :, 0:n] for b in (0, 2))
                    if l == 0:
                        dve.wait_ge(m_made, step_of(c, l, g))
                        tt(t_, m, eye, ALU.add).then_inc(t_made, 1)
                    elif l < levels_of(n) - 1:
                        dve.wait_ge(t_ready, t_product(c, l, g))
                        tt(t_, pt, t_, ALU.add).then_inc(t_made, 1)
                    dve.wait_ge(x_ready, step_of(c, l, g))
                    tt(x_, px, eye if l == 0 else x_, ALU.add).then_inc(x_made, 1)

            def inverse(c, s, n, scanned, prepared):
                for l in range(levels_of(n)):
                    mask(c, l, n)
                    if scanned and l == 0:
                        rest_of_values(c - 1, 1 - s, P)
                    if scanned and l == 1:
                        new_values(c - 1, P)
                    if scanned and l == 2:
                        output_squares(c - 1, P)
                    if prepared and l == 4:
                        unit_norms(c + 1, prepared)
                    if prepared and l == 5:
                        decayed_keys(c + 1, 1 - s, prepared)
                    if prepared and l == 6:
                        query_matrix(c + 1, 1 - s, prepared)
                    renew(c, s, l, n)
                    if prepared and l == 0:
                        decay_logs(c + 1, prepared)
                    if scanned and l == 1:
                        new_state(c - 1)
                    if scanned and l == 2:
                        normed_output(c - 1, P)
                    if scanned and l == 3:
                        split_output(c - 1, P)
                    if prepared and l == 3:
                        decay_differences(c + 1, prepared)
                    if prepared and l == 4:
                        decayed_queries(c + 1, 1 - s, prepared)
                    if prepared and l == 5:
                        key_matrix(c + 1, 1 - s, prepared)

            decay_logs(0, P)
            decay_differences(0, P)
            unit_norms(0, P)
            decayed_queries(0, 0, P)
            decayed_keys(0, 0, P)
            key_matrix(0, 0, P)
            query_matrix(0, 0, P)
            inverse(0, 0, P, False, P)
            with dve.Fori(0, (NT - 2) // 2) as i:
                own.enter(i, 6)
                for u in range(2):
                    inverse(2 * i + u + 1, 1 - u, P, True, P)
                own.leave((NT - 2) // 2)
            inverse(NT - 1, (NT - 1) % 2, P, True, TS)
            inverse(NT, NT % 2, TS, True, None)
            rest_of_values(NT, NT % 2, TS)
            new_values(NT, TS)
            new_state(NT)
            output_squares(NT, TS)
            normed_output(NT, TS)
            split_output(NT, TS)

            def add_tile(J, b, k):
                dve.wait_ge(dense_ready, J + 1)
                h3 = h_t[:, k, :].rearrange("p o (c t) -> p (o c) t", c=3)
                dve.tensor_tensor(h3, psum[:, b:b + 3, 0:CH], h3, ALU.add).then_inc(added, 1)

            dve.wait_ge(h_placed, NTT)
            with dve.Fori(0, 2) as i:
                for j in range(4):
                    add_tile(4 * i + j + OUT0, 3 * (j % 2), bass.ds(4 * i + j, 1))

            def norm_scale(n, gain):
                dve.wait_ge(nsd, n + 1)
                own.link(dve.reciprocal(wide[:, 2, :], wide[:, 2, :]))

                def scaled(k):
                    dve.scalar_tensor_tensor(out=wide[:, k % 2, :], in0=h_t[:, k, :],
                                             scalar=params[:, gain + k:gain + k + 1], in1=wide[:, 2, :],
                                             op0=ALU.mult, op1=ALU.mult).then_inc(ntmp, 1)

                scaled(0)
                for k in range(KT):
                    if k + 1 < KT:
                        if k:
                            dve.wait_ge(nlo, KT * n + k)
                        scaled(k + 1)
                    dve.wait_ge(nhi, KT * n + k + 1)
                    dve.tensor_tensor(act_lo[:, k, :], wide[:, k % 2, :], act_hi[:, k, :].bitcast(F32),
                                      ALU.subtract).then_inc(nlo, 1)

            norm_scale(0, 0)
            with dve.Fori(0, ROUNDS) as g:
                own.enter(g, 4)
                for j in range(4):
                    dve.wait_ge(relu_made, 4 * g + j + 1)
                    own.link(dve.tensor_copy(hid_hi[:, j, :], wide[:, j % 2, :]))
                    dve.tensor_tensor(hid_lo[:, j, :], wide[:, j % 2, :], hid_hi[:, j, :].bitcast(F32),
                                      ALU.subtract).then_inc(hid_split, 1)
                for j in range(KT):
                    add_tile(PER * g + MLP0 + 4 + j, 3 * (j % 2), slice(j, j + 1))
                own.leave(ROUNDS)
            for t, rows in enumerate(tile_rows):
                cols = slice(P * t, P * t + rows)
                dve.wait_ge(p_hi, t + 1)
                dve.tensor_tensor(hid_lo[:, 0:2, cols],
                                  bank(6 + t % 2)[:, 0:256].rearrange("p (k t) -> p k t", k=2)[:, :, 0:rows],
                                  hid_hi[:, 0:2, cols].bitcast(F32), ALU.subtract).then_inc(p_lo, 1)
            norm_scale(1, KT)
            for y in range(2 * NTT):
                rows = tile_rows[y % NTT]
                dve.wait_ge(sg_made, y + 1)
                sg = sg_buf[0:rows, y % 2, :]
                own.link(dve.tensor_tensor(sg, bank(2 + y % 2)[0:rows, :], sg, ALU.mult))
                if y >= 2:
                    dve.wait_ge(y_stored[y % 2], 16 * (y // 2))
                dve.tensor_tensor(y_buf[0:rows, y % 2, :], bank(4 + y % 2)[0:rows, :], sg, ALU.add).then_inc(y_made, 1)

        @block.tensor
        def _(pe):
            for started in (scores_ready, att_turned, o_ready):
                pe.sem_inc(started, 1)
            pe.sem_inc(tok_free, 2)
            pe.sem_inc(dense_free, 2)
            pe.sem_inc(added, 2)
            pe.wait_ge(consts_made, 2)
            pe.wait_ge(vecs_loaded, 160)
            pe.transpose(bank(7)[:, 0:100], param_rows[0:100, :], ident[0:100, 0:100]).then_inc(par_t, 1)
            for t, rows in enumerate(tile_rows):
                pe.wait_ge(x_scaled, t + 1)
                if t >= 2:
                    pe.wait_ge(x_lo, t - 1)
                for k in range(KT):
                    last = pe.transpose(bank(2 * (t % 2) + k // 4)[:, P * (k % 4):P * (k % 4) + rows],
                                        x_sc[0:rows, t % 2, P * k:P * k + P], ident[0:rows, 0:rows])
                last.then_inc(x_turned, 1)
            pe.wait_ge(x_lo, NTT)

            def token_product(out, rows, t, w_h, w_l, K=KT, hi=act_hi, lo=act_lo):
                cols = slice(P * t, P * t + rows)
                for k in range(K):
                    pe.matmul(out, hi[:, k, cols], w_h(k), start=(k == 0), stop=False)
                    pe.matmul(out, hi[:, k, cols], w_l(k), start=False, stop=False)
                    last = pe.matmul(out, lo[:, k, cols], w_h(k), start=False, stop=(k == K - 1))
                return last

            def turn_qk(y):
                t, rows = y % NTT, tile_rows[y % NTT]
                pe.wait_ge(qk_normed, y + 1)
                if y >= 2:
                    pe.wait_ge(qk_placed, y - 1)
                for k in range(HT):
                    last = pe.transpose(bank(2 + y % 2)[:, P * k:P * k + rows],
                                        qk_buf[0:rows, y % 2, P * k:P * k + P], ident[0:rows, 0:rows])
                last.then_inc(qk_turned, 1)

            for b in range(8):
                pe.wait_ge(w_split, b + 1)
                for t, rows in enumerate(tile_rows):
                    y = NTT * b + t
                    pe.wait_ge(tok_free, y + 1)
                    token_product(bank(y % 2)[0:rows, 0:HC], rows, t, lambda k: whi_cols[:, b % 2, k, :],
                                  lambda k: wlo_cols[:, b % 2, k, :]).then_inc(tok_ready, 1)
                    if 1 <= y <= 2 * HALF:
                        turn_qk(y - 1)
            pe.wait_ge(ab_split, 1)
            for t, rows in enumerate(tile_rows):
                last = token_product(bank(6)[0:rows, 2 * H * t:2 * H * (t + 1)], rows, t,
                                     lambda k: ab_hi[:, k, :], lambda k: ab_lo[:, k, :])
            last.then_inc(ab_ready, 1)

            def dense(base, lhs_hi, lhs_lo, K=KT, hi=act_hi, lo=act_lo, before=None):
                for k in range(K):
                    if before:
                        before(k)
                    for w, a in ((lhs_hi, hi), (lhs_hi, lo), (lhs_lo, hi)):
                        for c in range(3):
                            last = pe.matmul(bank(base + c)[:, 0:CH], w(k), a[:, k, CH * c:CH * (c + 1)],
                                             start=(k == 0 and w is lhs_hi and a is hi),
                                             stop=(k == K - 1 and w is lhs_lo))
                return last

            pe.wait_ge(tok_free, 4 * HALF + 2)
            pe.wait_ge(qk_placed, 2 * HALF)
            with pe.Fori(0, 3) as i:
                for j in range(4):
                    slot, mm = j // 2, j % 2
                    if mm == 0:
                        pe.wait_ge(w_split, 8 + 2 * i + slot + 1)
                    pe.wait_ge(dense_free, 4 * i + j + 1)
                    last = dense(3 * (j % 2), lambda k: whi_cols[:, slot, k, P * mm:P * mm + P],
                                 lambda k: wlo_cols[:, slot, k, P * mm:P * mm + P])
                    last.then_inc(dense_ready, 1)
            pe.wait_ge(tails_made, 1)
            pe.transpose(bank(7)[0:72, 0:P], tails[:].rearrange("p a i m -> p (a i m)"), ident[:]).then_inc(tails_t, 1)

            def scores(i, j):
                u, w = j % 2, P * (j // 2 + 1)
                pe.wait_ge(q_staged, 1 + UNITS * i + j + 1)
                pe.wait_ge(sig_made, 1 + earlier(i, j, 2))
                for c in range(0, w, 512):
                    n = min(512, w - c)
                    last = pe.matmul(bank(2 * u + c // 512)[:, 0:n], q_stage[:, u, :],
                                     k_t[:, bass.ds(i, 1), c:c + n].rearrange("p o t -> p (o t)"),
                                     start=True, stop=True)
                last.then_inc(scores_ready, 1)

            def turn_out(i, t):
                pe.wait_ge(o_copied, NT * i + t + 1)
                pe.transpose(bank(6 + t % 2)[:, P:2 * P], o_buf[:, t % 2, :], ident[:]).then_inc(o_turned, 1)

            def turn_weights(i, j):
                pe.wait_ge(att_made, UNITS * i + j + 1)
                pe.wait_ge(att_placed, 1 + UNITS * i + j)
                for n in range(j // 2 + 1):
                    last = pe.transpose(bank(4 + n // 4)[:, P * (n % 4):P * (n % 4 + 1)],
                                        sig_buf[:, j % 2, P * n:P * (n + 1)], ident[:])
                last.then_inc(att_turned, 1)

            def values(i, j):
                u, t = j % 2, j // 2
                pe.wait_ge(att_placed, 1 + UNITS * i + j + 1)
                if u == 0:
                    pe.wait_ge(o_split, 1 + NT * i + max(t - 1, 0))
                for n in range(t + 1):
                    v = v_tok[:, n, bass.ds(P * i + HD * u, HD)]
                    last = pe.matmul(bank(6 + t % 2)[:, HD * u:HD * (u + 1)], at_buf[:, u, P * n:P * (n + 1)], v,
                                     start=(n == 0), stop=(n == t))
                last.then_inc(o_ready, 1)

            with pe.Fori(0, WT) as i:
                scores(i, 0)
                scores(i, 1)
                turn_weights(i, 0)
                for j in range(UNITS):
                    if j + 2 < UNITS:
                        scores(i, j + 2)
                    if j + 1 < UNITS:
                        turn_weights(i, j + 1)
                    values(i, j)
                    if j % 2 and j >= 3:
                        turn_out(i, (j - 3) // 2)
                turn_out(i, NT - 1)

            pe.wait_ge(o_split, 1 + WT * NT)
            pe.wait_ge(s_staged, 1)
            for g in range(2):
                pe.wait_ge(kc_loaded, 16 * (g + 1))
                if g:
                    pe.wait_ge(so_split, g)
                for n in range(8):
                    if 8 * g + n >= 2:
                        pe.wait_ge(kc_placed, 8 * g + n - 1)
                    for b in range(4):
                        last = pe.transpose(bank(4 + n % 2)[:, P * b:P * (b + 1)],
                                            k_raw[:, 4 * (n % 4) + b, P * (n // 4):P * (n // 4 + 1)], ident[:])
                    last.then_inc(kc_turned, 1)
                pe.wait_ge(kc_placed, 8 * (g + 1))
                for j in range(4):
                    q = q_s[:, 2 * g + j // 2, j % 2, :]
                    for c in range(PAST // 512):
                        pe.matmul(psum[TS * j:TS * (j + 1), c, :], q, kc_t[:, j // 2, 512 * c:512 * (c + 1)],
                                  start=True, stop=True)
                    last = pe.matmul(psum[TS * j:TS * (j + 1), 6, 0:TS], q, k_s[:, 2 * g + j // 2, :],
                                     start=True, stop=True)
                last.then_inc(s_scores, 1)
                pe.wait_ge(s_att, g + 1)
                pe.wait_ge(vc_loaded, 16 * (g + 1))

                def turn_stacked(n):
                    rows = P if n < 4 else TS
                    if n >= 2:
                        pe.wait_ge(s_placed, 5 * g + n - 1)
                    for b in range(4 if n < 4 else 1):
                        src = sig_s[:, 512 * n + P * b:512 * n + P * b + rows]
                        last = pe.transpose(bank(4 + n % 2)[0:rows, P * b:P * (b + 1)], src, ident[:])
                    last.then_inc(s_turned, 1)

                turn_stacked(0)
                for n in range(5):
                    if n < 4:
                        turn_stacked(n + 1)
                    pe.wait_ge(s_placed, 5 * g + n + 1)
                    for b in range(4 if n < 4 else 1):
                        for j in range(4):
                            rows = P if n < 4 else TS
                            v = v_c[:, 4 * n + b, HD * j:HD * (j + 1)] if n < 4 else \
                                v_s[0:TS, HD * (4 * g + j):HD * (4 * g + j + 1)]
                            last = pe.matmul(bank(7)[TS * j:TS * (j + 1), 0:HD],
                                             at_buf[0:rows, n % 2, P * b + TS * j:P * b + TS * (j + 1)], v,
                                             start=(n == 0 and b == 0), stop=(n == 4))
                last.then_inc(so_ready, 1)
                pe.wait_ge(so_copied, g + 1)
                for j in range(4):
                    rows = slice(TS * j, TS * (j + 1))
                    last = pe.matmul(psum[HD * (j % 2):HD * (j % 2 + 1), 5 + j // 2, 64:64 + TS],
                                     o_buf[rows, g, 0:HD], ident[rows, rows], start=True, stop=True)
                last.then_inc(so_turned, 1)

            pe.wait_ge(so_split, 2)

            def group(b, h, n):
                return bank(b + h % 2)[0:n, P * (h // 2):P * (h // 2) + n]

            def value(h, n):
                return bank(6 + h % 2)[0:n, HD * (h // 2):HD * (h // 2 + 1)]

            def half(h):
                return slice(HD * (h % 2), HD * (h % 2) + HD)

            def decay_sums(c, n, first=False):
                if not first:
                    pe.wait_ge(at_made, c)
                    pe.wait_ge(qt_made, c)
                pe.wait_ge(gu_made, c + 1)
                for g in range(2):
                    pe.matmul(bank(6 + g).rearrange("p (h t) -> p h t", h=4)[:, :, 0:n], ones[0:n, :],
                              d_gu[0:n, 4 * g:4 * g + 4, 0:n], start=True, stop=True)
                pe.matmul(bank(4)[0:n, 0:H], tri[0:n, 0:n], glog[0:n, bass.ds(c, 1), :].rearrange("p o h -> p (o h)"),
                          start=True, stop=True).then_inc(gc_ready, 1)

            def square_sums(c, n, first=False):
                pe.wait_ge(sq2_made, c + 1)
                pe.wait_ge(eg_made, c + 1)
                if not first:
                    pe.wait_ge(mix_split, c)
                for g in range(2):
                    last = pe.matmul(bank(4 + g).rearrange("p (h t) -> p h t", h=4)[:, :, 0:n], halves[:],
                                     d_rs[:, 4 * g:4 * g + 4, 0:n], start=True, stop=True)
                last.then_inc(ss_ready, 1)

            def turn_keys(c, n):
                pe.wait_ge(cn_made, c + 1)
                pe.wait_ge(t0_made, c + 1)
                for k in range(WT):
                    pe.transpose(bank(6)[0:n, P * k:P * (k + 1)], d_cn[:, WT + k, 0:n], ident[:])
                for k in range(WT):
                    last = pe.transpose(bank(7)[0:n, P * k:P * (k + 1)], d_c[:, 2 * WT + k, 0:n], ident[:])
                last.then_inc(kv_turned, 1)

            def with_keys(b, at, n):
                for h in range(H):
                    last = pe.matmul(group(b, h, n), d_cn[half(h), WT + h // 2, 0:n], d_cn[half(h), at + h // 2, 0:n],
                                     start=True, stop=True)
                return last

            def key_products(c, n):
                with_keys(4, WT, n).then_inc(g_ready, 1)

            def query_products(c, n):
                pe.wait_ge(kd_made, c + 1)
                pe.wait_ge(kv_placed, c + 1)
                with_keys(6, 0, n).then_inc(qk_ready, 1)

            def values_of_state(c, s, n):
                pe.wait_ge(kg_made, c + 1)
                pe.wait_ge(s_new, c + 1)
                for h in range(H):
                    last = pe.matmul(value(h, n), d_kg[half(h), s, h // 2, 0:n], d_s[half(h), h // 2, :],
                                     start=True, stop=True)
                last.then_inc(ks_ready, 1)

            def solved_values(c, s, n):
                pe.wait_ge(r_made, c + 1)
                for h in range(H):
                    cols = slice(HD * h, HD * (h + 1))
                    last = pe.matmul(bank(5)[0:n, cols], d_x[0:n, s, place_of(h), 0:n], d_r[0:n, cols],
                                     start=True, stop=True)
                last.then_inc(vn_ready, 1)

            def outputs(c, s, n):
                pe.wait_ge(vn_made, c + 1)
                pe.wait_ge(qg_made, 2 * c + 2)
                for h in range(H):
                    cols = slice(HD * h, HD * (h + 1))
                    pe.matmul(value(h, n), d_qg[half(h), s, h // 2, 0:n], d_s[half(h), h // 2, :],
                              start=True, stop=False)
                    last = pe.matmul(value(h, n), d_qt[0:n, s, place_of(h), 0:n], d_vn[0:n, cols],
                                     start=False, stop=True)
                last.then_inc(o_made, 1)
                for h in range(H):
                    cols = slice(HD * h, HD * (h + 1))
                    last = pe.matmul(bank(5)[half(h), HD * (h // 2):HD * (h // 2 + 1)], d_kd[0:n, s, cols],
                                     d_vn[0:n, cols], start=True, stop=True)
                last.then_inc(ds_ready, 1)

            def turn_outputs(c, n):
                pe.wait_ge(on_made, c + 1)
                for k in range(WT):
                    last = pe.transpose(bank(5)[:, P * k:P * k + n], d_on[0:n, P * k:P * (k + 1)], ident[0:n, 0:n])
                last.then_inc(ot_ready, 1)

            def level_products(c, s, l, n):
                for g in range(2):
                    if l == 0:
                        pe.wait_ge(at_made, c + 1)
                    else:
                        pe.wait_ge(t_made, t_step(c, l - 1, g))
                    for h in range(g, H, 2):
                        if l == 0:
                            last = pe.transpose(group(0, h, n), d_at[0:n, s, place_of(h), 0:n], ident[0:n, 0:n])
                        else:
                            last = pe.matmul(group(0, h, n), d_at[0:n, s, place_of(h), 0:n],
                                             d_t[0:n, place_of(h), 0:n], start=True, stop=True)
                    last.then_inc(m_ready, 1)

            def renewing_products(c, s, l, n):
                for g in range(2):
                    pe.wait_ge(m_made, step_of(c, l, g))
                    if l > 0:
                        pe.wait_ge(x_made, step_of(c, l - 1, g))
                        if l < levels_of(n) - 1:
                            for h in range(g, H, 2):
                                last = pe.matmul(group(0, h, n), d_x[0:n, s, place_of(h), 0:n],
                                                 d_m[0:n, place_of(h), 0:n], start=True, stop=True)
                            last.then_inc(t_ready, 1)
                    for h in range(g, H, 2):
                        m = d_m[0:n, place_of(h), 0:n]
                        if l == 0:
                            last = pe.transpose(group(2, h, n), m, ident[0:n, 0:n])
                        else:
                            last = pe.matmul(group(2, h, n), m, d_x[0:n, s, place_of(h), 0:n], start=True, stop=True)
                    last.then_inc(x_ready, 1)

            def inverse(c, s, n, scanned, prepared):
                for l in range(levels_of(n)):
                    level_products(c, s, l, n)
                    if scanned and l == 0:
                        pe.wait_ge(qt_made, c + 1)
                        values_of_state(c - 1, 1 - s, P)
                    if scanned and l == 1:
                        solved_values(c - 1, 1 - s, P)
                    if prepared and l == 3:
                        decay_sums(c + 1, prepared)
                    if prepared and l == 5:
                        key_products(c + 1, prepared)
                    renewing_products(c, s, l, n)
                    if scanned and l == 1:
                        outputs(c - 1, 1 - s, P)
                    if scanned and l == 2:
                        turn_outputs(c - 1, P)
                    if prepared and l == 3:
                        square_sums(c + 1, prepared)
                    if prepared and l == 4:
                        turn_keys(c + 1, prepared)
                    if prepared and l == 5:
                        query_products(c + 1, prepared)

            decay_sums(0, P, True)
            square_sums(0, P, True)
            turn_keys(0, P)
            key_products(0, P)
            query_products(0, P)
            inverse(0, 0, P, False, P)
            with pe.Fori(0, (NT - 2) // 2) as i:
                for u in range(2):
                    inverse(2 * i + u + 1, 1 - u, P, True, P)
            inverse(NT - 1, (NT - 1) % 2, P, True, TS)
            inverse(NT, NT % 2, TS, True, None)
            pe.wait_ge(s_loaded, 16)
            pe.wait_ge(x_made, step_of(NT, levels_of(TS) - 1, 1))
            values_of_state(NT, NT % 2, TS)
            solved_values(NT, NT % 2, TS)
            outputs(NT, NT % 2, TS)
            turn_outputs(NT, TS)

            pe.wait_ge(mix_split, 1 + CHUNKS)
            for t, rows in enumerate(tile_rows):
                pe.wait_ge(xr_loaded[t % 3], 16 * (t // 3 + 1))
                if t >= 2:
                    pe.wait_ge(h_placed, t - 1)
                for k in range(KT):
                    last = pe.transpose(bank(2 * (t % 2) + k // 4)[:, P * (k % 4):P * (k % 4) + rows],
                                        xr_in[0:rows, t % 3, P * k:P * k + P], ident[0:rows, 0:rows])
                last.then_inc(xr_turned, 1)
            pe.wait_ge(h_placed, NTT)
            with pe.Fori(0, 2) as i:
                for j in range(4):
                    slot, mm = j // 2, j % 2
                    if mm == 0:
                        pe.wait_ge(w_split, 14 + 2 * i + slot + 1)
                    pe.wait_ge(added, 4 * i + j + 1)
                    dense(3 * (j % 2), lambda k: whi_cols[:, slot, k, P * mm:P * mm + P],
                          lambda k: wlo_cols[:, slot, k, P * mm:P * mm + P]).then_inc(dense_ready, 1)

            def norm_sums(n, tiles):
                pe.wait_ge(added, tiles + 2)
                for k in range(KT):
                    pe.wait_ge(nsq_made, KT * n + k + 1)
                    for c in range(3):
                        last = pe.matmul(bank(c)[:, 0:CH], ones[:], wide[:, k % 2, CH * c:CH * (c + 1)],
                                         start=(k == 0), stop=(k == KT - 1))
                    last.then_inc(nsum, 1)

            norm_sums(0, KT)
            pe.wait_ge(nsd, 1)
            whi_down = w_hi[:, :, :].rearrange("p s (k n) -> p s k n", k=4)
            wlo_down = w_lo[:, :, :].rearrange("p s (k n) -> p s k n", k=4)
            with pe.Fori(0, ROUNDS) as g:
                for j in range(PER):
                    if 2 <= j < 6:
                        pe.wait_ge(relu_free, 4 * g + j - 1)
                    else:
                        pe.wait_ge(added, KT * g + KT + (1 + j if j < 2 else j - 3))
                    if j < 4:
                        slot, mm = j // 2, j % 2
                        if mm == 0:
                            pe.wait_ge(w_split, 18 + 4 * g + slot + 1)
                        last = dense(3 * (j % 2), lambda k: whi_cols[:, slot, k, P * mm:P * mm + P],
                                     lambda k: wlo_cols[:, slot, k, P * mm:P * mm + P],
                                     before=(lambda k: pe.wait_ge(nlo, k + 1)) if j == 0 else None)
                    else:
                        slot, mm = (j - 4) // 4, (j - 4) % 4
                        if mm == 0:
                            pe.wait_ge(w_split, 20 + 4 * g + slot + 1)
                        last = dense(3 * (j % 2), lambda k: whi_down[:, slot, k, P * mm:P * mm + P],
                                     lambda k: wlo_down[:, slot, k, P * mm:P * mm + P], 4, hid_hi, hid_lo,
                                     before=(lambda k: pe.wait_ge(hid_split, 1 + 4 * g + k + 1)) if j == 4 else None)
                    last.then_inc(dense_ready, 1)

            for t, rows in enumerate(tile_rows):
                pe.wait_ge(p_loaded[t % 2], 16 * (t // 2 + 1))
                if t >= 2:
                    pe.wait_ge(p_lo, t - 1)
                for k in range(2):
                    last = pe.transpose(bank(6 + t % 2)[:, P * k:P * k + rows], p_in[0:rows, t % 2, P * k:P * k + P],
                                        ident[0:rows, 0:rows])
                last.then_inc(p_turned, 1)
            norm_sums(1, KT + KT * ROUNDS)
            pe.wait_ge(nlo, 2 * KT)
            pe.wait_ge(p_lo, NTT)
            pj_hi = proj_hi.rearrange("p (k n) -> p k n", k=2)
            pj_lo = proj_lo.rearrange("p (k n) -> p k n", k=2)
            for half in range(2):
                pe.wait_ge(w_split, 53 + 2 * half)
                for t, rows in enumerate(tile_rows):
                    y = NTT * half + t
                    if y >= 2:
                        pe.wait_ge(y_made, y - 1)
                    token_product(bank(y % 2)[0:rows, :], rows, t, lambda k: whi_cols[:, ::-1, k, :],
                                  lambda k: wlo_cols[:, ::-1, k, :])
                    token_product(bank(2 + y % 2)[0:rows, :], rows, t, lambda k: pj_hi[:, k, 512 * half:512 * half + 512],
                                  lambda k: pj_lo[:, k, 512 * half:512 * half + 512], 2, hid_hi, hid_lo)
                    for f in range(4):
                        last = pe.transpose(bank(4 + y % 2)[0:rows, P * f:P * (f + 1)],
                                            h_t[:, 4 * half + f, P * t:P * t + rows], ident[:])
                    last.then_inc(ple_ready, 1)


_INS = ["x_prompt", "x_sample", "cache_conv", "state_delta", "cache_k", "cache_v", "p_prompt", "p_sample", "g_mix",
        "w_in", "conv_w", "a_log", "dt_bias", "g_out_dn", "g_q_sb", "g_k_sb", "w_out", "g_mlp", "w_up", "w_down",
        "g_ple", "w_ple_gate", "w_ple_proj"]


def kernel(**inputs):
    import numpy as _np
    import concourse.bacc as _bacc
    from concourse import mybir as _mybir
    from concourse.bass_utils import run_bass_kernel_spmd as _run

    nc = _bacc.Bacc("TRN2", target_bir_lowering=False, num_devices=1)
    arrays, args = {}, []
    for name in _INS:
        a = _np.ascontiguousarray(inputs[name])
        arrays[f"in_{name}_dram"] = a
        args.append(nc.dram_tensor(f"in_{name}_dram", a.shape, _mybir.dt.from_np(a.dtype), kind="ExternalInput").ap())
    depth, streams, seq = 1, inputs["x_prompt"].shape[0], inputs["x_prompt"].shape[1]
    conv, delta = tuple(inputs["cache_conv"].shape), tuple(inputs["state_delta"].shape)
    heads = tuple(inputs["cache_k"].shape[3:])
    dec = inputs["x_sample"].shape[1]
    outs = [tuple(inputs["x_prompt"].shape), tuple(inputs["x_sample"].shape),
            conv, delta, (depth, streams, seq) + heads, (depth, streams, seq) + heads,
            conv, delta, (depth, streams, dec) + heads, (depth, streams, dec) + heads]
    for i, shape in enumerate(outs):
        args.append(nc.dram_tensor(f"out_{i}_dram", shape, _mybir.dt.float32, kind="ExternalOutput").ap())
    trunk_step(nc, *args)
    r = _run(nc, [arrays], core_ids=[0])
    return tuple(r.results[0][f"out_{i}_dram"] for i in range(len(outs)))
```

```python
from contextlib import ExitStack

import concourse.bass as bass
from concourse import mybir

F32 = mybir.dt.float32
F32R = mybir.dt.float32r
ALU = mybir.AluOpType
ACT = mybir.ActivationFunctionType
AX = mybir.AxisListType

P = 128
EPS = 1e-6


class Chain:

    def __init__(self, eng, sem):
        self.eng, self.sem, self.count, self.offset = eng, sem, 0, 0

    def mark(self, instruction):
        instruction.then_inc(self.sem, 1)
        self.count += 1
        return instruction

    def wait(self):
        self.eng.wait_ge(self.sem, self.count + self.offset)

    def link(self, instruction):
        self.mark(instruction)
        self.wait()

    def enter(self, i, per):
        self.start, self.per, self.offset = self.count, per, i * per

    def leave(self, trips):
        assert self.count - self.start == self.per, (self.count - self.start, self.per)
        self.count = self.start + self.per * trips
        self.offset = 0


def trunk_step(nc, x_prompt, x_sample, cache_conv, state_delta, cache_k, cache_v, p_prompt, p_sample, g_mix,
               w_in, conv_w, a_log, dt_bias, g_out_dn, g_q_sb, g_k_sb, w_out, g_mlp, w_up, w_down, g_ple,
               w_ple_gate, w_ple_proj, y_prompt, y_sample, conv_prompt, delta_prompt, k_prompt, v_prompt,
               conv_sample, delta_sample, k_sample, v_sample):
    D = x_prompt.shape[2]
    TP, TS = x_prompt.shape[1], x_sample.shape[1]
    T = TP + TS
    H, HD = a_log.shape[1], g_out_dn.shape[1]
    W = H * HD
    CD = 3 * W
    PAST = cache_k.shape[2]
    FF = w_up.shape[2]
    PD = p_prompt.shape[3]
    KT = D // P
    NT = TP // P
    CH = T // 3
    WT = W // P
    NC = CD // P
    BLK = 2048
    assert 3 * CH == T and TP % P == 0 and TS == 32 and W == 512 and KT == 8 and HD == 64
    tile_rows = [P] * NT + [TS]
    NTT = len(tile_rows)

    x_rows = [x_prompt[0, P * t:P * (t + 1), :] for t in range(NT)] + [x_sample[0, :, :]]
    p_rows = [p_prompt[0, 0, P * t:P * (t + 1), :] for t in range(NT)] + [p_sample[0, 0, :, :]]
    win = w_in[0].rearrange("(k p) n -> p k n", p=P)
    wout = w_out[0].rearrange("(k p) n -> p k n", p=P)
    wup = w_up[0].rearrange("(k p) n -> p k n", p=P)
    wdown = w_down[0].rearrange("(g k p) n -> g p k n", p=P, k=4)
    wgate = w_ple_gate[0].rearrange("(k p) n -> p k n", p=P)
    wproj = w_ple_proj[0].rearrange("(k p) n -> p k n", p=P)
    k_out = k_prompt[0, 0].rearrange("t h d -> t (h d)")
    v_out = v_prompt[0, 0].rearrange("t h d -> t (h d)")
    ks_out = k_sample[0, 0].rearrange("t h d -> t (h d)")
    vs_out = v_sample[0, 0].rearrange("t h d -> t (h d)")
    kcache = cache_k[0, 0].rearrange("(b p) h d -> p b (h d)", p=P)
    vcache = cache_v[0, 0].rearrange("(b p) h d -> p b (h d)", p=P)
    state_of = {n: a[0, 0].rearrange("(t u) d e -> (u d) t e", u=2)
                for n, a in (("in", state_delta), ("prompt", delta_prompt), ("sample", delta_sample))}
    conv_dram = nc.dram_tensor("conv_scratch", (NC, P, T), F32).ap()
    z_dram = nc.dram_tensor("z_scratch", (T, W), F32).ap()

    with ExitStack() as ctx:
        def sb(name, shape, dt=F32):
            return ctx.enter_context(nc.sbuf_tensor(name, shape, dt))

        def sem(name):
            return ctx.enter_context(nc.semaphore(name))

        act_hi = sb("act_hi", [P, KT, T], F32R)
        act_lo = sb("act_lo", [P, KT, T], F32R)
        w_raw = sb("w_raw", [P, 2, BLK])
        w_hi = sb("w_hi", [P, 2, BLK], F32R)
        w_lo = sb("w_lo", [P, 2, BLK], F32R)
        ident = sb("ident", [P, P])
        ones = sb("ones", [P, P])
        halves = sb("halves", [P, P])
        tri = sb("tri", [P, P])
        tri8 = sb("tri8", [P, P])
        neg_strict = sb("neg_strict", [P, P])
        below = sb("below", [P, P])
        not_below = sb("not_below", [P, P])
        LEVELS = 7
        level = sb("level", [P, LEVELS - 1, P])
        eps = sb("eps", [P, 1])
        below_s = sb("below_s", [P, 2, TS])
        params = sb("params", [P, 100])
        gates = sb("gates", [P, NTT, 2 * H])
        glog = sb("glog", [P, NTT, H])
        beta = sb("beta", [P, NTT, H])
        small = sb("small", [P, 64])
        heads_g = sb("heads_g", [P, 3, HD])
        dn_par = sb("dn_par", [P, 2, H])
        AW = 11776
        area = sb("area", [P, AW])
        with ExitStack() as late:
            hid_hi = late.enter_context(nc.sbuf_tensor("hid_hi", [P, 4, T], F32R))
            hid_lo = late.enter_context(nc.sbuf_tensor("hid_lo", [P, 4, T], F32R))
        area2 = sb("area2", [P, 8 * T])

        psum = ctx.enter_context(nc.psum_tensor("psum", [P, 8, 512], F32))

        def bank(b):
            return psum[:, b, :]

        consts_made = sem("consts_made")
        ident_made = sem("ident_made")
        vecs_loaded = sem("vecs_loaded")
        par_t = sem("par_t")
        raw_loaded = [sem("raw_loaded0"), sem("raw_loaded1")]
        raw_free = sem("raw_free")
        w_split = sem("w_split")
        ab_loaded = sem("ab_loaded")
        ab_split = sem("ab_split")
        pool_own = sem("pool_own")
        act_own = sem("act_own")
        dve_own = sem("dve_own")
        x_loaded = [sem(f"x_loaded{i}") for i in range(3)]
        x_sd = sem("x_sd")
        x_scaled = sem("x_scaled")
        x_turned = sem("x_turned")
        x_hi = sem("x_hi")
        x_lo = sem("x_lo")
        tok_ready = sem("tok_ready")
        tok_free = sem("tok_free")
        sq_made = sem("sq_made")
        ss_made = sem("ss_made")
        sd_made = sem("sd_made")
        qk_normed = sem("qk_normed")
        qk_turned = sem("qk_turned")
        qk_placed = sem("qk_placed")
        k_stored = [sem("k_stored0"), sem("k_stored1")]
        v_stored = sem("v_stored")
        z_silu = sem("z_silu")
        z_made = sem("z_made")
        z_stored = [sem("z_stored0"), sem("z_stored1")]
        ab_ready = sem("ab_ready")
        ab_copied = sem("ab_copied")
        ab_turned = sem("ab_turned")
        gates_act_done = sem("gates_act_done")
        gates_dve_done = sem("gates_dve_done")
        dense_ready = sem("dense_ready")
        dense_free = sem("dense_free")
        added = sem("added")
        relu_free = sem("relu_free")
        xb_ready = sem("xb_ready")
        y_ready = sem("y_ready")
        cs_ready = sem("cs_ready")
        cs_stored = sem("cs_stored")
        tails_made = sem("tails_made")
        tails_t = sem("tails_t")
        tails_c = sem("tails_c")
        tails_stored = sem("tails_stored")

        q_staged = sem("q_staged")
        scores_ready = sem("scores_ready")
        sig_made = sem("sig_made")
        att_made = sem("att_made")
        att_turned = sem("att_turned")
        att_placed = sem("att_placed")
        o_ready = sem("o_ready")
        o_copied = sem("o_copied")
        o_turned = sem("o_turned")
        o_split = sem("o_split")
        s_staged = sem("s_staged")
        kc_loaded = sem("kc_loaded")
        vc_loaded = sem("vc_loaded")
        kc_turned = sem("kc_turned")
        kc_placed = sem("kc_placed")
        s_scores = sem("s_scores")
        s_sig = sem("s_sig")
        s_att = sem("s_att")
        s_turned = sem("s_turned")
        s_placed = sem("s_placed")
        so_ready = sem("so_ready")
        so_copied = sem("so_copied")
        so_turned = sem("so_turned")
        so_split = sem("so_split")

        c_loaded = sem("c_loaded")
        z_loaded = sem("z_loaded")
        gu_made = sem("gu_made")
        gc_ready = sem("gc_ready")
        eg_made = sem("eg_made")
        t0_made = sem("t0_made")
        t1_made = sem("t1_made")
        x0_made = sem("x0_made")
        last_m_made = sem("last_m_made")
        last_x_made = sem("last_x_made")
        t0_ready = sem("t0_ready")
        dt_made = sem("dt_made")
        sq2_made = sem("sq2_made")
        ss_ready = sem("ss_ready")
        ln_made = sem("ln_made")
        sd2_made = sem("sd2_made")
        kz_made = sem("kz_made")
        cn_made = sem("cn_made")
        kv_turned = sem("kv_turned")
        kv_placed = sem("kv_placed")
        g_ready = sem("g_ready")
        qk_ready = sem("qk_ready")
        dts_made = sem("dts_made")
        dtq_made = sem("dtq_made")
        kd_made = sem("kd_made")
        kg_made = sem("kg_made")
        sdec_made = sem("sdec_made")
        at_made = sem("at_made")
        qt_made = sem("qt_made")
        qg_made = sem("qg_made")
        m_ready = sem("m_ready")
        m_made = sem("m_made")
        t_ready = sem("t_ready")
        x_ready = sem("x_ready")
        t_made = sem("t_made")
        x_made = sem("x_made")
        ks_ready = sem("ks_ready")
        r_made = sem("r_made")
        vn_ready = sem("vn_ready")
        vn_made = sem("vn_made")
        ds_ready = sem("ds_ready")
        s_new = sem("s_new")
        s_stored = sem("s_stored")
        s_loaded = sem("s_loaded")
        o_made = sem("o_made")
        osq_made = sem("osq_made")
        ored_made = sem("ored_made")
        osd_made = sem("osd_made")
        on_made = sem("on_made")
        ot_ready = sem("ot_ready")
        mix_hi = sem("mix_hi")
        mix_split = sem("mix_split")
        xr_loaded = [sem(f"xr_loaded{i}") for i in range(4)]
        xr_turned = sem("xr_turned")
        h_placed = sem("h_placed")
        nsq_made = sem("nsq_made")
        nsum = sem("nsum")
        nln = sem("nln")
        acc_made = sem("acc_made")
        gate_hi = sem("gate_hi")
        gate_split = sem("gate_split")
        nsd = sem("nsd")
        ntmp = sem("ntmp")
        nhi = sem("nhi")
        nlo = sem("nlo")
        relu_made = sem("relu_made")
        hid_split = sem("hid_split")
        p_loaded = [sem(f"p_loaded{i}") for i in range(2)]
        p_turned = sem("p_turned")
        p_hi = sem("p_hi")
        p_lo = sem("p_lo")
        ple_ready = sem("ple_ready")
        sg_made = sem("sg_made")
        y_made = sem("y_made")
        y_stored = [sem(f"y_stored{i}") for i in range(2)]

        def carve(base, at, *shape):
            n = 1
            for d in shape:
                n *= d
            flat = base[:, at:at + n]
            if len(shape) == 1:
                return flat
            names = "abcd"[:len(shape)]
            return flat.rearrange(f"p ({' '.join(names)}) -> p {' '.join(names)}",
                                  **dict(zip(names, shape)))

        x_in = carve(area, 0, 3, D)
        x_sc = carve(area, 3 * D, 2, D)
        junk = carve(area, 5 * D, D)
        gmix_b = carve(area, 6 * D, D)
        param_rows = carve(area, 7 * D, P)
        q_t = carve(area2, 0, WT, T)
        k_t = carve(area2, WT * T, WT, T)
        v_tok = carve(area, 0, NTT, W)
        tok0 = NTT * W
        HC = 256
        HH, HT, HALF = HC // HD, HC // P, 2 * NTT
        sq_buf = carve(area, tok0, HC)
        qk_buf = carve(area, tok0 + W, 2, HC)
        z_buf = carve(area, tok0 + 3 * W, 2, HC)
        XB = T + 6
        YB = T + 3
        xb = carve(area, tok0 + 5 * W, 2, XB)
        yb = carve(area, tok0 + 5 * W + 2 * XB, YB)
        cb = carve(area, tok0 + 5 * W + 2 * XB + YB, YB)
        ab_flat = carve(area, tok0 + 5 * W + 2 * XB, T)[0:2 * H, :]
        ab_t = ab_flat.rearrange("p (c t) -> p c t", c=3)
        tails = sb("tails", [P, 2, 3, NC])
        sp_x = carve(area, tok0, 2, NTT, H)
        sp_x = (sp_x[:, 0, :, :], sp_x[:, 1, :, :])
        sp_e = carve(area, tok0 + 2 * NTT * H, NTT, H)
        tails_out = carve(area, tok0 + 4 * NTT * H, P)[0:72, :]
        ab_raw = sb("ab_raw", [P, KT, 2 * H])
        ab_hi = sb("ab_hi", [P, KT, 2 * H], F32R)
        ab_lo = sb("ab_lo", [P, KT, 2 * H], F32R)

        SW = PAST + TS
        assert SW == 2 * (TP + TS // 2) and 4 * TS == P
        keep_buf = carve(area, tok0, 2, SW // 2)
        sig_buf = carve(area, tok0 + SW, 2, SW // 2)
        at_buf = carve(area, tok0 + 2 * SW, 2, TP)
        q_stage = carve(area, tok0 + 2 * SW + 2 * TP + 5 * P, 2, P)
        o_buf = carve(area, tok0 + 2 * SW + 2 * TP, 2, P)
        q_s = carve(area, tok0 + 2 * SW + 2 * TP + 2 * P, WT, 2, TS)
        k_s = carve(area, tok0 + 2 * SW + 2 * TP + 4 * P, WT, TS)
        v_s = sb("v_s", [P, W])
        PB = PAST // P
        k_raw = w_raw[:, :, :].rearrange("p s (b c) -> p (s b) c", c=256)
        kc_t = carve(area2, 0, 2, 2, PAST)
        v_c = carve(area, 0, PB, 256)
        keep_s = carve(area, tok0, SW)
        sig_s = carve(area, tok0 + SW, SW)

        d_c = carve(area, 0, NC, P)
        d_cn = carve(area, 1536, KT, P)
        d_rs = carve(area, 2560, KT, P)
        d_gu = carve(area, 2560, H, P)
        d_kz = carve(area, 2560, 2, WT, P)
        d_z = carve(area, 3584, W)
        d_eg = carve(area, 4096, H, P)
        d_dt = carve(area, 5120, H, P)
        d_m = carve(area, 6144, H, P)
        d_t = carve(area, 7168, H, P)
        d_x = carve(area2, 2048, 2, H, P)
        d_at = carve(area, 9216, 2, H, P)
        d_qt = carve(area2, 0, 2, H, P)
        d_kg = carve(area, 8192, 2, WT, P)
        d_qg = carve(area2, 4096, 2, WT, P)
        d_kd = carve(area2, 5120, 2, W)
        d_v = carve(area2, 6144, 2, W)
        d_r = carve(area, 11264, W)
        d_oq = carve(area, 11264, W)
        d_vn = carve(area2, 7168, W)
        d_on = carve(area2, 7168, W)
        d_s = carve(area2, 7680, WT, HD)
        d_sd = carve(area2, 7936, WT, HD)
        d_gc = carve(area2, 8192, H)
        d_el = carve(area2, 8200, 2, H)
        CHUNKS = NT + 1

        def place_of(h):
            return 4 * (h % 2) + h // 2

        def heads(x, n):
            return x[0:n, :].rearrange("p (k u d) -> p u k d", u=2, d=HD)

        def per_head(x, n, width):
            return x.rearrange("p (u k) -> p u k", u=2).unsqueeze(3).to_broadcast([n, 2, WT, width])

        def value_banks(n):
            return psum[0:n, 6:8, 0:4 * HD].rearrange("p u (k d) -> p u k d", k=WT)

        def head_banks(b, rows, n):
            return psum[0:rows, b:b + 2, :].rearrange("p a (h t) -> p (a h) t", h=4)[:, :, 0:n]

        def levels_of(n):
            return n.bit_length() - 1

        def step_of(c, l, g):
            return 2 * (LEVELS - 1) * c + 2 * (l - 1) + g + 1

        def t_step(c, l, g):
            return 2 * (LEVELS - 1) * c + 2 * l + g + 1

        def inner_step(c, l, g):
            return 2 * (LEVELS - 2) * c + 2 * (l - 1) + g + 1

        h_t = carve(area, 0, KT, T)
        wide = carve(area, KT * T, 3, T)
        assert NT % 2 == 0
        xr_in = [carve(area, 9216, D), carve(area, 10240, D), carve(area2, 1024, D), carve(area2, 3072, D)]
        sg_buf = carve(area, KT * T, 2, 512)
        y_buf = carve(area, KT * T + 1024, 2, 512)
        p_in = v_s[:, :].rearrange("p (s n) -> p s n", s=2)
        proj_hi = hid_hi[:, 2:4, :].rearrange("p k t -> p (k t)")[:, 0:BLK]
        proj_lo = hid_lo[:, 2:4, :].rearrange("p k t -> p (k t)")[:, 0:BLK]
        OUT0 = NC
        MLP0 = OUT0 + KT
        PER = 12
        ROUNDS = FF // 512

        whi_cols = w_hi[:, :, :].rearrange("p s (k n) -> p s k n", k=KT)
        wlo_cols = w_lo[:, :, :].rearrange("p s (k n) -> p s k n", k=KT)
        SBCOL = CD + W + 2 * H

        def token_banks(b, rows):
            return psum[:, b:b + 2, :].rearrange("p a (k t) -> p (a k) t", k=4)[:, :, 0:rows]

        UNITS = 2 * NT

        def earlier(i, j, lag):
            return UNITS * i + max(j - lag + 1, 0)

        block = ctx.enter_context(nc.Block())

        @block.sync
        def _(sp):
            sp.dma_start(x_in[:, 0, :], x_rows[0]).then_inc(x_loaded[0], 16)
            sp.dma_start(gmix_b, g_mix.broadcast_to([P, D])).then_inc(vecs_loaded, 16)
            sp.wait_ge(consts_made, 1)
            sp.dma_start(param_rows[0:8, :], g_mlp[0].rearrange("(a b) -> a b", b=P)).then_inc(vecs_loaded, 16)
            sp.dma_start(param_rows[8:16, :], g_ple[0].rearrange("(a b) -> a b", b=P)).then_inc(vecs_loaded, 16)
            sp.dma_start(param_rows[16:64, :], conv_w[0].rearrange("i (m b) -> (i m) b", b=P)).then_inc(vecs_loaded, 16)
            sp.dma_start(param_rows[64:100, :], cache_conv[0, 0].rearrange("i (m b) -> (i m) b", b=P)).then_inc(vecs_loaded, 16)
            for n, g in enumerate((g_q_sb, g_k_sb, g_out_dn)):
                sp.dma_start(heads_g[:, n, :], g.broadcast_to([P, HD])).then_inc(vecs_loaded, 16)
            sp.dma_start(dn_par[:, 0, :], a_log.broadcast_to([P, H])).then_inc(vecs_loaded, 16)
            sp.dma_start(dn_par[:, 1, :], dt_bias.broadcast_to([P, H])).then_inc(vecs_loaded, 16)
            for t, rows in enumerate(tile_rows):
                if t >= 3:
                    sp.wait_ge(x_scaled, t - 2)
                if t:
                    sp.dma_start(x_in[0:rows, t % 3, :], x_rows[t]).then_inc(x_loaded[t % 3], 16)
                if t == 2:
                    sp.dma_start(ab_raw[:], win[:, :, CD + W:SBCOL]).then_inc(ab_loaded, 16)

            def block_in(n, slot, src, before=None):
                if before:
                    sp.wait_ge(*before)
                else:
                    sp.wait_ge(raw_free, n + 1)
                dst = w_raw[:, slot, :].rearrange("p (k n) -> p k n", k=src.shape[1])
                sp.dma_start(dst, src).then_inc(raw_loaded[slot], 16)

            with sp.Fori(0, 3) as i:
                for u in range(2):
                    block_in(2 * i + u, u, win[:, :, bass.ds(SBCOL + 512 * i + 256 * u, 256)])
            for u in range(2):
                block_in(6 + u, u, win[:, :, CD + 256 * u:CD + 256 * u + 256])
            with sp.Fori(0, 3) as i:
                for u in range(2):
                    block_in(8 + 2 * i + u, u, win[:, :, bass.ds(512 * i + 256 * u, 256)])
            sp.wait_ge(tails_c, 1)
            for n, dst in enumerate((conv_prompt, conv_sample)):
                sp.dma_start(dst[0, 0].rearrange("i (m b) -> (i m) b", b=P),
                             tails_out[36 * n:36 * n + 36, :]).then_inc(tails_stored, 16)
            sp.wait_ge(raw_free, 14 + 2)
            for g in range(2):
                if g:
                    sp.wait_ge(kc_turned, 8)
                sp.dma_start(k_raw, kcache[:, :, 256 * g:256 * g + 256]).then_inc(kc_loaded, 16)
                if g:
                    sp.wait_ge(so_ready, 1)
                else:
                    sp.wait_ge(o_split, 1 + WT * NT)
                    sp.wait_ge(s_staged, 4)
                sp.dma_start(v_c, vcache[:, :, 256 * g:256 * g + 256]).then_inc(vc_loaded, 16)
            sp.wait_ge(kc_turned, 16)
            for u in range(2):
                block_in(14 + u, u, wout[:, :, 256 * u:256 * u + 256])
            sp.wait_ge(so_split, 2)
            sp.wait_ge(cs_stored, 1 + 32 * NC)
            for u in range(2):
                sp.wait_ge(z_stored[u], 16 * NTT)

            def conv_in(c, n):
                cols = bass.ds(P * c, n)
                sp.dma_start(d_c[:, :, 0:n], conv_dram[:, :, cols].rearrange("m p t -> p m t")).then_inc(c_loaded, 16)

            def z_in(c, n):
                sp.dma_start(d_z[0:n, :], z_dram[bass.ds(P * c, n), :]).then_inc(z_loaded, 16)

            conv_in(0, P)
            z_in(0, P)
            sp.wait_ge(kv_turned, 1)
            conv_in(1, P)
            for u in range(2):
                block_in(16 + u, u, wout[:, :, 512 + 256 * u:768 + 256 * u])
            with sp.Fori(1, NT - 1) as c:
                sp.wait_ge(kv_turned, c + 1)
                conv_in(c + 1, P)
                sp.wait_ge(on_made, c)
                z_in(c, P)
            sp.wait_ge(kv_turned, NT)
            conv_in(NT, TS)
            sp.wait_ge(on_made, NT - 1)
            z_in(NT - 1, P)
            sp.wait_ge(s_new, NT + 1)
            sp.dma_start(state_of["prompt"], d_s).then_inc(s_stored, 16)
            sp.wait_ge(s_stored, 16)
            sp.dma_start(d_s, state_of["in"]).then_inc(s_loaded, 16)
            sp.wait_ge(on_made, NT)
            z_in(NT, TS)
            sp.wait_ge(x_ready, step_of(NT, levels_of(TS) - 1, 1))
            for t, rows in enumerate(tile_rows):
                if t >= 4:
                    sp.wait_ge(xr_turned, t - 3)
                sp.dma_start(xr_in[t % 4][0:rows, :], x_rows[t]).then_inc(xr_loaded[t % 4], 16)
                if t == 3:
                    sp.wait_ge(s_new, NT + 2)
                    sp.dma_start(state_of["sample"], d_s).then_inc(s_stored, 16)
            with sp.Fori(0, ROUNDS) as g:
                for u in range(2):
                    block_in(18 + 4 * g + u, u, wup[:, :, bass.ds(512 * g + 256 * u, 256)])
                for u in range(2):
                    src = wdown[bass.ds(g, 1), :, :, 512 * u:512 * (u + 1)].rearrange("g p k n -> (g p) k n")
                    block_in(20 + 4 * g + u, u, src)
            block_in(50, 0, wgate[:, :, 0:256])
            block_in(51, 1, wgate[:, :, 256:512])
            block_in(52, 0, wproj[:, :, :])

            def embedding_in(t):
                if t >= 2:
                    sp.wait_ge(p_turned, t - 1)
                sp.dma_start(p_in[0:tile_rows[t], t % 2, :], p_rows[t]).then_inc(p_loaded[t % 2], 16)

            for t in range(4):
                embedding_in(t)
            block_in(53, 1, wgate[:, :, 768:1024], before=(gate_split, 1))
            block_in(54, 0, wgate[:, :, 512:768], before=(raw_free, 54))
            for y in range(2 * NTT):
                t, rows, c = y % NTT, tile_rows[y % NTT], 512 * (y // NTT)
                if y + 4 < NTT:
                    embedding_in(y + 4)
                sp.wait_ge(y_made, y + 1)
                dst = y_prompt[0, P * t:P * t + rows, c:c + 512] if t < NT else y_sample[0, :, c:c + 512]
                sp.dma_start(dst, y_buf[0:rows, y % 2, :]).then_inc(y_stored[y % 2], 16)
            for u in range(2):
                sp.wait_ge(k_stored[u], 16 * NTT)
                sp.wait_ge(z_stored[u], 16 * NTT)
                sp.wait_ge(y_stored[u], 16 * NTT)
            sp.wait_ge(v_stored, 32)
            sp.wait_ge(cs_stored, 1 + 32 * NC)
            sp.wait_ge(tails_stored, 32)
            sp.wait_ge(s_stored, 32)

        @block.gpsimd
        def _(pool):
            own = Chain(pool, pool_own)
            pool.sem_inc(q_staged, 1)
            pool.memset(param_rows, 0.0).then_inc(consts_made, 1)
            for m, value in ((ident, 0.0), (ones, 1.0), (halves, 1.0), (tri, 1.0), (tri8, HD ** -0.5),
                             (neg_strict, -1.0), (below, 1.0), (not_below, 1.0)):
                own.mark(pool.memset(m[:], value))
            own.mark(pool.memset(eps[:], EPS))
            own.mark(pool.memset(level[:], 1.0))
            own.mark(pool.memset(below_s[:, 0, :], 1.0))
            own.mark(pool.memset(gates[:], 0.0))
            own.wait()

            def keep(m, op, base, pattern, mult, fill=0.0):
                own.mark(pool.affine_select(out=m, in_=m, compare_op=op, fill=fill, base=base,
                                            pattern=pattern, channel_multiplier=mult))

            keep(ident[:], ALU.not_equal, 0, [[-1, P]], 1, 1.0)
            own.wait()
            pool.sem_inc(ident_made, 1)
            keep(tri[:], ALU.is_ge, 0, [[1, P]], -1)
            keep(tri8[:], ALU.is_ge, 0, [[1, P]], -1)
            keep(neg_strict[:], ALU.is_gt, 0, [[1, P]], -1)
            keep(below[:], ALU.is_gt, 0, [[-1, P]], 1)
            keep(not_below[:], ALU.is_ge, 0, [[1, P]], -1)
            keep(halves[:, 0:HD], ALU.is_gt, HD, [[0, HD]], -1)
            keep(halves[:, HD:P], ALU.is_ge, -HD, [[0, HD]], 1)
            v = level[:, 0, :].rearrange("p (n c) -> p n c", c=2)
            own.wait()
            keep(v, ALU.is_equal, -1, [[2, P // 2], [1, 2]], -1)
            own.wait()
            keep(v, ALU.is_gt, 0, [[0, P // 2], [1, 2]], 0)
            for l in range(1, LEVELS - 1):
                b = 1 << l
                v = level[:, l, :].rearrange("p (n c) -> p n c", c=2 * b)
                own.wait()
                keep(v, ALU.is_ge, -b, [[-2 * b, P // (2 * b)], [0, 2 * b]], 1)
                own.wait()
                keep(v, ALU.is_gt, 2 * b, [[2 * b, P // (2 * b)], [0, 2 * b]], -1)
                own.wait()
                keep(v, ALU.is_gt, b, [[0, P // (2 * b)], [-1, 2 * b]], 0)
            for j in range(4):
                own.wait()
                rows = below_s[TS * j:TS * (j + 1), 0, :]
                keep(rows, ALU.is_gt, 0, [[-1, TS]], 1)
            own.wait()
            own.mark(pool.tensor_scalar(below_s[:, 1, :], below_s[:, 0, :], -1.0, 1.0, ALU.mult, ALU.add))
            own.wait()
            pool.sem_inc(consts_made, 1)
            pool.sem_inc(raw_free, 2)
            pool.wait_ge(ab_loaded, 16)
            own.link(pool.tensor_copy(ab_hi[:], ab_raw[:]))
            pool.tensor_tensor(ab_lo[:], ab_raw[:], ab_hi[:].bitcast(F32), ALU.subtract).then_inc(ab_split, 1)

            def split(turn, slot, used, count, hi=None, lo=None):
                hi = w_hi[:, slot, :] if hi is None else hi
                lo = w_lo[:, slot, :] if lo is None else lo
                pool.wait_ge(raw_loaded[slot], 16 * turn)
                pool.wait_ge(used, count)
                own.link(pool.tensor_tensor(hi, w_raw[:, slot, :], ones[:, 0:1].to_broadcast([P, BLK]), ALU.mult))
                own.mark(pool.tensor_tensor(lo, w_raw[:, slot, :], hi.bitcast(F32), ALU.subtract))
                own.wait()
                pool.sem_inc(w_split, 1)
                pool.sem_inc(raw_free, 1)

            for u in range(2):
                split(1, u, consts_made, 2)
            with pool.Fori(1, 5) as i:
                own.enter(i - 1, 4)
                for u in range(2):
                    split(i + 1, u, tok_ready, NTT * (2 * i + u - 1))
                own.leave(4)
            with pool.Fori(0, 2) as i:
                own.enter(i, 4)
                for u in range(2):
                    split(i + 6, u, dense_ready, 4 * i + 2 * u + 2)
                own.leave(2)

            own.link(pool.memset(q_stage, 0.0))
            with pool.Fori(0, WT) as i:
                for j in range(UNITS):
                    u, t = j % 2, j // 2
                    pool.wait_ge(scores_ready, 1 + earlier(i, j, 2))
                    pool.wait_ge(q_staged, 1 + UNITS * i + j)
                    rows = slice(HD * u, HD * (u + 1))
                    src = q_t[rows, bass.ds(i, 1), P * t:P * (t + 1)].rearrange("p o t -> p (o t)")
                    pool.tensor_tensor(q_stage[rows, u, :], src, ones[rows, :], ALU.mult).then_inc(q_staged, 1)

            pool.wait_ge(q_staged, 1 + UNITS * WT)
            for u in range(2):
                split(8, u, dense_ready, NC - 2 + 2 * u)
            pool.wait_ge(so_split, 2)
            tt = pool.tensor_tensor

            def decay_logs(c, n, first=False):
                if not first:
                    pool.wait_ge(qk_ready, c)
                g = glog[0:n, bass.ds(c, 1), :].rearrange("p o h -> p h o").to_broadcast([n, H, n])
                tt(d_gu[0:n, :, 0:n], tri[0:n, 0:n].unsqueeze(1).to_broadcast([n, H, n]), g,
                   ALU.mult).then_inc(gu_made, 1)

            def decays(c, s, n):
                b = beta[0:n, bass.ds(c, 1), :].rearrange("p o h -> p h o").to_broadcast([n, H, n])
                dt, at, qt = (x[0:n, :, 0:n] for x in (d_dt, d_at[:, s], d_qt[:, s]))
                pool.wait_ge(dt_made, c + 1)
                own.link(tt(at, dt, b, ALU.mult))
                tt(at, at, neg_strict[0:n, 0:n].unsqueeze(1).to_broadcast([n, H, n]), ALU.mult).then_inc(dts_made, 1)
                pool.wait_ge(dts_made, c + 1)
                tt(qt, dt, tri8[0:n, 0:n].unsqueeze(1).to_broadcast([n, H, n]), ALU.mult).then_inc(dtq_made, 1)
                pool.wait_ge(dtq_made, c + 1)
                pool.wait_ge(cn_made, c + 1)
                eg = d_eg.rearrange("p (u k) t -> p u k t", u=2)
                own.link(tt(d_kg[0:HD, s, :, 0:n], d_cn[0:HD, WT:KT, 0:n], eg[0:HD, 0, :, 0:n], ALU.mult))
                tt(d_kg[HD:P, s, :, 0:n], d_cn[HD:P, WT:KT, 0:n], eg[HD:P, 1, :, 0:n], ALU.mult).then_inc(kg_made, 1)
                pool.wait_ge(kg_made, c + 1)

            def first_level(c, s, n):
                pool.wait_ge(at_made, c + 1)
                at, x = d_at[0:n, s, :, 0:n], d_x[0:n, s, :, 0:n]
                own.link(tt(x, at, level[0:n, 0, 0:n].unsqueeze(1).to_broadcast([n, H, n]), ALU.mult))
                tt(x, x, ident[0:n, 0:n].unsqueeze(1).to_broadcast([n, H, n]), ALU.add).then_inc(x0_made, 1)
                pool.wait_ge(x0_made, c + 1)

            def decay_state(c, s):
                pool.wait_ge(s_new, c + 1)
                if s is None:
                    s = NT % 2
                    pool.wait_ge(s_loaded, 16)
                el = d_el[:, s, :].rearrange("p (u k) -> p u k", u=2).unsqueeze(3)
                own.link(tt(d_sd[0:HD], d_s[0:HD], el[0:HD, 0].to_broadcast([HD, WT, HD]), ALU.mult))
                tt(d_sd[HD:P], d_s[HD:P], el[HD:P, 1].to_broadcast([HD, WT, HD]), ALU.mult).then_inc(sdec_made, 1)
                pool.wait_ge(sdec_made, c + 1)

            decay_logs(0, P, True)
            decays(0, 0, P)
            first_level(0, 0, P)
            decay_logs(1, P)
            decays(1, 1, P)
            first_level(1, 1, P)
            decay_logs(2, P)
            with pool.Fori(0, (NT - 4) // 2) as i:
                own.enter(i, 8)
                for u in range(2):
                    decay_state(2 * i + u, u)
                    decays(2 * i + u + 2, u, P)
                    first_level(2 * i + u + 2, u, P)
                    decay_logs(2 * i + u + 3, P)
                own.leave((NT - 4) // 2)
            for c in (NT - 4, NT - 3, NT - 2):
                decay_state(c, c % 2)
                decays(c + 2, c % 2, P if c + 2 < NT else TS)
                first_level(c + 2, c % 2, P if c + 2 < NT else TS)
                if c + 3 <= NT:
                    decay_logs(c + 3, P if c + 3 < NT else TS)
            decay_state(NT - 1, (NT - 1) % 2)
            decay_state(NT, None)

            for u in range(2):
                split(9, u, dense_ready, NC + 2 * u + 2)
            with pool.Fori(0, ROUNDS) as g:
                own.enter(g, 8)
                for b, used in enumerate((-2, 0, 2, 4)):
                    split(2 * g + 10 + b // 2, b % 2, dense_ready, PER * g + MLP0 + used)
                own.leave(ROUNDS)
            split(26, 0, dense_ready, MLP0 + PER * ROUNDS - 4)
            split(27, 0, dense_ready, MLP0 + PER * ROUNDS, proj_hi, proj_lo)

        @block.scalar
        def _(act):
            own = Chain(act, act_own)
            for started in (sig_made, att_placed, cs_ready, cs_stored):
                act.sem_inc(started, 1)
            def square_x(t, rows):
                act.wait_ge(x_loaded[t % 3], 16 * (t // 3 + 1))
                own.link(act.activation(junk[0:rows, :], x_in[0:rows, t % 3, :], ACT.Square,
                                        accum_out=small[0:rows, t:t + 1]))
                act.activation(small[0:rows, 16 + t:17 + t], small[0:rows, t:t + 1], ACT.Sqrt, scale=1.0 / D,
                               bias=eps[0:rows, :]).then_inc(x_sd, 1)

            act.wait_ge(ident_made, 1)
            square_x(0, P)
            act.wait_ge(par_t, 1)
            act.activation(params[:], bank(7)[:, 0:100], ACT.Copy)
            for t, rows in enumerate(tile_rows):
                if t + 1 < NTT:
                    square_x(t + 1, tile_rows[t + 1])
                act.wait_ge(x_turned, t + 1)
                act.activation(act_hi[:, :, P * t:P * t + rows], token_banks(2 * (t % 2), rows),
                               ACT.Copy).then_inc(x_hi, 1)

            act.wait_ge(consts_made, 2)
            def place(y):
                t, rows = y % NTT, tile_rows[y % NTT]
                part, h = y // HALF, y // NTT % 2
                act.wait_ge(qk_turned, y + 1)
                act.activation((q_t, k_t)[part][:, HT * h:HT * (h + 1), P * t:P * t + rows],
                               bank(2 + y % 2)[:, 0:HC].rearrange("p (k t) -> p k t", k=HT)[:, :, 0:rows],
                               ACT.Copy).then_inc(qk_placed, 1)

            def store(y):
                t, rows = y % NTT, tile_rows[y % NTT]
                if y >= HALF:
                    c = HC * (y // NTT % 2)
                    act.wait_ge(qk_normed, y + 1)
                    act.dma_start(k_out[P * t:P * t + rows, c:c + HC] if t < NT else ks_out[:, c:c + HC],
                                  qk_buf[0:rows, y % 2, :]).then_inc(k_stored[y % 2], 16)

            for y in range(2 * HALF):
                rows = tile_rows[y % NTT]
                act.wait_ge(tok_ready, y + 1)
                if y:
                    act.wait_ge(ss_made, y)
                act.activation(sq_buf[0:rows, :], bank(y % 2)[0:rows, 0:HC], ACT.Square).then_inc(sq_made, 1)
                act.wait_ge(ss_made, y + 1)
                act.activation(small[0:rows, 8:8 + HH], small[0:rows, 0:HH], ACT.Sqrt, scale=1.0 / HD,
                               bias=eps[0:rows, :]).then_inc(sd_made, 1)
                if y:
                    store(y - 1)
                    place(y - 1)
            store(2 * HALF - 1)
            place(2 * HALF - 1)
            for y in range(2 * HALF, 3 * HALF):
                t, rows, c = y % NTT, tile_rows[y % NTT], HC * (y // NTT % 2)
                act.wait_ge(tok_ready, y + 1)
                act.activation(v_tok[0:rows, t, c:c + HC], bank(y % 2)[0:rows, 0:HC], ACT.Copy).then_inc(tok_free, 1)
            act.wait_ge(tok_free, 3 * HALF + 2)
            act.dma_start(v_out.rearrange("(t p) c -> p t c", p=P), v_tok[:, 0:NT, :]).then_inc(v_stored, 16)
            act.dma_start(vs_out, v_tok[0:TS, NT, :]).then_inc(v_stored, 16)
            for n in range(HALF):
                y, t, rows, c = 3 * HALF + n, n % NTT, tile_rows[n % NTT], HC * (n // NTT)
                act.wait_ge(tok_ready, y + 1)
                if n >= 2:
                    act.wait_ge(z_stored[n % 2], 16 * (n // 2))
                act.activation(z_buf[0:rows, n % 2, :], bank(y % 2)[0:rows, 0:HC], ACT.Silu).then_inc(z_silu, 1)
                act.wait_ge(z_made, n + 1)
                act.sem_inc(tok_free, 1)
                act.dma_start(z_dram[P * t:P * t + rows, c:c + HC], z_buf[0:rows, n % 2, :])\
                   .then_inc(z_stored[n % 2], 16)

            act.wait_ge(ab_ready, 1)
            act.activation(ab_t, psum[0:2 * H, 5:8, 0:CH], ACT.Copy).then_inc(ab_copied, 1)
            act.wait_ge(ab_turned, 1)
            both = bank(6)[:, 0:2 * H * NTT].rearrange("p (t a k u) -> p t a k u", a=2, u=2, k=WT)
            into = gates[:].rearrange("p t (a u k) -> p t a u k", a=2, u=2)
            for a in range(2):
                for u in range(2):
                    own.mark(act.activation(into[:, 0:NT, a, u, :], both[:, 0:NT, a, :, u], ACT.Copy))
                    own.mark(act.activation(into[0:TS, NT, a, u, :], both[0:TS, NT, a, :, u], ACT.Copy))
            own.wait()
            act.activation(beta[:], gates[:, :, H:2 * H], ACT.Sigmoid).then_inc(gates_act_done, 1)
            act.wait_ge(gates_dve_done, 1)
            own.link(act.activation(sp_e, sp_x[1], ACT.Exp))
            act.activation(sp_e, sp_e, ACT.Ln, bias=ones[:, 0:1]).then_inc(gates_act_done, 1)
            act.activation(small[:, 56:64].rearrange("p (u k) -> p u k", u=2),
                           dn_par[:, 0, :].rearrange("p (k u) -> p u k", u=2), ACT.Exp).then_inc(gates_act_done, 1)

            with act.Fori(0, 3) as i:
                own.enter(i, 8)
                for j in range(4):
                    m = 4 * i + j
                    act.wait_ge(dense_ready, m + 1)
                    own.wait()
                    x3 = xb[:, j % 2, :]
                    pieces = [(0, 0, CH, 3), (1, 0, CH, 3 + CH), (2, 0, TP - 2 * CH, 3 + 2 * CH),
                              (2, TP - 2 * CH, CH, TP + 6)]
                    for b, lo, hi, to in pieces:
                        last = act.activation(x3[:, to:to + hi - lo], bank(3 * (j % 2) + b)[:, lo:hi], ACT.Copy)
                    own.link(last)
                    act.sem_inc(dense_free, 1)
                    hist = params[:, 64:100].rearrange("p (i m) -> p i m", m=NC)
                    act.activation(x3[:, TP + 3:TP + 6].unsqueeze(2), hist[:, :, bass.ds(m, 1)], ACT.Copy).then_inc(xb_ready, 1)
                    act.activation(tails[:, 0, :, bass.ds(m, 1)], x3[:, TP:TP + 3].unsqueeze(2), ACT.Copy)
                    own.mark(act.activation(tails[:, 1, :, bass.ds(m, 1)], x3[:, T + 3:T + 6].unsqueeze(2), ACT.Copy))
                    act.wait_ge(y_ready, m + 1)
                    act.wait_ge(cs_stored, 1 + 32 * m)
                    act.activation(cb, yb, ACT.Silu).then_inc(cs_ready, 1)
                    act.wait_ge(cs_ready, 1 + m + 1)
                    dst = conv_dram[bass.ds(m, 1), :, :].rearrange("o p t -> p (o t)")
                    act.dma_start(dst[:, 0:TP], cb[:, 0:TP]).then_inc(cs_stored, 16)
                    act.dma_start(dst[:, TP:T], cb[:, TP + 3:T + 3]).then_inc(cs_stored, 16)
                own.leave(3)
            own.wait()
            act.sem_inc(tails_made, 1)
            act.wait_ge(tails_t, 1)
            act.activation(tails_out, bank(7)[0:72, 0:P], ACT.Copy).then_inc(tails_c, 1)

            def sigmoids(i, j):
                u, w = j % 2, P * (j // 2 + 1)
                act.wait_ge(scores_ready, 1 + UNITS * i + j + 1)
                act.wait_ge(att_turned, 1 + earlier(i, j, 2))
                z = psum[:, 2 * u:2 * u + 2, :].rearrange("p b c -> p (b c)")[:, 0:w]
                act.activation(keep_buf[:, u, 0:w], z, ACT.Sigmoid, scale=-(HD ** -0.5))
                act.activation(sig_buf[:, u, 0:w], z, ACT.Sigmoid, scale=HD ** -0.5).then_inc(sig_made, 1)

            def copy_out(i, t):
                act.wait_ge(o_ready, 1 + UNITS * i + 2 * t + 2)
                act.activation(o_buf[:, t % 2, :], bank(6 + t % 2)[:, 0:P], ACT.Copy).then_inc(o_copied, 1)

            act.wait_ge(cs_stored, 1 + 32 * NC)
            act.wait_ge(tails_stored, 32)
            for u in range(2):
                act.wait_ge(k_stored[u], 16 * NTT)
                act.wait_ge(z_stored[u], 16 * NTT)
            for u in range(2):
                act.activation(q_s[:, :, u, :], q_t[:, :, TP:T], ACT.Copy,
                               scale=halves[:, HD * u:HD * u + 1]).then_inc(s_staged, 1)
            act.activation(k_s, k_t[:, :, TP:T], ACT.Copy).then_inc(s_staged, 1)
            act.activation(v_s[0:TS, :], v_tok[0:TS, NT, :], ACT.Copy).then_inc(s_staged, 1)

            def copy_weights(i, j):
                w = P * (j // 2 + 1)
                act.wait_ge(att_turned, 1 + UNITS * i + j + 1)
                act.wait_ge(o_ready, 1 + earlier(i, j, 2))
                act.activation(at_buf[:, j % 2, 0:w], psum[:, 4:6, :].rearrange("p b c -> p (b c)")[:, 0:w],
                               ACT.Copy).then_inc(att_placed, 1)

            with act.Fori(0, WT) as i:
                sigmoids(i, 0)
                sigmoids(i, 1)
                copy_weights(i, 0)
                for j in range(UNITS):
                    if j + 2 < UNITS:
                        sigmoids(i, j + 2)
                    if j + 1 < UNITS:
                        copy_weights(i, j + 1)
                    if j and j % 2 == 0:
                        copy_out(i, j // 2 - 1)
                copy_out(i, NT - 1)

            def copy_cache(g):
                for n in range(8):
                    act.wait_ge(kc_turned, 8 * g + n + 1)
                    act.activation(kc_t[:, g, n // 4, 512 * (n % 4):512 * (n % 4 + 1)], bank(4 + n % 2),
                                   ACT.Copy).then_inc(kc_placed, 1)

            copy_cache(0)
            for g in range(2):
                act.wait_ge(s_scores, g + 1)
                old = psum[:, 0:4, :].rearrange("p b c -> p (b c)")
                for dst, sign in ((keep_s, -1.0), (sig_s, 1.0)):
                    act.activation(dst[:, 0:PAST], old, ACT.Sigmoid, scale=sign * HD ** -0.5)
                    last = act.activation(dst[:, PAST:SW], bank(6)[:, 0:TS], ACT.Sigmoid, scale=sign * HD ** -0.5)
                last.then_inc(s_sig, 1)
                if g == 0:
                    copy_cache(1)
                for n in range(5):
                    act.wait_ge(s_turned, 5 * g + n + 1)
                    rows, w = (P, 512) if n < 4 else (TS, P)
                    act.activation(at_buf[0:rows, n % 2, 0:w], bank(4 + n % 2)[0:rows, 0:w],
                                   ACT.Copy).then_inc(s_placed, 1)
                act.wait_ge(so_ready, g + 1)
                act.activation(o_buf[:, g, 0:HD], bank(7)[:, 0:HD], ACT.Copy).then_inc(so_copied, 1)

            act.wait_ge(so_split, 2)

            def prepare(c, s, n, first=False):
                act.wait_ge(gc_ready, c + 1)
                if not first:
                    act.wait_ge(kg_made, c)
                    act.wait_ge(qg_made, 2 * c)
                act.activation(d_gc[0:n, :], bank(4)[0:n, 0:H], ACT.Copy)
                act.activation(d_eg[:, :, 0:n], head_banks(6, P, n), ACT.Exp).then_inc(eg_made, 1)
                act.wait_ge(c_loaded, 16 * c + 16)
                act.activation(d_rs[:, :, 0:n], d_c[:, 0:KT, 0:n], ACT.Square).then_inc(sq2_made, 1)
                act.wait_ge(eg_made, c + 1)
                act.activation(d_el[:, s, :].unsqueeze(2), d_eg[:, :, n - 1:n], ACT.Copy)
                act.wait_ge(t0_made, c + 1)
                dt = d_dt[0:n, :, 0:n]
                act.activation(dt, dt, ACT.Relu, scale=-1.0).then_inc(t1_made, 1)
                act.wait_ge(t1_made, c + 1)
                act.activation(dt, dt, ACT.Exp, scale=-1.0).then_inc(dt_made, 1)
                act.wait_ge(ss_ready, c + 1)
                rs = d_rs[:, :, 0:n]
                act.activation(rs, head_banks(4, P, n), ACT.Ln, bias=eps[:]).then_inc(ln_made, 1)
                act.wait_ge(ln_made, c + 1)
                act.activation(rs, rs, ACT.Exp, scale=-0.5).then_inc(sd2_made, 1)
                act.wait_ge(cn_made, c + 1)
                for u in range(2):
                    act.activation(d_kz[:, u, :, 0:n], d_cn[:, WT:KT, 0:n], ACT.Copy,
                                   scale=halves[:, HD * u:HD * u + 1]).then_inc(kz_made, 1)
                act.wait_ge(kv_turned, c + 1)
                act.activation(d_v[0:n, s, :], bank(7)[0:n, :], ACT.Copy).then_inc(kv_placed, 1)

            def output(c, n):
                act.wait_ge(o_made, c + 1)
                act.activation(d_oq[0:n, :].rearrange("p (u v) -> p u v", u=2), psum[0:n, 6:8, 0:4 * HD],
                               ACT.Square).then_inc(osq_made, 1)
                act.wait_ge(ored_made, c + 1)
                act.activation(small[0:n, 8:16], small[0:n, 0:8], ACT.Sqrt, scale=1.0 / HD,
                               bias=eps[0:n, :]).then_inc(osd_made, 1)
                act.wait_ge(ot_ready, c + 1)
                src = bank(5).rearrange("p (k t) -> p k t", k=WT)[:, :, 0:n]
                act.activation(act_hi[:, 0:WT, bass.ds(P * c, n)], src, ACT.Copy).then_inc(mix_hi, 1)

            def first_level(c, n):
                for g in range(2):
                    act.wait_ge(t0_ready, 2 * c + g + 1)
                    act.activation(d_t[0:n, 4 * g:4 * g + 4, 0:n],
                                   bank(g)[0:n, :].rearrange("p (h t) -> p h t", h=4)[:, :, 0:n],
                                   ACT.Copy).then_inc(t_made, 1)

            def last_level(c, s):
                for g in range(2):
                    act.wait_ge(m_ready, step_of(c, LEVELS - 1, g))
                    act.activation(d_m[HD:P, 4 * g:4 * g + 4, 0:HD],
                                   bank(g)[HD:P, :].rearrange("p (h t) -> p h t", h=4)[:, :, 0:HD],
                                   ACT.Copy).then_inc(last_m_made, 1)
                for g in range(2):
                    act.wait_ge(x_ready, step_of(c, LEVELS - 1, g))
                    act.activation(d_x[0:HD, s, 4 * g:4 * g + 4, HD:P],
                                   bank(2 + g)[0:HD, :].rearrange("p (h t) -> p h t", h=4)[:, :, HD:P],
                                   ACT.Copy).then_inc(last_x_made, 1)

            prepare(0, 0, P, True)
            first_level(0, P)
            prepare(1, 1, P)
            last_level(0, 0)
            with act.Fori(0, (NT - 2) // 2) as i:
                for u in range(2):
                    first_level(2 * i + u + 1, P)
                    output(2 * i + u, P)
                    prepare(2 * i + u + 2, u, P)
                    last_level(2 * i + u + 1, 1 - u)
            first_level(NT - 1, P)
            output(NT - 2, P)
            prepare(NT, NT % 2, TS)
            last_level(NT - 1, (NT - 1) % 2)
            first_level(NT, TS)
            output(NT - 1, P)
            output(NT, TS)

            act.wait_ge(s_stored, 32)
            for t, rows in enumerate(tile_rows):
                act.wait_ge(xr_turned, t + 1)
                act.activation(h_t[:, :, P * t:P * t + rows], token_banks(2 * (t % 2), rows),
                               ACT.Copy).then_inc(h_placed, 1)

            act.wait_ge(added, KT + 2)
            for k in range(KT):
                if k >= 2:
                    act.wait_ge(nsum, k - 1)
                act.activation(wide[:, k % 2, :], h_t[:, k, :], ACT.Square).then_inc(nsq_made, 1)
            act.wait_ge(nsum, KT)
            act.activation(wide[:, 2, :].rearrange("p (c t) -> p c t", c=3), psum[:, 0:3, 0:CH], ACT.Ln,
                           scale=1.0 / D, bias=eps[:]).then_inc(nln, 1)
            act.wait_ge(nln, 1)
            act.activation(wide[:, 2, :], wide[:, 2, :], ACT.Exp, scale=-0.5).then_inc(nsd, 1)
            for k in range(KT):
                act.wait_ge(ntmp, k + 1)
                act.activation(act_hi[:, k, :], wide[:, k % 2, :], ACT.Copy).then_inc(nhi, 1)

            with act.Fori(0, ROUNDS) as g:
                own.enter(g, 4)
                for j in range(4):
                    act.wait_ge(dense_ready, PER * g + MLP0 + j + 1)
                    act.wait_ge(hid_split, 1 + 4 * g + max(j - 1, 0))
                    w = wide[:, j % 2, :]
                    own.link(act.activation(w.rearrange("p (c t) -> p c t", c=3),
                                            psum[:, 3 * (j % 2):3 * (j % 2) + 3, 0:CH], ACT.Relu))
                    act.sem_inc(relu_free, 1)
                    act.activation(w, w, ACT.Square).then_inc(relu_made, 1)
                own.leave(ROUNDS)
            def gate_head(slot, turn, used, count):
                act.wait_ge(raw_loaded[slot], 16 * turn)
                act.wait_ge(used, count)
                act.activation(w_hi[:, slot, :], w_raw[:, slot, :], ACT.Copy).then_inc(gate_hi, 1)

            for k in range(KT):
                act.wait_ge(added, KT * ROUNDS + k + 3)
                act.activation(act_hi[:, k, :], h_t[:, k, :], ACT.Copy, scale=params[:, KT + k:KT + k + 1])\
                   .then_inc(nhi, 1)
                if k == KT - 1:
                    gate_head(1, 26, dense_ready, MLP0 + PER * ROUNDS)
                if k >= 3:
                    act.wait_ge(acc_made, k - 2)
                act.activation(wide[:, k % 2 if k else 2, :], h_t[:, k, :], ACT.Square).then_inc(nsq_made, 1)

            def embed(t):
                rows = tile_rows[t]
                act.wait_ge(p_turned, t + 1)
                act.activation(hid_hi[:, 0:2, P * t:P * t + rows],
                               bank(6 + t % 2)[:, 0:256].rearrange("p (k t) -> p k t", k=2)[:, :, 0:rows],
                               ACT.Copy).then_inc(p_hi, 1)

            embed(0)
            embed(1)
            act.wait_ge(nsum, KT + 1)
            act.activation(small[:, 16:16 + NT], bank(5)[:, 0:NT], ACT.Sqrt, scale=1.0 / D, bias=eps[:])
            act.activation(small[0:TS, 16 + NT:17 + NT], bank(5)[0:TS, NT:NT + 1], ACT.Sqrt, scale=1.0 / D,
                           bias=eps[0:TS, :]).then_inc(nln, 1)
            act.wait_ge(nsd, 2)
            for y in range(2 * NTT):
                t, rows = y % NTT, tile_rows[y % NTT]
                act.wait_ge(ple_ready, y + 1)
                if y == NTT - 1:
                    gate_head(1, 27, ple_ready, NTT)
                    gate_head(0, 28, ple_ready, NTT)
                act.activation(sg_buf[0:rows, y % 2, :], bank(y % 2)[0:rows, :], ACT.Sigmoid,
                               scale=small[0:rows, 32 + t:33 + t]).then_inc(sg_made, 1)
                if y + 2 < NTT:
                    embed(y + 2)

        @block.vector
        def _(dve):
            own = Chain(dve, dve_own)
            for started in (o_split, mix_split, hid_split):
                dve.sem_inc(started, 1)
            dve.wait_ge(vecs_loaded, 160)

            def scale_x(t, rows):
                dve.wait_ge(x_sd, t + 1)
                own.link(dve.reciprocal(small[0:rows, 32 + t:33 + t], small[0:rows, 16 + t:17 + t]))
                if t >= 2:
                    dve.wait_ge(x_turned, t - 1)
                dve.scalar_tensor_tensor(out=x_sc[0:rows, t % 2, :], in0=x_in[0:rows, t % 3, :],
                                         scalar=small[0:rows, 32 + t:33 + t], in1=gmix_b[0:rows, :],
                                         op0=ALU.mult, op1=ALU.mult).then_inc(x_scaled, 1)

            scale_x(0, P)
            for t, rows in enumerate(tile_rows):
                if t + 1 < NTT:
                    scale_x(t + 1, tile_rows[t + 1])
                dve.wait_ge(x_hi, t + 1)
                cols = slice(P * t, P * t + rows)
                dve.tensor_tensor(act_lo[:, :, cols], token_banks(2 * (t % 2), rows),
                                  act_hi[:, :, cols].bitcast(F32), ALU.subtract).then_inc(x_lo, 1)

            dve.wait_ge(x_sd, NTT)
            for y in range(2 * HALF):
                rows = tile_rows[y % NTT]
                dve.wait_ge(sq_made, y + 1)
                dve.tensor_reduce(small[0:rows, 0:HH], sq_buf[0:rows, :].rearrange("p (h d) -> p h d", h=HH),
                                  AX.X, ALU.add).then_inc(ss_made, 1)
                dve.wait_ge(sd_made, y + 1)
                own.link(dve.reciprocal(small[0:rows, 48:48 + HH], small[0:rows, 8:8 + HH]))
                if y >= 2:
                    dve.wait_ge(qk_turned, y - 1)
                if y >= HALF + 2:
                    dve.wait_ge(k_stored[y % 2], 16 * ((y - HALF) // 2))
                buf = qk_buf[0:rows, y % 2, :].rearrange("p (h d) -> p h d", h=HH)
                own.link(dve.tensor_tensor(buf, bank(y % 2)[0:rows, 0:HC].rearrange("p (h d) -> p h d", h=HH),
                                           small[0:rows, 48:48 + HH].unsqueeze(2).to_broadcast([rows, HH, HD]),
                                           ALU.mult))
                dve.sem_inc(tok_free, 1)
                g = heads_g[0:rows, y // HALF:y // HALF + 1, :].to_broadcast([rows, HH, HD])
                dve.tensor_tensor(buf, buf, g, ALU.mult).then_inc(qk_normed, 1)
            for n in range(HALF):
                rows = tile_rows[n % NTT]
                dve.wait_ge(z_silu, n + 1)
                buf = z_buf[0:rows, n % 2, :].rearrange("p (h d) -> p h d", h=HH)
                dve.tensor_tensor(buf, buf, heads_g[0:rows, 2:3, :].to_broadcast([rows, HH, HD]),
                                  ALU.mult).then_inc(z_made, 1)
            dve.wait_ge(gates_act_done, 1)
            al, nal = sp_x
            bias = dn_par[:, 1, :].rearrange("p (k u) -> p u k", u=2).unsqueeze(1).to_broadcast([P, NTT, 2, WT])
            own.link(dve.tensor_tensor(al.rearrange("p t (u k) -> p t u k", u=2),
                                       gates[:, :, 0:H].rearrange("p t (u k) -> p t u k", u=2), bias, ALU.add))
            dve.scalar_tensor_tensor(out=nal, in0=al, scalar=-1.0, in1=al, op0=ALU.mult, op1=ALU.min).then_inc(gates_dve_done, 1)
            dve.wait_ge(gates_act_done, 3)
            own.link(dve.scalar_tensor_tensor(out=al, in0=al, scalar=0.0, in1=sp_e, op0=ALU.max, op1=ALU.add))
            own.link(dve.scalar_tensor_tensor(out=glog[:], in0=al, scalar=-1.0,
                                              in1=small[:, 56:64].unsqueeze(1).to_broadcast([P, NTT, H]),
                                              op0=ALU.mult, op1=ALU.mult))
            own.link(dve.memset(xb[:, :, 0:3], 0.0))
            with dve.Fori(0, 3) as i:
                own.enter(i, 12)
                for j in range(4):
                    m = 4 * i + j
                    dve.wait_ge(xb_ready, m + 1)
                    dve.wait_ge(cs_ready, 1 + m)
                    taps = params[:, 16:64].rearrange("p (i m) -> p i m", m=NC)
                    x3 = xb[:, j % 2, :]
                    for tap in range(4):
                        w = taps[:, tap, bass.ds(m, 1)]
                        if tap == 0:
                            own.link(dve.tensor_scalar(yb, x3[:, 0:YB], w, None, ALU.mult))
                        elif tap < 3:
                            own.link(dve.scalar_tensor_tensor(out=yb, in0=x3[:, tap:tap + YB], scalar=w, in1=yb,
                                                              op0=ALU.mult, op1=ALU.add))
                        else:
                            dve.scalar_tensor_tensor(out=yb, in0=x3[:, tap:tap + YB], scalar=w, in1=yb,
                                                     op0=ALU.mult, op1=ALU.add).then_inc(y_ready, 1)
                own.leave(3)

            def split_out(i, t):
                dve.wait_ge(o_turned, NT * i + t + 1)
                src = bank(6 + t % 2)[:, P:2 * P].unsqueeze(1)
                cols = slice(P * t, P * (t + 1))
                dst = act_hi[:, bass.ds(WT + i, 1), cols]
                own.link(dve.tensor_copy(dst, src))
                own.link(dve.tensor_tensor(act_lo[:, bass.ds(WT + i, 1), cols], src, dst.bitcast(F32),
                                           ALU.subtract))
                dve.sem_inc(o_split, 1)

            with dve.Fori(0, WT) as i:
                own.enter(i, 3 * UNITS + 2 * NT)
                for j in range(UNITS):
                    u, w = j % 2, P * (j // 2 + 1)
                    keep, sig = keep_buf[:, u, :], sig_buf[:, u, :]
                    dve.wait_ge(sig_made, 1 + UNITS * i + j + 1)
                    own.mark(dve.tensor_tensor(sig[:, w - P:w], sig[:, w - P:w], below[:], ALU.mult))
                    own.link(dve.tensor_tensor(keep[:, w - P:w], keep[:, w - P:w], not_below[:], ALU.max))
                    back = keep[:, 0:w][:, ::-1]
                    own.link(dve.tensor_tensor_scan(back, back, back, 1.0, ALU.mult, ALU.min))
                    dve.tensor_tensor(sig[:, 0:w - 1], sig[:, 0:w - 1], keep[:, 1:w], ALU.mult).then_inc(att_made, 1)
                    if j % 2 and j >= 5:
                        split_out(i, (j - 5) // 2)
                split_out(i, NT - 2)
                split_out(i, NT - 1)
                own.leave(WT)

            for g in range(2):
                dve.wait_ge(s_sig, g + 1)
                own.mark(dve.tensor_tensor(sig_s[:, PAST:SW], sig_s[:, PAST:SW], below_s[:, 0, :], ALU.mult))
                own.link(dve.tensor_tensor(keep_s[:, PAST:SW], keep_s[:, PAST:SW], below_s[:, 1, :], ALU.max))
                back = keep_s[:, ::-1]
                own.link(dve.tensor_tensor_scan(back, back, back, 1.0, ALU.mult, ALU.min))
                dve.tensor_tensor(sig_s[:, 0:SW - 1], sig_s[:, 0:SW - 1], keep_s[:, 1:SW],
                                  ALU.mult).then_inc(s_att, 1)
            for g in range(2):
                dve.wait_ge(so_turned, 1)
                src = psum[:, 5:7, 64 + TS * g:64 + TS * (g + 1)]
                dst = act_hi[:, WT + 2 * g:WT + 2 * g + 2, TP:T]
                own.link(dve.tensor_copy(dst, src))
                dve.tensor_tensor(act_lo[:, WT + 2 * g:WT + 2 * g + 2, TP:T], src, dst.bitcast(F32),
                                  ALU.subtract).then_inc(so_split, 1)

            dve.memset(d_s, 0.0).then_inc(s_new, 1)

            tt = dve.tensor_tensor

            def decay_differences(c, n):
                dve.wait_ge(eg_made, c + 1)
                tt(d_dt[0:n, :, 0:n], head_banks(6, n, n), d_gc[0:n, :].unsqueeze(2).to_broadcast([n, H, n]),
                   ALU.subtract).then_inc(t0_made, 1)

            def unit_norms(c, n):
                dve.wait_ge(sd2_made, c + 1)
                tt(d_cn[:, :, 0:n], d_c[:, 0:KT, 0:n], d_rs[:, :, 0:n], ALU.mult).then_inc(cn_made, 1)

            def decayed_queries(c, s, n):
                dve.wait_ge(cn_made, c + 1)
                for u in range(2):
                    rows = slice(HD * u, HD * (u + 1))
                    dve.scalar_tensor_tensor(out=d_qg[rows, s, :, 0:n], in0=d_cn[rows, 0:WT, 0:n], scalar=HD ** -0.5,
                                             in1=d_eg[rows, 4 * u:4 * u + 4, 0:n], op0=ALU.mult,
                                             op1=ALU.mult).then_inc(qg_made, 1)

            def decayed_keys(c, s, n):
                dve.wait_ge(kv_turned, c + 1)
                dve.wait_ge(dt_made, c + 1)
                last = d_dt[0:n, :, n - 1:n].rearrange("p h o -> p (h o)")
                tt(heads(d_kd[:, s], n), heads(bank(6), n), per_head(last, n, HD), ALU.mult).then_inc(kd_made, 1)

            def key_matrix(c, s, n):
                dve.wait_ge(g_ready, c + 1)
                dve.wait_ge(dts_made, c + 1)
                at = d_at[0:n, s, :, 0:n]
                tt(at, head_banks(4, n, n), at, ALU.mult).then_inc(at_made, 1)

            def query_matrix(c, s, n):
                dve.wait_ge(qk_ready, c + 1)
                dve.wait_ge(dtq_made, c + 1)
                qt = d_qt[0:n, s, :, 0:n]
                tt(qt, head_banks(6, n, n), qt, ALU.mult).then_inc(qt_made, 1)

            def rest_of_values(c, s, n):
                dve.wait_ge(ks_ready, c + 1)
                dve.wait_ge(kv_placed, c + 1)
                tt(heads(d_r, n), heads(d_v[:, s], n), value_banks(n), ALU.subtract).then_inc(r_made, 1)

            def new_values(c, n):
                dve.wait_ge(vn_ready, c + 1)
                b = per_head(beta[0:n, bass.ds(c, 1), :].rearrange("p o h -> p (o h)"), n, HD)
                tt(heads(d_vn, n), heads(bank(5), n), b, ALU.mult).then_inc(vn_made, 1)

            def new_state(c):
                dve.wait_ge(ds_ready, c + 1)
                dve.wait_ge(sdec_made, c + 1)
                tt(d_s, bank(5)[:, 0:4 * HD].rearrange("p (k e) -> p k e", k=WT), d_sd, ALU.add).then_inc(s_new, 1)

            def output_squares(c, n):
                dve.wait_ge(osq_made, c + 1)
                dve.tensor_reduce(small[0:n, 0:8], d_oq[0:n, :].rearrange("p (h d) -> p h d", h=H), AX.X,
                                  ALU.add).then_inc(ored_made, 1)

            def normed_output(c, n):
                dve.wait_ge(osd_made, c + 1)
                own.link(dve.reciprocal(small[0:n, 48:56], small[0:n, 8:16]))
                own.link(tt(heads(d_on, n), value_banks(n), per_head(small[0:n, 48:56], n, HD), ALU.mult))
                dve.wait_ge(z_loaded, 16 * c + 16)
                tt(d_on[0:n, :], d_on[0:n, :], d_z[0:n, :], ALU.mult).then_inc(on_made, 1)

            def split_output(c, n):
                dve.wait_ge(mix_hi, c + 1)
                src = bank(5).rearrange("p (k t) -> p k t", k=WT)[:, :, 0:n]
                cols = bass.ds(P * c, n)
                tt(act_lo[:, 0:WT, cols], src, act_hi[:, 0:WT, cols].bitcast(F32), ALU.subtract).then_inc(mix_split, 1)

            def mask(c, l, n):
                for g in range(2):
                    dve.wait_ge(m_ready, step_of(c, l, g))
                    tt(d_m[0:n, 4 * g:4 * g + 4, 0:n], bank(g)[0:n, :].rearrange("p (h t) -> p h t", h=4)[:, :, 0:n],
                       level[0:n, l, 0:n].unsqueeze(1).to_broadcast([n, 4, n]), ALU.mult).then_inc(m_made, 1)

            def renew(c, s, l, n):
                for g in range(2):
                    hs = slice(4 * g, 4 * g + 4)
                    t_, x_ = d_t[0:n, hs, 0:n], d_x[0:n, s, hs, 0:n]
                    pt, px = (bank(b + g)[0:n, :].rearrange("p (h t) -> p h t", h=4)[:, :, 0:n] for b in (0, 2))
                    if l < levels_of(n) - 1:
                        dve.wait_ge(t_ready, inner_step(c, l, g))
                        tt(t_, pt, t_, ALU.add).then_inc(t_made, 1)
                    dve.wait_ge(x_ready, step_of(c, l, g))
                    tt(x_, px, x_, ALU.add).then_inc(x_made, 1)

            def inverse(c, s, n, scanned, prepared):
                for l in range(levels_of(n)):
                    if 0 < l < LEVELS - 1:
                        mask(c, l, n)
                    if scanned and l == 0:
                        rest_of_values(c - 1, 1 - s, P)
                    if scanned and l == 1:
                        new_values(c - 1, P)
                    if scanned and l == 2:
                        normed_output(c - 1, P)
                    if scanned and l == 3:
                        split_output(c - 1, P)
                    if prepared and l == 4:
                        unit_norms(c + 1, prepared)
                    if prepared and l == 5:
                        key_matrix(c + 1, 1 - s, prepared)
                        decayed_keys(c + 1, 1 - s, prepared)
                    if 0 < l < LEVELS - 1:
                        renew(c, s, l, n)
                    if scanned and l == 1:
                        new_state(c - 1)
                        output_squares(c - 1, P)
                    if prepared and l == 3:
                        decay_differences(c + 1, prepared)
                    if prepared and l == 4:
                        decayed_queries(c + 1, 1 - s, prepared)
                    if prepared and l == 6:
                        query_matrix(c + 1, 1 - s, prepared)

            decay_differences(0, P)
            unit_norms(0, P)
            decayed_queries(0, 0, P)
            decayed_keys(0, 0, P)
            key_matrix(0, 0, P)
            query_matrix(0, 0, P)
            inverse(0, 0, P, False, P)
            with dve.Fori(0, (NT - 2) // 2) as i:
                own.enter(i, 4)
                for u in range(2):
                    inverse(2 * i + u + 1, 1 - u, P, True, P)
                own.leave((NT - 2) // 2)
            inverse(NT - 1, (NT - 1) % 2, P, True, TS)
            inverse(NT, NT % 2, TS, True, None)
            rest_of_values(NT, NT % 2, TS)
            new_values(NT, TS)
            new_state(NT)
            output_squares(NT, TS)
            normed_output(NT, TS)
            split_output(NT, TS)

            def add_tile(J, b, k):
                dve.wait_ge(dense_ready, J + 1)
                h3 = h_t[:, k, :].rearrange("p o (c t) -> p (o c) t", c=3)
                dve.tensor_tensor(h3, psum[:, b:b + 3, 0:CH], h3, ALU.add).then_inc(added, 1)

            dve.wait_ge(h_placed, NTT)
            with dve.Fori(0, 2) as i:
                for j in range(4):
                    add_tile(4 * i + j + OUT0, 3 * (j % 2), bass.ds(4 * i + j, 1))

            dve.wait_ge(nsd, 1)

            def scaled(k):
                dve.scalar_tensor_tensor(out=wide[:, k % 2, :], in0=h_t[:, k, :], scalar=params[:, k:k + 1],
                                         in1=wide[:, 2, :], op0=ALU.mult, op1=ALU.mult).then_inc(ntmp, 1)

            scaled(0)
            for k in range(KT):
                if k + 1 < KT:
                    if k:
                        dve.wait_ge(nlo, k)
                    scaled(k + 1)
                dve.wait_ge(nhi, k + 1)
                dve.tensor_tensor(act_lo[:, k, :], wide[:, k % 2, :], act_hi[:, k, :].bitcast(F32),
                                  ALU.subtract).then_inc(nlo, 1)

            def split_hidden(g):
                for j in range(4):
                    dve.wait_ge(relu_made, 4 * g + j + 1)
                    own.link(dve.tensor_copy(hid_hi[:, j, :], wide[:, j % 2, :]))
                    dve.tensor_tensor(hid_lo[:, j, :], wide[:, j % 2, :], hid_hi[:, j, :].bitcast(F32),
                                      ALU.subtract).then_inc(hid_split, 1)

            with dve.Fori(0, ROUNDS - 1) as g:
                own.enter(g, 4)
                split_hidden(g)
                for j in range(KT):
                    add_tile(PER * g + MLP0 + 4 + j, 3 * (j % 2), slice(j, j + 1))
                own.leave(ROUNDS - 1)
            def gate_rest(n, slot):
                dve.wait_ge(gate_hi, n + 1)
                dve.tensor_tensor(w_lo[:, slot, :], w_raw[:, slot, :], w_hi[:, slot, :].bitcast(F32),
                                  ALU.subtract).then_inc(gate_split, 1)

            split_hidden(ROUNDS - 1)
            acc = wide[:, 2, :]
            for k in range(KT):
                add_tile(PER * (ROUNDS - 1) + MLP0 + 4 + k, 3 * (k % 2), slice(k, k + 1))
                dve.wait_ge(nhi, KT + k + 1)
                dve.scalar_tensor_tensor(out=act_lo[:, k, :], in0=h_t[:, k, :], scalar=params[:, KT + k:KT + k + 1],
                                         in1=act_hi[:, k, :].bitcast(F32), op0=ALU.mult,
                                         op1=ALU.subtract).then_inc(nlo, 1)
                if k == KT - 1:
                    gate_rest(0, 1)
                if k:
                    dve.wait_ge(nsq_made, KT + k + 1)
                    if k > 1:
                        dve.wait_ge(acc_made, k - 1)
                    dve.tensor_tensor(acc, acc, wide[:, k % 2, :], ALU.add).then_inc(acc_made, 1)

            def embed(t):
                rows = tile_rows[t]
                cols = slice(P * t, P * t + rows)
                dve.wait_ge(p_hi, t + 1)
                dve.tensor_tensor(hid_lo[:, 0:2, cols],
                                  bank(6 + t % 2)[:, 0:256].rearrange("p (k t) -> p k t", k=2)[:, :, 0:rows],
                                  hid_hi[:, 0:2, cols].bitcast(F32), ALU.subtract).then_inc(p_lo, 1)

            embed(0)
            embed(1)
            dve.wait_ge(nln, 2)
            dve.reciprocal(small[:, 32:32 + NT], small[:, 16:16 + NT])
            dve.reciprocal(small[0:TS, 32 + NT:33 + NT], small[0:TS, 16 + NT:17 + NT]).then_inc(nsd, 1)
            for y in range(2 * NTT):
                rows = tile_rows[y % NTT]
                if y == NTT - 1:
                    gate_rest(1, 1)
                    gate_rest(2, 0)
                dve.wait_ge(sg_made, y + 1)
                sg = sg_buf[0:rows, y % 2, :]
                own.link(dve.tensor_tensor(sg, bank(2 + y % 2)[0:rows, :], sg, ALU.mult))
                if y >= 2:
                    dve.wait_ge(y_stored[y % 2], 16 * (y // 2))
                dve.tensor_tensor(y_buf[0:rows, y % 2, :], bank(4 + y % 2)[0:rows, :], sg, ALU.add).then_inc(y_made, 1)
                if y + 2 < NTT:
                    embed(y + 2)

        @block.tensor
        def _(pe):
            for started in (scores_ready, att_turned, o_ready):
                pe.sem_inc(started, 1)
            pe.sem_inc(tok_free, 2)
            pe.sem_inc(dense_free, 2)
            pe.sem_inc(added, 2)
            pe.wait_ge(ident_made, 1)
            pe.wait_ge(vecs_loaded, 160)
            pe.transpose(bank(7)[:, 0:100], param_rows[0:100, :], ident[0:100, 0:100]).then_inc(par_t, 1)
            for t, rows in enumerate(tile_rows):
                pe.wait_ge(x_scaled, t + 1)
                if t >= 2:
                    pe.wait_ge(x_lo, t - 1)
                for k in range(KT):
                    last = pe.transpose(bank(2 * (t % 2) + k // 4)[:, P * (k % 4):P * (k % 4) + rows],
                                        x_sc[0:rows, t % 2, P * k:P * k + P], ident[0:rows, 0:rows])
                last.then_inc(x_turned, 1)
            pe.wait_ge(x_lo, NTT)
            pe.wait_ge(consts_made, 2)

            def token_product(out, rows, t, w_h, w_l, K=KT, hi=act_hi, lo=act_lo, before=None):
                cols = slice(P * t, P * t + rows)
                for k in range(K):
                    if before:
                        before(k)
                    pe.matmul(out, hi[:, k, cols], w_h(k), start=(k == 0), stop=False)
                    pe.matmul(out, hi[:, k, cols], w_l(k), start=False, stop=False)
                    last = pe.matmul(out, lo[:, k, cols], w_h(k), start=False, stop=(k == K - 1))
                return last

            def turn_qk(y):
                t, rows = y % NTT, tile_rows[y % NTT]
                pe.wait_ge(qk_normed, y + 1)
                if y >= 2:
                    pe.wait_ge(qk_placed, y - 1)
                for k in range(HT):
                    last = pe.transpose(bank(2 + y % 2)[:, P * k:P * k + rows],
                                        qk_buf[0:rows, y % 2, P * k:P * k + P], ident[0:rows, 0:rows])
                last.then_inc(qk_turned, 1)

            for b in range(8):
                pe.wait_ge(w_split, b + 1)
                for t, rows in enumerate(tile_rows):
                    y = NTT * b + t
                    pe.wait_ge(tok_free, y + 1)
                    token_product(bank(y % 2)[0:rows, 0:HC], rows, t, lambda k: whi_cols[:, b % 2, k, :],
                                  lambda k: wlo_cols[:, b % 2, k, :]).then_inc(tok_ready, 1)
                    if 1 <= y <= 2 * HALF:
                        turn_qk(y - 1)
            def dense(base, lhs_hi, lhs_lo, K=KT, hi=act_hi, lo=act_lo, before=None, rows=P):
                for k in range(K):
                    if before:
                        before(k)
                    for w, a in ((lhs_hi, hi), (lhs_hi, lo), (lhs_lo, hi)):
                        for c in range(3):
                            last = pe.matmul(bank(base + c)[0:rows, 0:CH], w(k), a[:, k, CH * c:CH * (c + 1)],
                                             start=(k == 0 and w is lhs_hi and a is hi),
                                             stop=(k == K - 1 and w is lhs_lo))
                return last

            pe.wait_ge(ab_split, 1)
            dense(5, lambda k: ab_hi[:, k, :], lambda k: ab_lo[:, k, :], rows=2 * H).then_inc(ab_ready, 1)
            pe.wait_ge(ab_copied, 1)
            for t, rows in enumerate(tile_rows):
                last = pe.transpose(bank(6)[0:rows, 2 * H * t:2 * H * (t + 1)],
                                    ab_flat[:, P * t:P * t + rows], ident[0:2 * H, 0:2 * H])
            last.then_inc(ab_turned, 1)

            pe.wait_ge(tok_free, 4 * HALF + 2)
            pe.wait_ge(qk_placed, 2 * HALF)
            with pe.Fori(0, 3) as i:
                for j in range(4):
                    slot, mm = j // 2, j % 2
                    if mm == 0:
                        pe.wait_ge(w_split, 8 + 2 * i + slot + 1)
                    pe.wait_ge(dense_free, 4 * i + j + 1)
                    last = dense(3 * (j % 2), lambda k: whi_cols[:, slot, k, P * mm:P * mm + P],
                                 lambda k: wlo_cols[:, slot, k, P * mm:P * mm + P])
                    last.then_inc(dense_ready, 1)
            pe.wait_ge(tails_made, 1)
            pe.transpose(bank(7)[0:72, 0:P], tails[:].rearrange("p a i m -> p (a i m)"), ident[:]).then_inc(tails_t, 1)

            def scores(i, j):
                u, w = j % 2, P * (j // 2 + 1)
                pe.wait_ge(q_staged, 1 + UNITS * i + j + 1)
                pe.wait_ge(sig_made, 1 + earlier(i, j, 2))
                for c in range(0, w, 512):
                    n = min(512, w - c)
                    last = pe.matmul(bank(2 * u + c // 512)[:, 0:n], q_stage[:, u, :],
                                     k_t[:, bass.ds(i, 1), c:c + n].rearrange("p o t -> p (o t)"),
                                     start=True, stop=True)
                last.then_inc(scores_ready, 1)

            def turn_out(i, t):
                pe.wait_ge(o_copied, NT * i + t + 1)
                pe.transpose(bank(6 + t % 2)[:, P:2 * P], o_buf[:, t % 2, :], ident[:]).then_inc(o_turned, 1)

            def turn_weights(i, j):
                pe.wait_ge(att_made, UNITS * i + j + 1)
                pe.wait_ge(att_placed, 1 + UNITS * i + j)
                for n in range(j // 2 + 1):
                    last = pe.transpose(bank(4 + n // 4)[:, P * (n % 4):P * (n % 4 + 1)],
                                        sig_buf[:, j % 2, P * n:P * (n + 1)], ident[:])
                last.then_inc(att_turned, 1)

            def values(i, j):
                u, t = j % 2, j // 2
                pe.wait_ge(att_placed, 1 + UNITS * i + j + 1)
                if u == 0:
                    pe.wait_ge(o_split, 1 + NT * i + max(t - 1, 0))
                for n in range(t + 1):
                    v = v_tok[:, n, bass.ds(P * i + HD * u, HD)]
                    last = pe.matmul(bank(6 + t % 2)[:, HD * u:HD * (u + 1)], at_buf[:, u, P * n:P * (n + 1)], v,
                                     start=(n == 0), stop=(n == t))
                last.then_inc(o_ready, 1)

            with pe.Fori(0, WT) as i:
                scores(i, 0)
                scores(i, 1)
                turn_weights(i, 0)
                for j in range(UNITS):
                    if j + 2 < UNITS:
                        scores(i, j + 2)
                    if j + 1 < UNITS:
                        turn_weights(i, j + 1)
                    values(i, j)
                    if j % 2 and j >= 3:
                        turn_out(i, (j - 3) // 2)
                turn_out(i, NT - 1)

            pe.wait_ge(o_split, 1 + WT * NT)
            pe.wait_ge(s_staged, 4)
            def turn_cache(g):
                pe.wait_ge(kc_loaded, 16 * (g + 1))
                for n in range(8):
                    if 8 * g + n >= 2:
                        pe.wait_ge(kc_placed, 8 * g + n - 1)
                    for b in range(4):
                        last = pe.transpose(bank(4 + n % 2)[:, P * b:P * (b + 1)],
                                            k_raw[:, 4 * (n % 4) + b, P * (n // 4):P * (n // 4 + 1)], ident[:])
                    last.then_inc(kc_turned, 1)

            def stream_scores(g):
                pe.wait_ge(kc_placed, 8 * (g + 1))
                for j in range(4):
                    q = q_s[:, 2 * g + j // 2, j % 2, :]
                    for c in range(PAST // 512):
                        pe.matmul(psum[TS * j:TS * (j + 1), c, :], q, kc_t[:, g, j // 2, 512 * c:512 * (c + 1)],
                                  start=True, stop=True)
                    last = pe.matmul(psum[TS * j:TS * (j + 1), 6, 0:TS], q, k_s[:, 2 * g + j // 2, :],
                                     start=True, stop=True)
                last.then_inc(s_scores, 1)

            def turn_stacked(g, n):
                rows = P if n < 4 else TS
                if n >= 2:
                    pe.wait_ge(s_placed, 5 * g + n - 1)
                for b in range(4 if n < 4 else 1):
                    src = sig_s[:, 512 * n + P * b:512 * n + P * b + rows]
                    last = pe.transpose(bank(4 + n % 2)[0:rows, P * b:P * (b + 1)], src, ident[:])
                last.then_inc(s_turned, 1)

            turn_cache(0)
            stream_scores(0)
            turn_cache(1)
            pe.wait_ge(kc_placed, 16)
            for g in range(2):
                pe.wait_ge(s_att, g + 1)
                pe.wait_ge(vc_loaded, 16 * (g + 1))
                turn_stacked(g, 0)
                for n in range(5):
                    if n < 4:
                        turn_stacked(g, n + 1)
                    elif g == 0:
                        stream_scores(1)
                    if g and n == 0:
                        pe.wait_ge(so_copied, 1)
                    pe.wait_ge(s_placed, 5 * g + n + 1)
                    for b in range(4 if n < 4 else 1):
                        for j in range(4):
                            rows = P if n < 4 else TS
                            v = v_c[:, 4 * n + b, HD * j:HD * (j + 1)] if n < 4 else \
                                v_s[0:TS, HD * (4 * g + j):HD * (4 * g + j + 1)]
                            last = pe.matmul(bank(7)[TS * j:TS * (j + 1), 0:HD],
                                             at_buf[0:rows, n % 2, P * b + TS * j:P * b + TS * (j + 1)], v,
                                             start=(n == 0 and b == 0), stop=(n == 4))
                last.then_inc(so_ready, 1)
            pe.wait_ge(so_copied, 2)
            for g in range(2):
                for j in range(4):
                    rows = slice(TS * j, TS * (j + 1))
                    last = pe.matmul(psum[HD * (j % 2):HD * (j % 2 + 1), 5 + j // 2, 64 + TS * g:64 + TS * (g + 1)],
                                     o_buf[rows, g, 0:HD], ident[rows, rows], start=True, stop=True)
            last.then_inc(so_turned, 1)

            pe.wait_ge(so_split, 2)

            def group(b, h, n):
                return bank(b + h % 2)[0:n, P * (h // 2):P * (h // 2) + n]

            def value(h, n):
                return bank(6 + h % 2)[0:n, HD * (h // 2):HD * (h // 2 + 1)]

            def half(h):
                return slice(HD * (h % 2), HD * (h % 2) + HD)

            def decay_sums(c, n, first=False):
                if not first:
                    pe.wait_ge(at_made, c)
                    pe.wait_ge(qt_made, c)
                pe.wait_ge(gu_made, c + 1)
                for g in range(2):
                    pe.matmul(bank(6 + g).rearrange("p (h t) -> p h t", h=4)[:, :, 0:n], ones[0:n, :],
                              d_gu[0:n, 4 * g:4 * g + 4, 0:n], start=True, stop=True)
                pe.matmul(bank(4)[0:n, 0:H], tri[0:n, 0:n], glog[0:n, bass.ds(c, 1), :].rearrange("p o h -> p (o h)"),
                          start=True, stop=True).then_inc(gc_ready, 1)

            def square_sums(c, n, first=False):
                pe.wait_ge(sq2_made, c + 1)
                pe.wait_ge(eg_made, c + 1)
                if not first:
                    pe.wait_ge(mix_split, c)
                for g in range(2):
                    last = pe.matmul(bank(4 + g).rearrange("p (h t) -> p h t", h=4)[:, :, 0:n], halves[:],
                                     d_rs[:, 4 * g:4 * g + 4, 0:n], start=True, stop=True)
                last.then_inc(ss_ready, 1)

            def turn_keys(c, n):
                pe.wait_ge(cn_made, c + 1)
                pe.wait_ge(t0_made, c + 1)
                for k in range(WT):
                    pe.transpose(bank(6)[0:n, P * k:P * (k + 1)], d_cn[:, WT + k, 0:n], ident[:])
                for k in range(WT):
                    last = pe.transpose(bank(7)[0:n, P * k:P * (k + 1)], d_c[:, 2 * WT + k, 0:n], ident[:])
                last.then_inc(kv_turned, 1)

            def with_keys(b, at, n):
                for h in range(H):
                    last = pe.matmul(group(b, h, n), d_kz[:, h % 2, h // 2, 0:n], d_cn[:, at + h // 2, 0:n],
                                     start=True, stop=True)
                return last

            def key_products(c, n):
                pe.wait_ge(kz_made, 2 * c + 2)
                with_keys(4, WT, n).then_inc(g_ready, 1)

            def query_products(c, n):
                pe.wait_ge(kd_made, c + 1)
                pe.wait_ge(kv_placed, c + 1)
                with_keys(6, 0, n).then_inc(qk_ready, 1)

            def values_of_state(c, s, n):
                pe.wait_ge(kg_made, c + 1)
                pe.wait_ge(s_new, c + 1)
                for h in range(H):
                    last = pe.matmul(value(h, n), d_kg[half(h), s, h // 2, 0:n], d_s[half(h), h // 2, :],
                                     start=True, stop=True)
                last.then_inc(ks_ready, 1)

            def solved_values(c, s, n):
                pe.wait_ge(r_made, c + 1)
                if n == P:
                    pe.wait_ge(last_x_made, 2 * c + 2)
                else:
                    pe.wait_ge(x_made, inner_step(c, levels_of(n) - 1, 1))
                for h in range(H):
                    cols = slice(HD * h, HD * (h + 1))
                    last = pe.matmul(bank(5)[0:n, cols], d_x[0:n, s, place_of(h), 0:n], d_r[0:n, cols],
                                     start=True, stop=True)
                last.then_inc(vn_ready, 1)

            def outputs(c, s, n):
                pe.wait_ge(vn_made, c + 1)
                pe.wait_ge(qg_made, 2 * c + 2)
                for h in range(H):
                    cols = slice(HD * h, HD * (h + 1))
                    pe.matmul(value(h, n), d_qg[half(h), s, h // 2, 0:n], d_s[half(h), h // 2, :],
                              start=True, stop=False)
                    last = pe.matmul(value(h, n), d_qt[0:n, s, place_of(h), 0:n], d_vn[0:n, cols],
                                     start=False, stop=True)
                last.then_inc(o_made, 1)
                for h in range(H):
                    cols = slice(HD * h, HD * (h + 1))
                    last = pe.matmul(bank(5)[half(h), HD * (h // 2):HD * (h // 2 + 1)], d_kd[0:n, s, cols],
                                     d_vn[0:n, cols], start=True, stop=True)
                last.then_inc(ds_ready, 1)

            def turn_outputs(c, n):
                pe.wait_ge(on_made, c + 1)
                for k in range(WT):
                    last = pe.transpose(bank(5)[:, P * k:P * k + n], d_on[0:n, P * k:P * (k + 1)], ident[0:n, 0:n])
                last.then_inc(ot_ready, 1)

            def first_level(c, s, n):
                pe.wait_ge(x0_made, c + 1)
                for g in range(2):
                    for h in range(g, H, 2):
                        last = pe.transpose(group(0, h, n), d_x[0:n, s, place_of(h), 0:n], ident[0:n, 0:n])
                    last.then_inc(t0_ready, 1)

            def level_products(c, s, l, n):
                for g in range(2):
                    pe.wait_ge(t_made, t_step(c, l - 1, g))
                    for h in range(g, H, 2):
                        last = pe.matmul(group(0, h, n), d_at[0:n, s, place_of(h), 0:n],
                                         d_t[0:n, place_of(h), 0:n], start=True, stop=True)
                    last.then_inc(m_ready, 1)

            def renewing_products(c, s, l, n):
                for g in range(2):
                    pe.wait_ge(m_made, inner_step(c, l, g))
                    if l > 1:
                        pe.wait_ge(x_made, inner_step(c, l - 1, g))
                    if l < levels_of(n) - 1:
                        for h in range(g, H, 2):
                            last = pe.matmul(group(0, h, n), d_x[0:n, s, place_of(h), 0:n],
                                             d_m[0:n, place_of(h), 0:n], start=True, stop=True)
                        last.then_inc(t_ready, 1)
                    for h in range(g, H, 2):
                        last = pe.matmul(group(2, h, n), d_m[0:n, place_of(h), 0:n], d_x[0:n, s, place_of(h), 0:n],
                                         start=True, stop=True)
                    last.then_inc(x_ready, 1)

            def last_level_products(c, s):
                for g in range(2):
                    pe.wait_ge(t_made, t_step(c, LEVELS - 2, g))
                    for h in range(g, H, 2):
                        last = pe.matmul(bank(g)[:, P * (h // 2):P * (h // 2) + HD],
                                         d_at[:, s, place_of(h), :], d_t[:, place_of(h), 0:HD],
                                         start=True, stop=True)
                    last.then_inc(m_ready, 1)

            def last_renewing_products(c, s):
                for g in range(2):
                    pe.wait_ge(last_m_made, 2 * c + g + 1)
                    pe.wait_ge(x_made, inner_step(c, LEVELS - 2, g))
                    for h in range(g, H, 2):
                        last = pe.matmul(bank(2 + g)[:, P * (h // 2) + HD:P * (h // 2 + 1)],
                                         d_m[:, place_of(h), :], d_x[:, s, place_of(h), HD:P],
                                         start=True, stop=True)
                    last.then_inc(x_ready, 1)

            def inverse(c, s, n, scanned, prepared):
                for l in range(levels_of(n)):
                    if l == 0:
                        first_level(c, s, n)
                    elif l < LEVELS - 1:
                        level_products(c, s, l, n)
                    else:
                        last_level_products(c, s)
                    if scanned and l == 0:
                        pe.wait_ge(qt_made, c + 1)
                        values_of_state(c - 1, 1 - s, P)
                    if scanned and l == 1:
                        solved_values(c - 1, 1 - s, P)
                    if prepared and l == 3:
                        decay_sums(c + 1, prepared)
                    if 0 < l < LEVELS - 1:
                        renewing_products(c, s, l, n)
                    elif l:
                        last_renewing_products(c, s)
                    if scanned and l == 1:
                        outputs(c - 1, 1 - s, P)
                    if scanned and l == 2:
                        turn_outputs(c - 1, P)
                    if prepared and l == 3:
                        square_sums(c + 1, prepared)
                    if prepared and l == 4:
                        turn_keys(c + 1, prepared)
                        key_products(c + 1, prepared)
                    if prepared and l == 5:
                        query_products(c + 1, prepared)

            decay_sums(0, P, True)
            square_sums(0, P, True)
            turn_keys(0, P)
            key_products(0, P)
            query_products(0, P)
            inverse(0, 0, P, False, P)
            with pe.Fori(0, (NT - 2) // 2) as i:
                for u in range(2):
                    inverse(2 * i + u + 1, 1 - u, P, True, P)
            inverse(NT - 1, (NT - 1) % 2, P, True, TS)
            inverse(NT, NT % 2, TS, True, None)
            pe.wait_ge(s_loaded, 16)
            values_of_state(NT, NT % 2, TS)
            solved_values(NT, NT % 2, TS)
            outputs(NT, NT % 2, TS)
            turn_outputs(NT, TS)

            pe.wait_ge(mix_split, 1 + CHUNKS)
            for t, rows in enumerate(tile_rows):
                pe.wait_ge(xr_loaded[t % 4], 16 * (t // 4 + 1))
                if t >= 2:
                    pe.wait_ge(h_placed, t - 1)
                for k in range(KT):
                    last = pe.transpose(bank(2 * (t % 2) + k // 4)[:, P * (k % 4):P * (k % 4) + rows],
                                        xr_in[t % 4][0:rows, P * k:P * k + P], ident[0:rows, 0:rows])
                last.then_inc(xr_turned, 1)
            pe.wait_ge(h_placed, NTT)
            with pe.Fori(0, 2) as i:
                for j in range(4):
                    slot, mm = j // 2, j % 2
                    if mm == 0:
                        pe.wait_ge(w_split, 14 + 2 * i + slot + 1)
                    pe.wait_ge(added, 4 * i + j + 1)
                    dense(3 * (j % 2), lambda k: whi_cols[:, slot, k, P * mm:P * mm + P],
                          lambda k: wlo_cols[:, slot, k, P * mm:P * mm + P]).then_inc(dense_ready, 1)

            pe.wait_ge(added, KT + 2)
            for k in range(KT):
                pe.wait_ge(nsq_made, k + 1)
                for c in range(3):
                    last = pe.matmul(bank(c)[:, 0:CH], ones[:], wide[:, k % 2, CH * c:CH * (c + 1)],
                                     start=(k == 0), stop=(k == KT - 1))
                last.then_inc(nsum, 1)
            pe.wait_ge(nsd, 1)
            whi_down = w_hi[:, :, :].rearrange("p s (k n) -> p s k n", k=4)
            wlo_down = w_lo[:, :, :].rearrange("p s (k n) -> p s k n", k=4)
            with pe.Fori(0, ROUNDS) as g:
                for j in range(PER):
                    if 2 <= j < 6:
                        pe.wait_ge(relu_free, 4 * g + j - 1)
                    else:
                        pe.wait_ge(added, KT * g + KT + (1 + j if j < 2 else j - 3))
                    if j < 4:
                        slot, mm = j // 2, j % 2
                        if mm == 0:
                            pe.wait_ge(w_split, 18 + 4 * g + slot + 1)
                        last = dense(3 * (j % 2), lambda k: whi_cols[:, slot, k, P * mm:P * mm + P],
                                     lambda k: wlo_cols[:, slot, k, P * mm:P * mm + P],
                                     before=(lambda k: pe.wait_ge(nlo, k + 1)) if j == 0 else None)
                    else:
                        slot, mm = (j - 4) // 4, (j - 4) % 4
                        if mm == 0:
                            pe.wait_ge(w_split, 20 + 4 * g + slot + 1)
                        last = dense(3 * (j % 2), lambda k: whi_down[:, slot, k, P * mm:P * mm + P],
                                     lambda k: wlo_down[:, slot, k, P * mm:P * mm + P], 4, hid_hi, hid_lo,
                                     before=(lambda k: pe.wait_ge(hid_split, 1 + 4 * g + k + 1)) if j == 4 else None)
                    last.then_inc(dense_ready, 1)

            def turn_embedding(t):
                rows = tile_rows[t]
                pe.wait_ge(p_loaded[t % 2], 16 * (t // 2 + 1))
                if t >= 2:
                    pe.wait_ge(p_lo, t - 1)
                for k in range(2):
                    last = pe.transpose(bank(6 + t % 2)[:, P * k:P * k + rows], p_in[0:rows, t % 2, P * k:P * k + P],
                                        ident[0:rows, 0:rows])
                last.then_inc(p_turned, 1)

            pe.wait_ge(added, KT + KT * ROUNDS - 1 + 2)
            turn_embedding(0)
            turn_embedding(1)
            pj_hi = proj_hi.rearrange("p (k n) -> p k n", k=2)
            pj_lo = proj_lo.rearrange("p (k n) -> p k n", k=2)
            for half in range(2):
                if half == 0:
                    pe.wait_ge(w_split, 51)
                pe.wait_ge(gate_split, 1 + 2 * half)
                for t, rows in enumerate(tile_rows):
                    y = NTT * half + t
                    if y >= 2:
                        pe.wait_ge(y_made, y - 1)
                    token_product(bank(y % 2)[0:rows, :], rows, t, lambda k: whi_cols[:, :, k, :],
                                  lambda k: wlo_cols[:, :, k, :],
                                  before=(lambda k: pe.wait_ge(nlo, KT + k + 1)) if y == 0 else None)
                    if y == 0:
                        pe.wait_ge(acc_made, KT - 1)
                        for i, n in enumerate(tile_rows):
                            last = pe.matmul(bank(5)[0:n, i:i + 1], wide[:, 2, P * i:P * i + n], ones[:, 0:1],
                                             start=True, stop=True)
                        last.then_inc(nsum, 1)
                    if y == 1:
                        pe.wait_ge(nln, 2)
                    if y + 2 < NTT:
                        turn_embedding(y + 2)
                    if y < NTT:
                        pe.wait_ge(p_lo, y + 1)
                    if y == 0:
                        pe.wait_ge(w_split, 52)
                    token_product(bank(2 + y % 2)[0:rows, :], rows, t, lambda k: pj_hi[:, k, 512 * half:512 * half + 512],
                                  lambda k: pj_lo[:, k, 512 * half:512 * half + 512], 2, hid_hi, hid_lo)
                    for f in range(4):
                        last = pe.transpose(bank(4 + y % 2)[0:rows, P * f:P * (f + 1)],
                                            h_t[:, 4 * half + f, P * t:P * t + rows], ident[:])
                    last.then_inc(ple_ready, 1)


_INS = ["x_prompt", "x_sample", "cache_conv", "state_delta", "cache_k", "cache_v", "p_prompt", "p_sample", "g_mix",
        "w_in", "conv_w", "a_log", "dt_bias", "g_out_dn", "g_q_sb", "g_k_sb", "w_out", "g_mlp", "w_up", "w_down",
        "g_ple", "w_ple_gate", "w_ple_proj"]


def kernel(**inputs):
    import numpy as _np
    import concourse.bacc as _bacc
    from concourse import mybir as _mybir
    from concourse.bass_utils import run_bass_kernel_spmd as _run

    nc = _bacc.Bacc("TRN2", target_bir_lowering=False, num_devices=1)
    arrays, args = {}, []
    for name in _INS:
        a = _np.ascontiguousarray(inputs[name])
        arrays[f"in_{name}_dram"] = a
        args.append(nc.dram_tensor(f"in_{name}_dram", a.shape, _mybir.dt.from_np(a.dtype), kind="ExternalInput").ap())
    depth, streams, seq = 1, inputs["x_prompt"].shape[0], inputs["x_prompt"].shape[1]
    conv, delta = tuple(inputs["cache_conv"].shape), tuple(inputs["state_delta"].shape)
    heads = tuple(inputs["cache_k"].shape[3:])
    dec = inputs["x_sample"].shape[1]
    outs = [tuple(inputs["x_prompt"].shape), tuple(inputs["x_sample"].shape),
            conv, delta, (depth, streams, seq) + heads, (depth, streams, seq) + heads,
            conv, delta, (depth, streams, dec) + heads, (depth, streams, dec) + heads]
    for i, shape in enumerate(outs):
        args.append(nc.dram_tensor(f"out_{i}_dram", shape, _mybir.dt.float32, kind="ExternalOutput").ap())
    trunk_step(nc, *args)
    r = _run(nc, [arrays], core_ids=[0])
    return tuple(r.results[0][f"out_{i}_dram"] for i in range(len(outs)))
```
